# Optimizing a Trainium2 kernel written in Bass

```python
import math
import jax, jax.numpy as jnp
from jax import lax
import numpy as np
import functools

D_MODEL = 1024
BATCH = 1
SEQ = 512
DEPTH = 2

N_MEM = 256
HEAD_DIM = 64
N_MEM_HEADS = 4
MEM_WIDTH = N_MEM_HEADS * HEAD_DIM
CONV_WIDTH = D_MODEL - MEM_WIDTH
CONV_K = 3
N_Q_HEADS = CONV_WIDTH // HEAD_DIM
N_KV_HEADS = 4
GROUP = N_Q_HEADS // N_KV_HEADS
Q_WIDTH = N_Q_HEADS * HEAD_DIM
KV_WIDTH = N_KV_HEADS * HEAD_DIM
A_PROJ = 3 * CONV_WIDTH + MEM_WIDTH
B_PROJ = Q_WIDTH + MEM_WIDTH
WINDOW = 128
BLOCK = 128
REL_BUCKETS = 32
REL_MAX_DIST = 128
D_FF = ((8 * D_MODEL + 3 * 256 - 1) // (3 * 256)) * 256
N_A = DEPTH // 2
N_B = DEPTH - N_A
EPS = 1e-5


def rmsnorm(x, g):
    x32 = x.astype(jnp.float32)
    y = x32 * lax.rsqrt(jnp.mean(x32 * x32, axis=-1, keepdims=True) + EPS)
    return (y * g.astype(jnp.float32)).astype(x.dtype)

def _rel_bucket(dist):
    max_exact = REL_BUCKETS // 2
    d = jnp.maximum(dist, 1).astype(jnp.float32)
    large = max_exact + (jnp.log(d / max_exact) / math.log(REL_MAX_DIST / max_exact)
                         * (REL_BUCKETS - max_exact)).astype(jnp.int32)
    large = jnp.minimum(large, REL_BUCKETS - 1)
    return jnp.where(dist < max_exact, dist, large)

def _band_geometry(n_blocks):
    qi = jnp.arange(BLOCK, dtype=jnp.int32)[:, None]
    kj = jnp.arange(2 * BLOCK, dtype=jnp.int32)[None, :]
    dist = qi + BLOCK - kj
    in_window = (dist >= 0) & (dist < WINDOW)
    first = (jnp.arange(n_blocks) == 0)[:, None, None]
    mask = in_window[None] & ~(first & (kj[None] < BLOCK))
    bucket = _rel_bucket(jnp.maximum(dist, 0))
    return mask, bucket

def _band(t):
    bsz, s = t.shape[0], t.shape[1]
    tb = t.reshape(bsz, s // BLOCK, BLOCK, N_KV_HEADS, HEAD_DIM)
    prev = jnp.concatenate([jnp.zeros_like(tb[:, :1]), tb[:, :-1]], axis=1)
    return jnp.concatenate([prev, tb], axis=2)

def _short_conv(u, b_gate, c_gate, w):
    v = c_gate * u
    s = v.shape[1]
    vp = jnp.pad(v, ((0, 0), (CONV_K - 1, 0), (0, 0)))
    conv = w[0] * vp[:, 0:s] + w[1] * vp[:, 1:s + 1] + w[2] * vp[:, 2:s + 2]
    return b_gate * conv

def _swa_sinks(q, k_band, v_band, sinks, rel_bias, mask, bucket):
    bsz, s, _ = q.shape
    nb = s // BLOCK
    qb = q.reshape(bsz, nb, BLOCK, N_KV_HEADS, GROUP, HEAD_DIM)
    logits = jnp.einsum('bnqhgd,bnjhd->bnhgqj', qb, k_band).astype(jnp.float32) * (HEAD_DIM ** -0.5)
    bias = jnp.transpose(rel_bias.astype(jnp.float32)[bucket], (2, 0, 1))
    bias = bias.reshape(N_KV_HEADS, GROUP, BLOCK, 2 * BLOCK)
    logits = jnp.where(mask[None, :, None, None], logits + bias, -jnp.inf)
    sink = sinks.astype(jnp.float32).reshape(N_KV_HEADS, GROUP, 1, 1)
    m = jnp.maximum(jnp.max(logits, axis=-1, keepdims=True), sink)
    p = jnp.exp(logits - m)
    denom = jnp.sum(p, axis=-1, keepdims=True) + jnp.exp(sink - m)
    probs = (p / denom).astype(v_band.dtype)
    out = jnp.einsum('bnhgqj,bnjhd->bnqhgd', probs, v_band)
    return out.reshape(bsz, s, Q_WIDTH)

def _mem_attention(q_mem, mem_k, mem_v):
    bsz, s = q_mem.shape[0], q_mem.shape[1]
    logits = jnp.einsum('bshd,bmhd->bhsm', q_mem, mem_k).astype(jnp.float32) * (HEAD_DIM ** -0.5)
    probs = jax.nn.softmax(logits, axis=-1).astype(mem_v.dtype)
    return jnp.einsum('bhsm,bmhd->bshd', probs, mem_v).reshape(bsz, s, MEM_WIDTH)

def first_inputs(seed: int = 0) -> dict:
    key = jax.random.key(seed)
    ks = jax.random.split(key, 20)

    def nrm(k, shape, scale):
        return jax.random.normal(k, shape, jnp.float32) * scale

    def gain(k, shape):
        return 1.0 + nrm(k, shape, 0.05)

    return {
        'x': nrm(ks[0], (BATCH, SEQ, D_MODEL), 1.0),
        'mem': nrm(ks[1], (BATCH, N_MEM, D_MODEL), 1.0),
        'norm_mix': gain(ks[2], (DEPTH, D_MODEL)),
        'norm_ffn': gain(ks[3], (DEPTH, D_MODEL)),
        'a_w_in': nrm(ks[4], (N_A, D_MODEL, A_PROJ), D_MODEL ** -0.5),
        'a_conv_w': nrm(ks[5], (N_A, CONV_K, CONV_WIDTH), CONV_K ** -0.5),
        'a_w_out': nrm(ks[6], (N_A, CONV_WIDTH + MEM_WIDTH, D_MODEL), (CONV_WIDTH + MEM_WIDTH) ** -0.5),
        'kv_norm': gain(ks[7], (D_MODEL,)),
        'w_kv': nrm(ks[8], (D_MODEL, 2 * KV_WIDTH), D_MODEL ** -0.5),
        'b_w_q': nrm(ks[9], (N_B, D_MODEL, B_PROJ), D_MODEL ** -0.5),
        'b_sinks': nrm(ks[10], (N_B, N_Q_HEADS), 0.5),
        'b_w_out': nrm(ks[11], (N_B, Q_WIDTH + MEM_WIDTH, D_MODEL), (Q_WIDTH + MEM_WIDTH) ** -0.5),
        'rel_bias': nrm(ks[12], (REL_BUCKETS, N_Q_HEADS), 0.5),
        'mem_norm': gain(ks[13], (D_MODEL,)),
        'w_mem_kv': nrm(ks[14], (DEPTH, D_MODEL, 2 * MEM_WIDTH), D_MODEL ** -0.5),
        'w_gate': nrm(ks[15], (DEPTH, D_MODEL, D_FF), D_MODEL ** -0.5),
        'w_up': nrm(ks[16], (DEPTH, D_MODEL, D_FF), D_MODEL ** -0.5),
        'w_down': nrm(ks[17], (DEPTH, D_FF, D_MODEL), D_FF ** -0.5),
        'final_norm': gain(ks[18], (D_MODEL,)),
    }

def first_block(x, mem, norm_mix, norm_ffn, a_w_in, a_conv_w, a_w_out, kv_norm, w_kv,
              b_w_q, b_sinks, b_w_out, rel_bias, mem_norm, w_mem_kv, w_gate, w_up, w_down,
              final_norm):
    bsz, s, _ = x.shape
    mask, bucket = _band_geometry(s // BLOCK)
    mem_n = rmsnorm(mem, mem_norm)
    k_band = None
    v_band = None
    for i in range(DEPTH):
        if i == N_A:
            kv = rmsnorm(x, kv_norm) @ w_kv
            k, v = jnp.split(kv, 2, axis=-1)
            k_band = _band(k.reshape(bsz, s, N_KV_HEADS, HEAD_DIM))
            v_band = _band(v.reshape(bsz, s, N_KV_HEADS, HEAD_DIM))
        mem_kv = mem_n @ w_mem_kv[i]
        mk, mv = jnp.split(mem_kv, 2, axis=-1)
        mk = mk.reshape(bsz, N_MEM, N_MEM_HEADS, HEAD_DIM)
        mv = mv.reshape(bsz, N_MEM, N_MEM_HEADS, HEAD_DIM)
        h = rmsnorm(x, norm_mix[i])
        if i < N_A:
            proj = h @ a_w_in[i]
            u, b_gate, c_gate, q_mem = jnp.split(
                proj, [CONV_WIDTH, 2 * CONV_WIDTH, 3 * CONV_WIDTH], axis=-1)
            y_tok = _short_conv(u, b_gate, c_gate, a_conv_w[i])
            w_out = a_w_out[i]
        else:
            j = i - N_A
            proj = h @ b_w_q[j]
            q, q_mem = jnp.split(proj, [Q_WIDTH], axis=-1)
            y_tok = _swa_sinks(q, k_band, v_band, b_sinks[j], rel_bias, mask, bucket)
            w_out = b_w_out[j]
        y_mem = _mem_attention(q_mem.reshape(bsz, s, N_MEM_HEADS, HEAD_DIM), mk, mv)
        x = x + jnp.concatenate([y_tok, y_mem], axis=-1) @ w_out
        h = rmsnorm(x, norm_ffn[i])
        x = x + (jax.nn.silu(h @ w_gate[i]) * (h @ w_up[i])) @ w_down[i]
    return rmsnorm(x, final_norm)


DEPTH_2 = 1

NSA_HEADS = 8
NSA_KV_GROUPS = 2
NSA_HEAD_DIM = 64
NSA_WIDTH = NSA_HEADS * NSA_HEAD_DIM
NSA_KV_WIDTH = NSA_KV_GROUPS * NSA_HEAD_DIM
CMP_LEN = 32
CMP_STRIDE = 16
CMP_HIDDEN = 256
SEL_BLOCK = 64
SEL_TOPN = 16
WINDOW_2 = 512
Q_BLOCK = 128
ROPE_THETA = 500000.0
ROPE_DIM = NSA_HEAD_DIM // 4

RET_HEADS = 4
RET_QK_DIM = 128
RET_V_DIM = 256
RET_QK_WIDTH = RET_HEADS * RET_QK_DIM
RET_V_WIDTH = RET_HEADS * RET_V_DIM
RET_CHUNK = 128
RET_ROPE_BASE = 10000.0

RMS_EPS = 1e-6
GN_EPS = 1e-6

PROJ_SIZES = (
    NSA_WIDTH,
    NSA_KV_WIDTH,
    NSA_KV_WIDTH,
    NSA_KV_WIDTH,
    NSA_KV_WIDTH,
    NSA_KV_WIDTH,
    NSA_KV_WIDTH,
    NSA_HEADS * 3,
    NSA_WIDTH,
    RET_QK_WIDTH,
    RET_QK_WIDTH,
    RET_V_WIDTH,
    RET_V_WIDTH,
    D_MODEL,
    D_MODEL,
)
PROJ_TOTAL = sum(PROJ_SIZES)


def rms_norm(x, g):
    x32 = x.astype(jnp.float32)
    y = x32 * lax.rsqrt(jnp.mean(x32 * x32, axis=-1, keepdims=True) + RMS_EPS)
    return (y * g.astype(jnp.float32)).astype(x.dtype)

def split_points():
    pts, acc = [], 0
    for s in PROJ_SIZES[:-1]:
        acc += s
        pts.append(acc)
    return pts

def apply_rotary(x, ang):
    half = ang.shape[-1]
    r = 2 * half
    cos = jnp.cos(ang)[:, None, :].astype(x.dtype)
    sin = jnp.sin(ang)[:, None, :].astype(x.dtype)
    x1 = x[..., :half]
    x2 = x[..., half:r]
    return jnp.concatenate([x1 * cos - x2 * sin, x2 * cos + x1 * sin, x[..., r:]], axis=-1)

def masked_softmax(s, mask):
    s = jnp.where(mask, s.astype(jnp.float32), -jnp.inf)
    m = jnp.max(s, axis=-1, keepdims=True)
    m = jnp.where(jnp.isfinite(m), m, 0.0)
    p = jnp.where(mask, jnp.exp(s - m), 0.0)
    return p / jnp.maximum(jnp.sum(p, axis=-1, keepdims=True), jnp.finfo(jnp.float32).tiny)

def compress_blocks(kv, pe, w1, w2):
    S, G, dh = kv.shape
    n_cmp = (S - CMP_LEN) // CMP_STRIDE + 1
    tok_idx = jnp.arange(n_cmp)[:, None] * CMP_STRIDE + jnp.arange(CMP_LEN)[None, :]
    blocks = kv[tok_idx] + pe[None, :, None, :]
    flat = blocks.transpose(0, 2, 1, 3).reshape(n_cmp, G, CMP_LEN * dh)
    return jax.nn.gelu(flat @ w1) @ w2

def nsa_sequence(q, k_cmp_raw, v_cmp_raw, k_sel, v_sel, k_win, v_win, gate,
                 cmp_pe_k, cmp_w1_k, cmp_w2_k, cmp_pe_v, cmp_w1_v, cmp_w2_v):
    S = q.shape[0]
    G, H, dh = NSA_KV_GROUPS, NSA_HEADS, NSA_HEAD_DIM
    hpg = H // G
    scale = dh ** -0.5

    kc = compress_blocks(k_cmp_raw, cmp_pe_k, cmp_w1_k, cmp_w2_k)
    vc = compress_blocks(v_cmp_raw, cmp_pe_v, cmp_w1_v, cmp_w2_v)
    n_cmp = kc.shape[0]
    cmp_start = jnp.arange(n_cmp) * CMP_STRIDE
    cmp_end = cmp_start + CMP_LEN - 1

    n_sel = S // SEL_BLOCK
    n_top = min(SEL_TOPN, n_sel)
    sel_start = jnp.arange(n_sel) * SEL_BLOCK
    overlap = ((cmp_start[:, None] < sel_start[None, :] + SEL_BLOCK)
               & (cmp_start[:, None] + CMP_LEN > sel_start[None, :])).astype(jnp.float32)
    kb = k_sel.reshape(n_sel, SEL_BLOCK, G, dh).transpose(2, 0, 1, 3)
    vb = v_sel.reshape(n_sel, SEL_BLOCK, G, dh).transpose(2, 0, 1, 3)

    k_pad = jnp.pad(k_win, ((WINDOW_2, 0), (0, 0), (0, 0)))
    v_pad = jnp.pad(v_win, ((WINDOW_2, 0), (0, 0), (0, 0)))

    n_qb = S // Q_BLOCK
    qb = q.reshape(n_qb, Q_BLOCK, G, hpg, dh)
    gb = gate.reshape(n_qb, Q_BLOCK, G, hpg, 3)
    blk_ids = jnp.arange(n_sel)
    g_idx = jnp.arange(G)[None, :, None]

    def block(args):
        qi, gi, b = args
        t = b * Q_BLOCK + jnp.arange(Q_BLOCK)
        s = jnp.einsum('qghd,cgd->qghc', qi, kc) * scale
        mask_c = (cmp_end[None, :] <= t[:, None])[:, None, None, :]
        p_c = masked_softmax(s, mask_c)
        o_c = jnp.einsum('qghc,cgd->qghd', p_c.astype(vc.dtype), vc)
        imp = jnp.einsum('qgc,cn->qgn', jnp.sum(p_c, axis=2), overlap)
        cur = t // SEL_BLOCK
        valid = blk_ids[None, :] <= cur[:, None]
        forced = ((blk_ids[None, :] == 0) | (blk_ids[None, :] == cur[:, None])
                  | (blk_ids[None, :] == cur[:, None] - 1))
        score = jnp.where(forced[:, None, :], jnp.inf,
                          jnp.where(valid[:, None, :], imp, -jnp.inf))
        _, idx = lax.top_k(score, n_top)
        sel_valid = jnp.take_along_axis(
            jnp.broadcast_to(valid[:, None, :], score.shape), idx, axis=-1)
        ks = kb[g_idx, idx]
        vs = vb[g_idx, idx]
        s = jnp.einsum('qghd,qgnbd->qghnb', qi, ks) * scale
        kpos = idx[..., None] * SEL_BLOCK + jnp.arange(SEL_BLOCK)
        mask_s = sel_valid[..., None] & (kpos <= t[:, None, None, None])
        nk = n_top * SEL_BLOCK
        p_s = masked_softmax(s.reshape(Q_BLOCK, G, hpg, nk),
                             mask_s.reshape(Q_BLOCK, G, 1, nk))
        o_s = jnp.einsum('qghk,qgkd->qghd', p_s.astype(vs.dtype),
                         vs.reshape(Q_BLOCK, G, nk, dh))
        kw = lax.dynamic_slice_in_dim(k_pad, b * Q_BLOCK, Q_BLOCK + WINDOW_2, axis=0)
        vw = lax.dynamic_slice_in_dim(v_pad, b * Q_BLOCK, Q_BLOCK + WINDOW_2, axis=0)
        wpos = b * Q_BLOCK - WINDOW_2 + jnp.arange(Q_BLOCK + WINDOW_2)
        diff = t[:, None] - wpos[None, :]
        mask_w = ((wpos[None, :] >= 0) & (diff >= 0) & (diff < WINDOW_2))[:, None, None, :]
        s = jnp.einsum('qghd,kgd->qghk', qi, kw) * scale
        p_w = masked_softmax(s, mask_w)
        o_w = jnp.einsum('qghk,kgd->qghd', p_w.astype(vw.dtype), vw)
        g = jax.nn.sigmoid(gi.astype(jnp.float32))
        o = g[..., 0:1] * o_c + g[..., 1:2] * o_s + g[..., 2:3] * o_w
        return o.reshape(Q_BLOCK, H * dh).astype(q.dtype)

    out = lax.map(block, (qb, gb, jnp.arange(n_qb)))
    return out.reshape(S, H * dh)

def retention_sequence(q, k, v):
    S = q.shape[0]
    H, dk, dv, C = RET_HEADS, RET_QK_DIM, RET_V_DIM, RET_CHUNK
    nc = S // C
    log_g = jnp.log(1.0 - 2.0 ** (-5.0 - jnp.arange(H, dtype=jnp.float32)))
    n = jnp.arange(C, dtype=jnp.float32)
    diff = n[:, None] - n[None, :]
    decay_mask = jnp.where(diff >= 0, jnp.exp(jnp.maximum(diff, 0.0)[None] * log_g[:, None, None]), 0.0)
    q_dec = jnp.exp((n[None, :] + 1.0) * log_g[:, None])
    k_dec = jnp.exp((C - 1.0 - n[None, :]) * log_g[:, None])
    chunk_dec = jnp.exp(C * log_g)

    qc = q.reshape(nc, C, H, dk)
    kc = k.reshape(nc, C, H, dk)
    vc = v.reshape(nc, C, H, dv)
    att = jnp.einsum('nihd,njhd->nhij', qc, kc) * decay_mask[None]
    o_inner = jnp.einsum('nhij,njhe->nihe', att, vc)
    kv = jnp.einsum('njhd,hj,njhe->nhde', kc, k_dec, vc).astype(jnp.float32)

    def step(R, kv_i):
        return chunk_dec[:, None, None] * R + kv_i, R

    _, R_prev = lax.scan(step, jnp.zeros((H, dk, dv), jnp.float32), kv)
    o_cross = jnp.einsum('nihd,hi,nhde->nihe', qc, q_dec, R_prev)
    o = (o_inner + o_cross).reshape(S, H, dv).astype(jnp.float32)
    mu = jnp.mean(o, axis=-1, keepdims=True)
    var = jnp.mean(jnp.square(o - mu), axis=-1, keepdims=True)
    o = (o - mu) * lax.rsqrt(var + GN_EPS)
    return o.reshape(S, H * dv).astype(q.dtype)

def second_inputs(seed: int = 0) -> dict:
    key = jax.random.key(seed)
    ks = jax.random.split(key, 16)
    f32 = jnp.float32
    nrm = lambda k, shape, fan_in: jax.random.normal(k, shape, f32) * (fan_in ** -0.5)
    cmp_in = CMP_LEN * NSA_HEAD_DIM
    return {
        "x": jax.random.normal(ks[0], (BATCH, SEQ, D_MODEL), f32),
        "norm_pre": 1.0 + 0.05 * jax.random.normal(ks[1], (D_MODEL,), f32),
        "w_in": nrm(ks[2], (D_MODEL, PROJ_TOTAL), D_MODEL),
        "b_nsa_gate": 0.1 * jax.random.normal(ks[3], (NSA_HEADS * 3,), f32),
        "cmp_pe_k": 0.02 * jax.random.normal(ks[4], (CMP_LEN, NSA_HEAD_DIM), f32),
        "cmp_w1_k": nrm(ks[5], (cmp_in, CMP_HIDDEN), cmp_in),
        "cmp_w2_k": nrm(ks[6], (CMP_HIDDEN, NSA_HEAD_DIM), CMP_HIDDEN),
        "cmp_pe_v": 0.02 * jax.random.normal(ks[7], (CMP_LEN, NSA_HEAD_DIM), f32),
        "cmp_w1_v": nrm(ks[8], (cmp_in, CMP_HIDDEN), cmp_in),
        "cmp_w2_v": nrm(ks[9], (CMP_HIDDEN, NSA_HEAD_DIM), CMP_HIDDEN),
        "w_nsa_o": nrm(ks[10], (NSA_WIDTH, D_MODEL), NSA_WIDTH),
        "w_ret_o": nrm(ks[11], (RET_V_WIDTH, D_MODEL), RET_V_WIDTH),
        "w_out": nrm(ks[12], (D_MODEL, D_MODEL), D_MODEL),
        "norm_post": 1.0 + 0.05 * jax.random.normal(ks[13], (D_MODEL,), f32),
    }

def second_block(x, norm_pre, w_in, b_nsa_gate, cmp_pe_k, cmp_w1_k, cmp_w2_k,
              cmp_pe_v, cmp_w1_v, cmp_w2_v, w_nsa_o, w_ret_o, w_out, norm_post):
    B, S, _ = x.shape
    pos = jnp.arange(S, dtype=jnp.float32)
    nsa_inv = 1.0 / (ROPE_THETA ** (jnp.arange(0, ROPE_DIM, 2, dtype=jnp.float32) / ROPE_DIM))
    nsa_ang = pos[:, None] * nsa_inv[None, :]
    ret_inv = 1.0 / (RET_ROPE_BASE ** jnp.linspace(0.0, 1.0, RET_QK_DIM // 2, dtype=jnp.float32))
    ret_ang = pos[:, None] * ret_inv[None, :]

    for _ in range(DEPTH_2):
        h = rms_norm(x, norm_pre)
        proj = h @ w_in
        (q_n, k_c, v_c, k_s, v_s, k_w, v_w, g_n, z_n,
         q_r, k_r, v_r, z_r, m_a, m_b) = jnp.split(proj, split_points(), axis=-1)

        kvshape = (B, S, NSA_KV_GROUPS, NSA_HEAD_DIM)
        q_n = apply_rotary(q_n.reshape(B, S, NSA_HEADS, NSA_HEAD_DIM), nsa_ang)
        k_c = apply_rotary(k_c.reshape(kvshape), nsa_ang)
        k_s = apply_rotary(k_s.reshape(kvshape), nsa_ang)
        k_w = apply_rotary(k_w.reshape(kvshape), nsa_ang)
        gate_n = (g_n + b_nsa_gate).reshape(B, S, NSA_HEADS, 3)
        nsa_fn = lambda a, b_, c, d, e, f, g, gt: nsa_sequence(
            a, b_, c, d, e, f, g, gt,
            cmp_pe_k, cmp_w1_k, cmp_w2_k, cmp_pe_v, cmp_w1_v, cmp_w2_v)
        o_a = jax.vmap(nsa_fn)(q_n, k_c, v_c.reshape(kvshape), k_s, v_s.reshape(kvshape),
                               k_w, v_w.reshape(kvshape), gate_n)
        y_a = (o_a * jax.nn.silu(z_n)) @ w_nsa_o

        q_r = apply_rotary(q_r.reshape(B, S, RET_HEADS, RET_QK_DIM), ret_ang)
        k_r = apply_rotary(k_r.reshape(B, S, RET_HEADS, RET_QK_DIM), ret_ang) * (RET_QK_DIM ** -0.5)
        o_b = jax.vmap(retention_sequence)(q_r, k_r, v_r.reshape(B, S, RET_HEADS, RET_V_DIM))
        y_b = (o_b * jax.nn.silu(z_r)) @ w_ret_o

        merged = jax.nn.sigmoid(m_a) * y_a + jax.nn.sigmoid(m_b) * y_b
        x = x + rms_norm(merged @ w_out, norm_post)
    return x


def setup_inputs(seed=0):
    out = dict(first_inputs(seed))
    for name, value in second_inputs(seed + 1).items():
        if name != "x":
            out[name + "_2"] = value
    return out


def reference(
    x, mem, norm_mix, norm_ffn, a_w_in, a_conv_w, a_w_out, kv_norm, w_kv, b_w_q, b_sinks,
    b_w_out, rel_bias, mem_norm, w_mem_kv, w_gate, w_up, w_down, final_norm, norm_pre_2, w_in_2,
    b_nsa_gate_2, cmp_pe_k_2, cmp_w1_k_2, cmp_w2_k_2, cmp_pe_v_2, cmp_w1_v_2, cmp_w2_v_2,
    w_nsa_o_2, w_ret_o_2, w_out_2, norm_post_2,
):
    x = first_block(
        x, mem, norm_mix, norm_ffn, a_w_in, a_conv_w, a_w_out, kv_norm, w_kv, b_w_q, b_sinks,
        b_w_out, rel_bias, mem_norm, w_mem_kv, w_gate, w_up, w_down, final_norm,
    )
    return second_block(
        x, norm_pre_2, w_in_2, b_nsa_gate_2, cmp_pe_k_2, cmp_w1_k_2, cmp_w2_k_2, cmp_pe_v_2,
        cmp_w1_v_2, cmp_w2_v_2, w_nsa_o_2, w_ret_o_2, w_out_2, norm_post_2,
    )


_drawn_inputs = setup_inputs


def setup_inputs(seed=0):
    import zlib

    import numpy as np

    out = dict(_drawn_inputs(seed))
    spreads = {}
    factors = {'kv_norm': 4.045,
     'b_sinks': 6.336,
     'mem_norm': 7.334,
     'b_nsa_gate_2': 8.0,
     'cmp_pe_k_2': 64.0,
     'cmp_pe_v_2': 8.0}
    for name, (base, spread) in spreads.items():
        noise = np.random.default_rng([zlib.crc32(name.encode()), seed]).standard_normal(out[name].shape)
        drawn = base * np.exp(spread * noise) if base else spread * noise
        out[name] = __import__('jax').numpy.asarray(drawn.astype(out[name].dtype))
    for name, factor in factors.items():
        out[name] = (out[name] * factor).astype(out[name].dtype)
    return out
```

```python
import math

import concourse.bass as bass
import numpy as np
from concourse import mybir

F32 = mybir.dt.float32
R32 = mybir.dt.float32r
BF16 = mybir.dt.bfloat16
ACT = mybir.ActivationFunctionType
ALU = mybir.AluOpType
AX = mybir.AxisListType

P = 128
S = 512
D = 1024
KT = D // P
NMEM = 256
HD = 64
FF = 2816
FT = FF // P
HALF = FT // 2
TB = S // P
CT = 6
RAW = 4
SLOT = HALF * P
SCALE = HD ** -0.5
EPS_A = 1e-5
EPS_B = 1e-6
MASKED = -1.0e30
GROUP = 3
NREL = 383
(G_MEM, G_MIX0, G_FFN0, G_KV, G_MIX1, G_FFN1, G_FINAL, G_PRE, G_POST) = range(9)

N_QM0 = 0
N_CONV0 = 2
N_MEMKV = 5
N_CONV = 13
N_OUT0 = 28
N_FFN0 = 36
N_DOWN0 = 80
N_KV = 96
N_QM1 = 100
N_Q = 102
N_OUT1 = 108
N_FFN1 = 116
N_DOWN1 = 160
N_SECOND = 176
N_GATE = 186
N_RET = 187
N_ZN = 203
N_MA = 207
N_ZR = 223
N_MB = 231
N_FIN = 247
N_END = 255

V_MIX0, V_MEM, V_FFN0, V_MIX1, V_FFN1, V_LAST, V_PRE, V_POST = range(8)
SQUARES = 9


NCMP = 31
CLEN = 32
CSTRIDE = 16
GH = 4
RH = 4
RDV = 256
EMPTY = -1.0e29
TINY = float(np.finfo(np.float32).tiny)


def out_index(n):
    return n if n <= N_DOWN0 else n - 8 if n <= N_DOWN1 else n - 16


def build(nc, a, out):
    base = (nc.sbuf_base + 31) // 32 * 32
    top = [base]

    def at(name, shape, dtype, offset):
        return nc.alloc_sbuf_tensor_at(name, shape, dtype, offset=offset)

    def sb(name, shape, dtype=F32):
        size = int(np.prod(shape[1:])) * (2 if dtype == BF16 else 4)
        t = at(name, shape, dtype, top[0])
        top[0] += (size + 31) // 32 * 32
        return t

    x = sb("x", [P, KT, S])
    a_hi = sb("a_hi", [P, KT, S], R32)
    a_lo = sb("a_lo", [P, KT, S], R32)
    raw = sb("raw", [P, RAW, SLOT])
    w_hi = sb("w_hi", [P, 2, SLOT], R32)
    w_lo = sb("w_lo", [P, 2, SLOT], R32)
    tmp_at = top[0]
    tmp = sb("tmp", [P, 4, S])
    rstd = sb("rstd", [P, S])
    diag = sb("diag", [P, TB, P])
    acc = sb("acc", [P, S])
    mk1_at = top[0]
    mk1 = sb("mk1", [P, 2, NMEM])
    mv1 = sb("mv1", [P, 2, NMEM])
    ident = sb("ident", [P, P])
    ones = sb("ones", [P, P])
    gains = sb("gains", [P, 9, KT])
    conv_w = sb("conv_w", [P, CT, 3])
    nsink = sb("nsink", [P, 12])
    sinks = sb("sinks", [P, 12])
    half = sb("half", [P, TB])
    acc2 = sb("acc2", [P, S])
    perm = sb("perm", [P, 2, P])
    w2 = sb("w2", [P, 2, 2, HD])
    pe2 = sb("pe2", [P, 2, CLEN])
    masks = sb("masks", [P, 2 * P + TB * GH * NCMP], BF16)
    gate_n = sb("gate_n", [P, TB, 24])
    hid = sb("hid", [P, 2, 2 * NCMP])
    kc = sb("kc", [P, NCMP])
    vc = sb("vc", [NCMP, 2, HD])
    gate_b = sb("gate_b", [24, 1])
    rs2 = sb("rs2", [P, TB])
    rs3 = sb("rs3", [P, TB])
    nm16 = sb("nm16", [P, 16])
    d16 = sb("d16", [P, 16])
    bn6 = sb("bn6", [P, TB, 6])
    bn2 = sb("bn2", [P, 2, TB, 2])
    var = sb("var", [P, TB])
    rs = sb("rs", [P, TB])
    nmx = sb("nmx", [P, 2, TB])
    den = sb("den", [P, 2, TB])
    es = sb("es", [P, 2, TB])
    sq = at("sq", [P, 2, S], F32, tmp_at)
    sq2 = at("sq2", [P, 2, S], F32, tmp_at + 4096)
    g0 = top[0]
    K1 = 1024

    g_hi = at("g_hi", [P, FT, S], R32, g0)
    g_lo = at("g_lo", [P, FT, S], R32, g0 + FT * 2 * K1)
    assert g0 + 2 * FT * 2 * K1 <= nc.sbuf_base + 212800, g0
    y_hi = at("y_hi", [P, KT, S], R32, g0)
    y_lo = at("y_lo", [P, KT, S], R32, g0 + 16 * K1)
    memx = at("memx", [P, KT, NMEM], F32, g0 + 32 * K1)
    mem_hi = at("mem_hi", [P, KT, NMEM], R32, g0 + 40 * K1)
    mem_lo = at("mem_lo", [P, KT, NMEM], R32, g0 + 48 * K1)
    u_s = at("u_s", [P, S], F32, g0 + 56 * K1)
    v_s = at("v_s", [P, S], F32, g0 + 58 * K1)
    y_s = at("y_s", [P, S], F32, g0 + 60 * K1)
    qm0 = at("qm0", [P, 2, S], F32, g0 + 62 * K1)
    pm0 = at("pm0", [P, 2, TB, NMEM], F32, g0 + 66 * K1)
    pmT0 = at("pmT0", [P, 2, S], F32, g0 + 74 * K1)
    mk0 = at("mk0", [P, 2, NMEM], F32, g0 + 78 * K1)
    mv0 = at("mv0", [P, 2, NMEM], F32, g0 + 80 * K1)
    mvt = at("mvt", [P, NMEM], F32, g0 + 82 * K1)
    rmem = at("rmem", [P, NMEM], F32, g0 + 83 * K1)
    table = at("table", [12, NREL], F32, g0 + 84 * K1)
    rb = at("rb", [33, 12], F32, g0 + 86 * K1)
    onehot = at("onehot", [33, NREL], F32, g0 + 86 * K1 + 256)
    kv_hi = at("kv_hi", [P, KT, S], R32, g0)
    kv_lo = at("kv_lo", [P, KT, S], R32, g0 + 16 * K1)
    kT = at("kT", [P, 2, S], F32, g0 + 32 * K1)
    vn = at("vn", [P, TB, NMEM], F32, g0 + 36 * K1)
    vT = at("vT", [P, S], F32, g0 + 40 * K1)
    qT = at("qT", [P, CT, S], F32, g0 + 42 * K1)
    band = at("band", [P, 12 * 256], F32, g0 + 42 * K1)
    qm1 = at("qm1", [P, 2, S], F32, g0 + 54 * K1)
    pm1 = at("pm1", [P, 2, TB, NMEM], F32, g0 + 58 * K1)
    pmT1 = at("pmT1", [P, 2, S], F32, g0 + 66 * K1)
    s_sw = at("s_sw", [P, 2, GROUP, 256], F32, g0 + 58 * K1)
    p_sw = at("p_sw", [P, 2, GROUP, 256], F32, g0 + 64 * K1)
    pT_sw = at("pT_sw", [P, 2, GROUP * P], F32, g0 + 70 * K1)
    bias = at("bias", [P, 12, 256], F32, g0 + 73 * K1)
    flip = at("flip", [P, P], F32, g0 + 85 * K1)

    t2 = at("t2", [P, 2, S], F32, mk1_at)
    pT_n = at("pT_n", [P, TB, GH * P], F32, tmp_at)
    qn = at("qn", [P, GH, S], F32, g0)
    ks = at("ks", [P, S], F32, g0 + 8 * K1)
    kw = at("kw", [P, S], F32, g0 + 10 * K1)
    bd = [at(f"bd{i}", [P, CLEN, 2 * NCMP], F32, g0 + (12 + 8 * i) * K1) for i in range(2)]
    p_n = at("p_n", [P, 2, GH, S], F32, g0 + 12 * K1)
    rope_n = at("rope_n", [P, 2, S], F32, g0 + 28 * K1)
    vs = at("vs", [P, TB, P], F32, g0 + 32 * K1)
    vw = at("vw", [P, TB, P], F32, g0 + 34 * K1)
    rope_r = at("rope_r", [P, 2, S], F32, g0 + 36 * K1)
    kcr = at("kcr", [P, S], F32, g0 + 40 * K1)
    vcr = at("vcr", [P, S], F32, g0 + 42 * K1)
    oa = at("oa", [P, GH, S], F32, g0 + 40 * K1)
    p_c = at("p_c", [P, 2, 16, NCMP], F32, g0 + 48 * K1)
    pT_c = at("pT_c", [NCMP, GH * P], F32, g0 + 52 * K1)
    r1 = at("r1", [P, S], F32, g0 + 54 * K1)
    w1 = at("w1", [P, CLEN, 256], F32, g0 + 56 * K1)
    qr = at("qr", [P, RH, S], F32, g0 + 56 * K1)
    kr = at("kr", [P, RH, S], F32, g0 + 64 * K1)
    vr = at("vr", [P, TB, RH * RDV], F32, g0 + 72 * K1)
    ya_hi = at("ya_hi", [P, GH, S], R32, g0)
    ya_lo = at("ya_lo", [P, GH, S], R32, g0 + 8 * K1)
    decay = at("decay", [P, RH, S], F32, g0 + 16 * K1)
    att = at("att", [P, TB, S], F32, g0 + 24 * K1)
    on = at("on", [P, TB, RDV], F32, g0 + 32 * K1)
    ob = [at("ob0", [P, 4, S], F32, g0 + 48 * K1), at("ob1", [P, 4, S], F32, g0 + 40 * K1)]
    merged = at("merged", [P, KT, S], F32, g0 + 16 * K1)
    yb_hi = at("yb_hi", [P, KT, S], R32, g0 + 56 * K1)
    yb_lo = at("yb_lo", [P, KT, S], R32, g0 + 72 * K1)
    mg_hi = at("mg_hi", [P, KT, S], R32, g0)
    mg_lo = at("mg_lo", [P, KT, S], R32, g0 + 32 * K1)
    yg = at("yg", [P, KT, S], F32, g0 + 16 * K1)
    ident_b = masks[:, 0:P]
    causal = masks[:, P:2 * P]
    mask_c = masks[:, 2 * P:]

    ps = nc.alloc_psum_tensor("ps", [P, 8, S], F32)

    def sem(name):
        return nc.alloc_semaphore(name)

    raw_in = [sem(f"raw_in{i}") for i in range(RAW)]
    x_in = [sem(f"x_in{i}") for i in range(4)]
    mem_in = sem("mem_in")
    const_in = sem("const_in")
    small_in = sem("small_in")
    w_hi_ready = sem("w_hi_ready")
    w_lo_ready = sem("w_lo_ready")
    blk_done = sem("blk_done")
    lin_read = sem("lin_read")
    ones_ready = sem("ones_ready")
    half_ready = sem("half_ready")
    sq_ready = sem("sq_ready")
    acc_ready = sem("acc_ready")
    norm_sum = sem("norm_sum")
    norm_var = sem("norm_var")
    norm_pow = sem("norm_pow")
    norm_diag = sem("norm_diag")
    norm_spread = sem("norm_spread")
    rstd_ready = sem("rstd_ready")
    a_hi_ready = sem("a_hi_ready")
    a_lo_ready = sem("a_lo_ready")
    memx_ready = sem("memx_ready")
    mem_hi_ready = sem("mem_hi_ready")
    mem_lo_ready = sem("mem_lo_ready")
    conv_step = sem("conv_step")
    yc_hi_ready = sem("yc_hi_ready")
    yc_lo_ready = sem("yc_lo_ready")
    mv_turned = sem("mv_turned")
    mv_ready = sem("mv_ready")
    mem_scores = sem("mem_scores")
    mem_max = sem("mem_max")
    mem_exp = sem("mem_exp")
    mem_rden = sem("mem_rden")
    mem_probs = sem("mem_probs")
    mem_turned = sem("mem_turned")
    mem_pT0 = sem("mem_pT0")
    mem_pT1 = sem("mem_pT1")
    mem_pv = sem("mem_pv")
    ym_hi_ready = sem("ym_hi_ready")
    ym_lo_ready = sem("ym_lo_ready")
    silu_ready = sem("silu_ready")
    gu_ready = sem("gu_ready")
    g_hi_ready = sem("g_hi_ready")
    g_lo_ready = sem("g_lo_ready")
    table_mm = sem("table_mm")
    table_ready = sem("table_ready")
    table_out = sem("table_out")
    band_in = sem("band_in")
    flip_mm = sem("flip_mm")
    bias_ready = sem("bias_ready")
    nsink_ready = sem("nsink_ready")
    kv_hi_ready = sem("kv_hi_ready")
    kv_lo_ready = sem("kv_lo_ready")
    v_turned = sem("v_turned")
    vn_ready = sem("vn_ready")
    sw_scores = sem("sw_scores")
    sw_biased = sem("sw_biased")
    sw_max = sem("sw_max")
    sw_sink = sem("sw_sink")
    sw_exp = sem("sw_exp")
    sw_den = sem("sw_den")
    sw_probs = sem("sw_probs")
    sw_turned = sem("sw_turned")
    sw_pT0 = sem("sw_pT0")
    sw_pT1 = sem("sw_pT1")
    sw_pv = sem("sw_pv")
    ys_hi_ready = sem("ys_hi_ready")
    ys_lo_ready = sem("ys_lo_ready")
    out_done = sem("out_done")
    sq2_ready = sem("sq2_ready")
    acc2_ready = sem("acc2_ready")
    gain_ready = sem("gain_ready")
    pre_step = sem("pre_step")
    small2_in = sem("small2_in")
    rope_in = sem("rope_in")
    w1k_in = sem("w1k_in")
    w1v_in = sem("w1v_in")
    bd_clear = sem("bd_clear")
    rope_mm = sem("rope_mm")
    rope_mul = sem("rope_mul")
    rope_ready = sem("rope_ready")
    turn_mm = sem("turn_mm")
    turn_ready = sem("turn_ready")
    bd_ready = sem("bd_ready")
    cmp_hidden = sem("cmp_hidden")
    cmp_gelu = sem("cmp_gelu")
    cmp_mm = sem("cmp_mm")
    cmp_ready = sem("cmp_ready")
    x1_ready = sem("x1_ready")
    gate_sig = sem("gate_sig")
    gate_mm = sem("gate_mm")
    gate_ready = sem("gate_ready")
    cm_scores = sem("cm_scores")
    cm_step = sem("cm_step")
    cm_exp = sem("cm_exp")
    cm_probs = sem("cm_probs")
    cm_turned = sem("cm_turned")
    cm_pT = sem("cm_pT")
    ns_scores = sem("ns_scores")
    ns_max = sem("ns_max")
    ns_exp = sem("ns_exp")
    ns_den = sem("ns_den")
    ns_probs = sem("ns_probs")
    ns_turned = sem("ns_turned")
    ns_pTd = sem("ns_pTd")
    ns_pTa = sem("ns_pTa")
    ns_pv = sem("ns_pv")
    oa_ready = sem("oa_ready")
    decay_in = sem("decay_in")
    rt_scores = sem("rt_scores")
    rt_att = sem("rt_att")
    rt_out = sem("rt_out")
    rt_stats = sem("rt_stats")
    rt_var = sem("rt_var")
    rt_pow = sem("rt_pow")
    rt_norm = sem("rt_norm")
    rt_turned = sem("rt_turned")
    rt_ob0 = sem("rt_ob0")
    rt_ob1 = sem("rt_ob1")
    gated = sem("gated")
    prod_ready = sem("prod_ready")
    zh_ready = sem("zh_ready")
    zl_ready = sem("zl_ready")
    fin_read = sem("fin_read")
    fin_gain = sem("fin_gain")
    out_part = sem("out_part")

    scratch = nc.dram_tensor("rel_scratch", (12, NREL), F32, kind="Internal").ap()

    stat_bank = 7

    def sw_unit(u):
        hp, b, s = u // 8, u % 8 // 2, u % 2
        keys = 256 if b else P
        return hp, b, s, keys, (b - 1) * P if b else 0

    NSW = 16
    MEM_STEPS = {0: {N_CONV + 1: 0, N_CONV + 4: 1, N_CONV + 7: 2, N_CONV + 10: 3},
                 1: {N_Q: 0, N_Q + 1: 1, N_Q + 2: 2, N_Q + 3: 3}}
    SW_FIRST = N_Q + 5

    NS = 16
    NS_FIRST, RT_FIRST = N_RET, N_ZN + 2

    def ns_unit(u):
        return u // 4, u % 4 // 2, u % 2, (u // 4 + 1) * P

    def width(n):
        return 24 * KT if n == N_GATE else GH * P if N_MA <= n < N_ZR and (n - N_MA) % 2 else KT * P

    ROPE = {N_SECOND: (0, kcr[:]), **{N_SECOND + 4 + t: (0, qn[:, t, :]) for t in range(GH)},
            N_SECOND + 8: (0, ks[:]), N_SECOND + 9: (0, kw[:])}
    for _h in range(RH):
        ROPE[N_RET + 4 * _h] = (1, qr[:, _h, :])
        ROPE[N_RET + 4 * _h + 1] = (1, kr[:, _h, :])
    TURN = {N_SECOND + 2: vs[:], N_SECOND + 3: vw[:]}
    for _f in range(2 * RH):
        TURN[N_RET + 4 * (_f // 2) + 2 + _f % 2] = vr[:, :, _f * P:(_f + 1) * P]
    ROPES, TURNS = sorted(ROPE), sorted(TURN)

    def turn_step(n):
        return N_SECOND + 4 if n == N_SECOND else N_SECOND + 5 if n == N_SECOND + 2 else n + 2

    def handled(n):
        return [m for m in ROPES + TURNS if turn_step(m) == n]

    def turn_bank(n):
        return 7 if n >= N_RET else 5 + n % 2

    def strip_of(n):
        return tmp[:, n % 4, :] if n < N_RET else t2[:, n % 2, :]

    def turned_before(n):
        order = [m for t in range(N_SECOND, N_END) for m in handled(t)]
        i = order.index(n)
        return sum(m in ROPE for m in order[:i]), sum(m in TURN for m in order[:i])

    def read_of(n):
        r, t = turned_before(n)
        return r + (n in ROPE), t + (n in TURN)

    def gated_index(n):
        if n < N_MA:
            return n - N_ZN
        if n < N_ZR:
            return 4 + (n - N_MA) // 2
        return 12 + n - N_ZR if n < N_MB else 20 + (n - N_MB) // 2

    def bank_of(n):
        if n >= N_SECOND:
            if n < N_GATE:
                return n % 4
            return 0 if n < RT_FIRST + 6 else n % 2
        if n < N_CONV:
            return n % 4
        if n in (N_KV + 2, N_KV + 3):
            return n - N_KV
        return 0 if n == N_OUT1 - 1 else n % 2

    with nc.Block() as block:

        @block.sync
        def _(sp):
            def load(n, slot, src, w):
                sp.wait_ge(w_lo_ready, n - (RAW - 1))
                sp.dma_start(raw[:, slot, 0:w], src).then_inc(raw_in[slot], 16)

            for n in range(RAW):
                sp.dma_start(raw[:, n, 0:KT * P], a["w8"][n]).then_inc(raw_in[n], 16)
            with sp.Fori(1, N_DOWN0 // RAW, 1) as i:
                for j in range(RAW):
                    load(i * RAW + j, j, a["w8"][i * RAW + j], KT * P)
            with sp.Fori(0, 2 * KT // RAW, 1) as i:
                for j in range(RAW):
                    load(i * RAW + (N_DOWN0 + j), j, a["w_down"][i * RAW + j], SLOT)
            with sp.Fori(0, (N_DOWN1 - N_KV) // RAW, 1) as i:
                for j in range(RAW):
                    load(i * RAW + (N_KV + j), j, a["w8"][i * RAW + (N_DOWN0 + j)], KT * P)
            with sp.Fori(0, 2 * KT // RAW, 1) as i:
                for j in range(RAW):
                    load(i * RAW + (N_DOWN1 + j), j, a["w_down"][i * RAW + (2 * KT + j)], SLOT)
            def source(n):
                if n == N_GATE:
                    return a["w_gates"]
                if n < N_GATE:
                    return a["w8b"][n - N_SECOND]
                if n < N_MA:
                    return a["w8b"][n - N_SECOND - 1]
                if n < N_ZR:
                    i = (n - N_MA) // 2
                    return a["w_nsa_o"][i] if (n - N_MA) % 2 else a["w8b"][30 + i]
                return a["w8b"][38 + n - N_ZR]

            for n in range(N_SECOND, N_END):
                if n == N_SECOND + RAW:
                    sp.wait_ge(lin_read, out_index(N_SECOND))
                    for half_at in (0, HD):
                        sp.dma_start(w1[half_at:half_at + HD], a["cmp_w1"][0]).then_inc(w1k_in, 16)
                if n == N_SECOND + 11:
                    sp.wait_ge(cmp_hidden, 1)
                    for half_at in (0, HD):
                        sp.dma_start(w1[half_at:half_at + HD], a["cmp_w1"][1]).then_inc(w1v_in, 16)
                load(n, n % RAW, source(n), width(n))
            for k in range(KT):
                sp.wait_ge(out_part, k + 1)
                sp.dma_start(out[:, k, :], x[:, k, :]).then_inc(out_done, 16)
            sp.wait_ge(out_done, 16 * KT)

        @block.gpsimd
        def _(pool):
            pool.memset(ones[:], 1.0).then_inc(ones_ready, 1)
            pool.memset(half[:], -0.5).then_inc(half_ready, 1)

            def clear(v):
                if v:
                    pool.wait_ge(norm_sum, v)
                pool.memset(acc[:], 0.0).then_inc(acc_ready, 1)
                pool.wait_ge(acc_ready, SQUARES * v + 1)

            def squares(v, cols=S):
                clear(v)
                for k in range(KT):
                    pool.wait_ge(sq_ready, KT * v + k + 1)
                    pool.wait_ge(acc_ready, SQUARES * v + 1 + k)
                    pool.tensor_tensor(acc[:, 0:cols], acc[:, 0:cols], sq[:, k % 2, 0:cols],
                                       ALU.add).then_inc(acc_ready, 1)

            def power(v, tiles=TB):
                pool.wait_ge(norm_var, v + 1)
                pool.tensor_tensor(rs[:, 0:tiles], var[:, 0:tiles], half[:, 0:tiles], ALU.pow)\
                    .then_inc(norm_pow, 1)

            squares(V_MIX0)
            power(V_MIX0)
            squares(V_MEM, NMEM)
            power(V_MEM, 2)
            for v in (V_FFN0, V_MIX1, V_FFN1):
                squares(v)
                power(v)
            clear(V_LAST)
            pool.memset(acc2[:], 0.0).then_inc(acc2_ready, 1)
            for k in range(KT):
                pool.wait_ge(sq_ready, KT * V_LAST + k + 1)
                pool.wait_ge(acc_ready, SQUARES * V_LAST + 1 + k)
                pool.tensor_tensor(acc[:], acc[:], sq[:, k % 2, :], ALU.add).then_inc(acc_ready, 1)
                pool.wait_ge(sq2_ready, k + 1)
                pool.wait_ge(acc2_ready, k + 1)
                pool.tensor_tensor(acc2[:], acc2[:], sq2[:, k % 2, :], ALU.add).then_inc(acc2_ready, 1)
            pool.wait_ge(lin_read, out_index(N_SECOND))
            for i in range(2):
                pool.memset(bd[i][:], 0.0).then_inc(bd_clear, 1)
            power(V_LAST)
            pool.wait_ge(norm_var, V_PRE + 1)
            pool.tensor_tensor(rs2[:], var[:], half[:], ALU.pow).then_inc(norm_pow, 1)
            for h in range(RH):
                pool.wait_ge(rt_var, h + 1)
                pool.tensor_tensor(bn2[:, h % 2, :, 1], bn2[:, h % 2, :, 1], half[:], ALU.pow)\
                    .then_inc(rt_pow, 1)
            squares(V_POST - 1)
            power(V_POST)

        @block.scalar
        def _(act):
            for j in range(4):
                act.dma_start(x[:, 2 * j:2 * j + 2, :], a["xT"][:, 2 * j:2 * j + 2, :])\
                    .then_inc(x_in[j], 16)
                if j == 0:
                    act.dma_start(gains[:], a["gains"]).then_inc(const_in, 16)
            act.dma_start(ident[:], a["ident"]).then_inc(const_in, 16)
            act.dma_start(conv_w[:], a["conv_w"]).then_inc(const_in, 16)
            act.dma_start(memx[:], a["memT"]).then_inc(mem_in, 16)
            act.dma_start(onehot[:], a["onehot"]).then_inc(small_in, 16)
            act.dma_start(rb[0:32, :], a["rel_bias"]).then_inc(small_in, 16)
            act.dma_start(rb[32:33, :], a["masked"]).then_inc(small_in, 16)
            act.dma_start(sinks[:], a["sinks"].partition_broadcast(P)).then_inc(small_in, 16)
            for dst, src in ((perm, "perm"), (w2, "cmp_w2"), (masks, "masks"), (gate_b, "gate_b")):
                act.dma_start(dst[:], a[src]).then_inc(small2_in, 16)
            for half_at in (0, HD):
                act.dma_start(pe2[half_at:half_at + HD], a["cmp_pe"]).then_inc(small2_in, 16)

            def split(n, w, slot=None, raw_slot=None, count=None):
                slot = n % 2 if slot is None else slot
                raw_slot = n % RAW if raw_slot is None else raw_slot
                act.wait_ge(raw_in[raw_slot], 16 * (n // RAW + 1) if count is None else count)
                if not isinstance(n, int) or n >= 2:
                    act.wait_ge(blk_done, n - 1)
                act.activation(w_hi[:, slot, 0:w], raw[:, raw_slot, 0:w], ACT.Copy)\
                    .then_inc(w_hi_ready, 1)

            def square(v, k, slot, src, cols=S, first=False):
                if v:
                    if first:
                        act.wait_ge(acc_ready, SQUARES * v)
                if not first:
                    act.wait_ge(acc_ready, k + SQUARES * v)
                act.activation(sq[:, slot, 0:cols], src, ACT.Square).then_inc(sq_ready, 1)

            def operand(k, g):
                act.activation(a_hi[:, k, :], x[:, k, :], ACT.Copy, scale=gains[:, g, bass.ds(k, 1)])\
                    .then_inc(a_hi_ready, 1)

            def spread(v, dst, cols=S):
                act.wait_ge(norm_spread, v + 1)
                act.activation(dst, ps[:, stat_bank, 0:cols], ACT.Copy).then_inc(rstd_ready, 1)

            def residual(k, q, v, g, slot, first=False):
                act.wait_ge(lin_read, q + 1)
                square(v, k, slot, x[:, k, :], first=first)
                if v == V_LAST:
                    if not first:
                        act.wait_ge(acc2_ready, k)
                    act.activation(sq2[:, slot, :], x[:, k, :], ACT.Square,
                                   scale=gains[:, G_FINAL, bass.ds(k, 1)]).then_inc(sq2_ready, 1)
                operand(k, g)

            def mem_exps(layer, i):
                u, pm = 4 * layer + i, (pm0, pm1)[layer]
                act.wait_ge(mem_max, u + 1)
                if i >= 2:
                    act.wait_ge(mem_turned, 2 * (u - 1))
                for b in range(TB):
                    act.activation(pm[:, u % 2, b, :], ps[:, 2 + b // 2, b % 2 * NMEM:(b % 2 + 1) * NMEM],
                                   ACT.Exp, bias=nmx[:, u % 2, b:b + 1],
                                   accum_out=den[:, u % 2, b:b + 1]).then_inc(mem_exp, 1)

            def mem_evac(layer, i):
                u, pT = 4 * layer + i, (pmT0, pmT1)[layer]
                act.wait_ge(mem_turned, 2 * u + 2)
                if i:
                    act.wait_ge(mem_pv, u)
                act.activation(pT[:, 1, :], ps[:, 5, :], ACT.Copy).then_inc(mem_pT1, 1)

            def mem_out(layer, t):
                act.wait_ge(mem_pv, 4 * layer + 2 * t + 2)
                act.activation(y_hi[:, CT + t, :], ps[:, 6 + t, :], ACT.Copy).then_inc(ym_hi_ready, 1)

            def mem_step(layer, n):
                if n in MEM_STEPS[layer]:
                    mem_exps(layer, MEM_STEPS[layer][n])
                if n - 1 in MEM_STEPS[layer]:
                    mem_evac(layer, MEM_STEPS[layer][n - 1])
                if n - 1 in MEM_STEPS[layer] and MEM_STEPS[layer][n - 1] % 2:
                    mem_out(layer, MEM_STEPS[layer][n - 1] // 2)

            split(0, KT * P)
            act.wait_ge(const_in, 16 * 3)
            for k in range(KT):
                act.wait_ge(x_in[k // 2], 16)
                square(V_MIX0, k, k % 2, x[:, k, :], first=k < 2)
                operand(k, G_MIX0)
                if k == 3:
                    split(1, KT * P)

            def l0_strip(n):
                if N_CONV0 <= n < N_MEMKV:
                    return "ucb"[n - N_CONV0], 0
                if n >= N_CONV:
                    return "ucb"[(n - N_CONV) % 3], 1 + (n - N_CONV) // 3
                return "q" if n < N_CONV0 else "m", 0

            def conv_out(i):
                act.wait_ge(conv_step, 5 * i + 5)
                act.activation(y_hi[:, i, :], y_s[:], ACT.Copy).then_inc(yc_hi_ready, 1)

            for n in range(N_QM0, N_OUT0 + 1):
                if n:
                    kind, i = l0_strip(n - 1)
                    if kind == "b":
                        conv_out(i)
                if n >= 1:
                    split(n + 1, KT * P)
                if n == 1:
                    act.wait_ge(mem_in, 16)
                    for k in range(KT):
                        square(V_MEM, k, k % 2, memx[:, k, :], NMEM, first=k < 2)
                if n == 2:
                    spread(V_MIX0, rstd[:])
                    act.wait_ge(table_mm, 1)
                    act.activation(table[:], ps[0:12, 6, 0:NREL], ACT.Copy).then_inc(table_ready, 1)
                if n == 4:
                    spread(V_MEM, rmem[:], NMEM)
                    for k in range(KT):
                        act.wait_ge(memx_ready, k + 1)
                        act.activation(mem_hi[:, k, :], memx[:, k, :], ACT.Copy).then_inc(mem_hi_ready, 1)
                mem_step(0, n)
            act.wait_ge(table_ready, 1)
            act.dma_start(scratch, table[:]).then_inc(table_out, 16)

            def out_phase(n0, v, g):
                for n in range(n0 + 1, n0 + KT):
                    residual(n - 1 - n0, out_index(n - 1), v, g, (n - 1 - n0) % 2, first=n - 1 - n0 < 2)
                    split(n + 1, KT * P)
                residual(KT - 1, out_index(n0 + KT - 1), v, g, 1)
                split(n0 + KT + 1, KT * P)

            def ffn(layer, n0, v, q0, r0):
                def body(i, first=False, last=False):
                    for j in range(2):
                        n = i * 4 + (n0 + 2 * j)
                        q = i * 4 + (q0 + 2 * j)
                        p = i * 2 + (FT * layer + j)
                        w = SLOT if last and j else KT * P
                        count = (i + (r0 + 1 + j)) * 16
                        m = i * 2 + j
                        if first and j == 0:
                            split(n + 2, w, 0, 2, count)
                            spread(v, rstd[:])
                        act.wait_ge(lin_read, q + 1)
                        act.activation(tmp[:, 2 * j, :], tmp[:, 2 * j, :], ACT.Silu).then_inc(silu_ready, 1)
                        if not (first and j == 0):
                            split(n + 2, w, 0, (2 * j + 2) % 4, count)
                        act.wait_ge(gu_ready, p + 1)
                        act.activation(g_hi[:, m, :], tmp[:, 2 * j + 1, :], ACT.Copy).then_inc(g_hi_ready, 1)
                        split(n + 3, w, 1, (2 * j + 3) % 4, count)
                body(0, first=True)
                with act.Fori(1, FT // 2 - 1, 1) as i:
                    body(i)
                body(FT // 2 - 1, last=True)

            def down(n0, q0, v, g, r0):
                def body(i, first=False, last=False):
                    for j in range(2):
                        n = i * 4 + (n0 + 2 * j)
                        w = KT * P if last and j else SLOT
                        count = (i + (r0 + 1 + (1 if j else 0))) * 16
                        split(n + 2, w, 0, (2 * j + 2) % 4, count)
                        residual(i * 2 + j, i * 2 + (q0 + j), v, g, j, first=first)
                        split(n + 3, w, 1, (2 * j + 3) % 4, count)
                body(0, first=True)
                with act.Fori(1, KT // 2 - 1, 1) as i:
                    body(i)
                body(KT // 2 - 1, last=True)

            out_phase(N_OUT0, V_FFN0, G_FFN0)
            ffn(0, N_FFN0, V_FFN0, out_index(N_FFN0), N_FFN0 // RAW)
            down(N_DOWN0, N_DOWN0, V_MIX1, G_MIX1, N_DOWN0 // RAW)

            act.dma_start(flip[:], a["flip"]).then_inc(band_in, 16)
            act.wait_ge(table_out, 16)
            toeplitz = bass.AP(tensor=scratch.tensor, offset=scratch.offset,
                               ap=[[1, P], [NREL, 12], [1, 256]])
            act.dma_start(band[:].rearrange("p (h j) -> p h j", h=12), toeplitz).then_inc(band_in, 16)
            for k in range(KT):
                act.activation(kv_hi[:, k, :], x[:, k, :], ACT.Copy, scale=gains[:, G_KV, k:k + 1])\
                    .then_inc(kv_hi_ready, 1)

            def sw_exps(u):
                hp, b, s, keys, _ = sw_unit(u)
                act.wait_ge(sw_sink, 2 * u + 2)
                if u >= 2:
                    act.wait_ge(sw_turned, 2 * (u - 1))
                for g in range(GROUP):
                    act.activation(p_sw[:, u % 2, g, 0:keys], s_sw[:, u % 2, g, 0:keys], ACT.Exp,
                                   bias=nmx[:, u % 2, g:g + 1], accum_out=den[:, u % 2, g:g + 1])\
                        .then_inc(sw_exp, 1)
                act.activation(es[:, u % 2, 0:GROUP], es[:, u % 2, 0:GROUP], ACT.Exp).then_inc(sw_exp, 1)

            def sw_evac(u):
                act.wait_ge(sw_turned, 2 * u + 2)
                if u:
                    act.wait_ge(sw_pv, u)
                act.activation(pT_sw[:, 1, :], ps[:, 7, 0:GROUP * P], ACT.Copy).then_inc(sw_pT1, 1)

            def sw_out(u):
                hp, b, s, _, _ = sw_unit(u)
                act.wait_ge(sw_pv, u + 1)
                act.activation(y_hi[:, GROUP * hp:GROUP * hp + GROUP, b * P:(b + 1) * P],
                               ps[:, 1, 0:GROUP * P].rearrange("p (g t) -> p g t", g=GROUP), ACT.Copy)\
                    .then_inc(ys_hi_ready, 1)

            def sw_step(u):
                if u < NSW:
                    sw_exps(u)
                if u and sw_unit(u - 1)[3] == 256:
                    sw_evac(u - 1)
                if u and u % 2 == 0:
                    sw_out(u - 1)

            for n in range(N_KV, N_OUT1 + 1):
                if n > N_KV:
                    split(n + 1, KT * P)
                if n == N_KV + 2:
                    spread(V_MIX1, rstd[:])
                mem_step(1, n)
                if SW_FIRST <= n < N_OUT1:
                    sw_step(n - SW_FIRST)
                if n == N_OUT1:
                    for u in range(n - SW_FIRST, NSW + 1):
                        sw_step(u)
            out_phase(N_OUT1, V_FFN1, G_FFN1)
            ffn(1, N_FFN1, V_FFN1, out_index(N_FFN1), N_FFN1 // RAW)
            act.wait_ge(gain_ready, 1)
            down(N_DOWN1, out_index(N_DOWN1), V_LAST, G_PRE, N_DOWN1 // RAW)

            act.wait_ge(lin_read, out_index(N_SECOND))
            act.dma_start(rope_n[:], a["rope"][0]).then_inc(rope_in, 16)
            act.dma_start(rope_r[:], a["rope"][1]).then_inc(rope_in, 16)

            def ns_exps(u):
                b, g, br, keys = ns_unit(u)
                act.wait_ge(ns_max, u + 1)
                if u >= 2:
                    act.wait_ge(ns_turned, GH * (u - 1))
                for j in range(GH):
                    act.activation(p_n[:, u % 2, j, 0:keys], ps[:, 2 + j, 0:keys], ACT.Exp,
                                   bias=nmx[:, u % 2, j:j + 1], accum_out=den[:, u % 2, j:j + 1])\
                        .then_inc(ns_exp, 1)

            def ns_evac(u):
                b, g, br, keys = ns_unit(u)
                if u:
                    act.wait_ge(ns_pv, u)
                for j in (1, 3):
                    act.wait_ge(ns_turned, GH * u + j + 1)
                    act.activation(pT_n[:, 0:b + 1, j * P:(j + 1) * P],
                                   ps[:, 7, 0:keys].rearrange("p (c t) -> p c t", t=P), ACT.Copy)\
                        .then_inc(ns_pTa, 1)
                if g and br:
                    act.wait_ge(ns_pv, u + 1)
                    act.activation(oa[:, :, b * P:(b + 1) * P],
                                   ps[:, 1, :].rearrange("p (j t) -> p j t", j=GH), ACT.Copy)\
                        .then_inc(oa_ready, 1)

            def ret_evac(h):
                act.wait_ge(rt_turned, 2 * h + 2)
                act.activation(ob[h // 2][:, h % 2 * 2 + 1, :], ps[:, 7, :], ACT.Copy).then_inc(rt_ob1, 1)

            def gate_strip(n, func):
                e = gated_index(n)
                act.wait_ge(lin_read, out_index(n) + 1)
                act.activation(tmp[:, e % 4, :], tmp[:, e % 4, :], func).then_inc(gated, 1)

            def rounded(i, src, dst):
                act.wait_ge(prod_ready, i + 1)
                act.activation(dst, src, ACT.Copy).then_inc(zh_ready, 1)

            def epilogue(n):
                e = gated_index(n)
                if n < N_ZN:
                    return
                if n < N_MA:
                    gate_strip(n, ACT.Silu)
                    rounded(n - N_ZN, tmp[:, e % 4, :], ya_hi[:, n - N_ZN, :])
                elif n < N_ZR:
                    if (n - N_MA) % 2 == 0:
                        gate_strip(n, ACT.Sigmoid)
                elif n < N_MB:
                    gate_strip(n, ACT.Silu)
                    rounded(4 + n - N_ZR, tmp[:, e % 4, :], yb_hi[:, n - N_ZR, :])
                elif n < N_FIN:
                    i = (n - N_MB) // 2
                    if (n - N_MB) % 2 == 0:
                        gate_strip(n, ACT.Sigmoid)
                    else:
                        rounded(12 + i, tmp[:, e % 4, :], mg_hi[:, i, :])
                else:
                    i = n - N_FIN
                    act.wait_ge(blk_done, n + 1)
                    square(V_POST - 1, i, i % 2, ps[:, n % 2, :], first=i < 2)
                    act.activation(yg[:, i, :], ps[:, n % 2, :], ACT.Copy,
                                   scale=gains[:, G_POST, i:i + 1]).then_inc(fin_read, 1)

            for n in range(N_SECOND, N_END):
                if n > N_SECOND:
                    epilogue(n - 1)
                    if n + 1 < N_END:
                        split(n + 1, width(n + 1))
                if n == N_SECOND + 3:
                    spread(V_LAST, rstd[:])
                if n == N_SECOND + 4:
                    spread(V_PRE, r1[:])
                if n in (N_SECOND + 6, N_RET):
                    i = 0 if n < N_RET else 1
                    act.wait_ge(cmp_hidden, i + 1)
                    if i:
                        act.wait_ge(cmp_mm, 1)
                    act.activation(hid[:], ps[:, 1 if i else 4, 0:4 * NCMP].rearrange("p (m c) -> p m c", m=2),
                                   ACT.Gelu_apprx_tanh).then_inc(cmp_gelu, 1)
                if n == N_RET:
                    act.wait_ge(small2_in, 16 * 6)
                    act.wait_ge(lin_read, out_index(N_GATE) + 1)
                    act.activation(tmp[0:24, 2, :], tmp[0:24, 2, :], ACT.Sigmoid, bias=gate_b[:])\
                        .then_inc(gate_sig, 1)
                if NS_FIRST <= n < NS_FIRST + NS:
                    ns_exps(n - NS_FIRST)
                if NS_FIRST <= n < NS_FIRST + 2:
                    g = n - NS_FIRST
                    act.wait_ge(cm_step, 3 * g + 3)
                    act.activation(p_c[:, g], p_c[:, g], ACT.Exp).then_inc(cm_exp, 1)
                if NS_FIRST < n <= NS_FIRST + NS:
                    ns_evac(n - 1 - NS_FIRST)
                if n == RT_FIRST - 1:
                    act.wait_ge(ns_turned, GH * NS)
                    act.dma_start(decay[:], a["decay"]).then_inc(decay_in, 16)
                if RT_FIRST + 2 <= n < RT_FIRST + 2 + RH:
                    ret_evac(n - RT_FIRST - 2)
            epilogue(N_END - 1)
            spread(V_POST, rstd[:])

        @block.vector
        def _(dve):
            def split(n, w, slot=None, raw_slot=None):
                slot = n % 2 if slot is None else slot
                raw_slot = n % RAW if raw_slot is None else raw_slot
                dve.wait_ge(w_hi_ready, n + 1)
                dve.tensor_tensor(w_lo[:, slot, 0:w], raw[:, raw_slot, 0:w],
                                  w_hi[:, slot, 0:w].bitcast(F32), ALU.subtract).then_inc(w_lo_ready, 1)

            def operand(k, g, count):
                dve.wait_ge(a_hi_ready, count)
                dve.scalar_tensor_tensor(a_lo[:, k, :], x[:, k, :], gains[:, g, bass.ds(k, 1)],
                                         a_hi[:, k, :].bitcast(F32), ALU.mult, ALU.subtract)\
                    .then_inc(a_lo_ready, 1)

            def variance(v, eps, tiles=TB):
                dve.wait_ge(norm_sum, v + 1)
                dve.tensor_scalar(var[:, 0:tiles], ps[:, stat_bank, 0:tiles], 1.0 / D, eps,
                                  ALU.mult, ALU.add).then_inc(norm_var, 1)

            def diagonal(v, tiles=TB, rs=rs):
                dve.wait_ge(norm_pow, v + 1)
                dve.tensor_tensor(diag[:, 0:tiles, :],
                                  ident[:].unsqueeze(1).to_broadcast([P, tiles, P]),
                                  rs[:, 0:tiles].unsqueeze(2).to_broadcast([P, tiles, P]), ALU.mult)\
                    .then_inc(norm_diag, 1)

            def scaled(n, bank, dst, factor=None):
                dve.wait_ge(blk_done, n + 1)
                if factor is None:
                    ins = dve.tensor_tensor(dst, ps[:, bank, :], rstd[:], ALU.mult)
                else:
                    ins = dve.scalar_tensor_tensor(dst, ps[:, bank, :], factor, rstd[:], ALU.mult, ALU.mult)
                ins.then_inc(lin_read, 1)

            def plain(n, bank, dst, cols=S):
                dve.wait_ge(blk_done, n + 1)
                dve.tensor_copy(dst, ps[:, bank, 0:cols]).then_inc(lin_read, 1)

            def residual(k, n, bank, g, count):
                dve.wait_ge(blk_done, n + 1)
                dve.tensor_tensor(x[:, k, :], x[:, k, :], ps[:, bank, :], ALU.add).then_inc(lin_read, 1)

            def mem_maxima(layer, i):
                u = 4 * layer + i
                dve.wait_ge(mem_scores, u + 1)
                dve.tensor_reduce(nmx[:, u % 2, :], ps[:, 2:4, :].rearrange("p k (b m) -> p (k b) m", b=2),
                                  AX.X, ALU.max, negate=True).then_inc(mem_max, 1)

            def mem_normalise(layer, i):
                u, pm = 4 * layer + i, (pm0, pm1)[layer]
                dve.wait_ge(mem_exp, 4 * u + 4)
                dve.reciprocal(den[:, u % 2, :], den[:, u % 2, :]).then_inc(mem_rden, 1)
                dve.wait_ge(mem_rden, u + 1)
                dve.tensor_tensor(pm[:, u % 2], pm[:, u % 2],
                                  den[:, u % 2, :].unsqueeze(2).to_broadcast([P, TB, NMEM]), ALU.mult)\
                    .then_inc(mem_probs, 1)

            def mem_evac(layer, i):
                u, pT = 4 * layer + i, (pmT0, pmT1)[layer]
                dve.wait_ge(mem_turned, 2 * u + 1)
                if i:
                    dve.wait_ge(mem_pv, u)
                dve.tensor_copy(pT[:, 0, :], ps[:, 4, :]).then_inc(mem_pT0, 1)

            def mem_out(layer, t):
                dve.wait_ge(ym_hi_ready, 2 * layer + t + 1)
                dve.tensor_tensor(y_lo[:, CT + t, :], ps[:, 6 + t, :], y_hi[:, CT + t, :].bitcast(F32),
                                  ALU.subtract).then_inc(ym_lo_ready, 1)

            def mem_step(layer, n):
                if n in MEM_STEPS[layer]:
                    mem_maxima(layer, MEM_STEPS[layer][n])
                if n - 1 in MEM_STEPS[layer]:
                    mem_normalise(layer, MEM_STEPS[layer][n - 1])
                    mem_evac(layer, MEM_STEPS[layer][n - 1])
                if n - 1 in MEM_STEPS[layer] and MEM_STEPS[layer][n - 1] % 2:
                    mem_out(layer, MEM_STEPS[layer][n - 1] // 2)

            split(0, KT * P)
            for k in range(KT):
                operand(k, G_MIX0, k + 1)
                if k == 3:
                    split(1, KT * P)

            def l0_epilogue(n):
                bank = bank_of(n)
                if n < N_CONV0:
                    scaled(n, bank, qm0[:, n, :], SCALE)
                    return
                if N_MEMKV <= n < N_CONV:
                    t = n - N_MEMKV
                    if t < 4:
                        plain(n, bank, (mk0, mk1)[t // 2][:, t % 2, :], NMEM)
                    else:
                        t -= 4
                        if t:
                            dve.wait_ge(mv_turned, t)
                        plain(n, bank, mvt[:], NMEM)
                    return
                i = 0 if n < N_CONV else 1 + (n - N_CONV) // 3
                what = n - N_CONV0 if n < N_CONV else (n - N_CONV) % 3
                if what == 0:
                    scaled(n, bank, u_s[:])
                elif what == 1:
                    scaled(n, bank, v_s[:])
                    dve.wait_ge(lin_read, n + 1)
                    dve.tensor_tensor(v_s[:], v_s[:], u_s[:], ALU.mult).then_inc(conv_step, 1)
                    dve.wait_ge(conv_step, 5 * i + 1)
                    dve.tensor_scalar(y_s[:], v_s[:], conv_w[:, i, 2:3], None, ALU.mult)\
                        .then_inc(conv_step, 1)
                    for back in (1, 2):
                        dve.wait_ge(conv_step, 5 * i + 1 + back)
                        dve.scalar_tensor_tensor(y_s[:, back:S], v_s[:, 0:S - back],
                                                 conv_w[:, i, 2 - back:3 - back], y_s[:, back:S],
                                                 ALU.mult, ALU.add).then_inc(conv_step, 1)
                else:
                    scaled(n, bank, u_s[:])
                    dve.wait_ge(lin_read, n + 1)
                    dve.tensor_tensor(y_s[:], y_s[:], u_s[:], ALU.mult).then_inc(conv_step, 1)
                    dve.wait_ge(yc_hi_ready, i + 1)
                    dve.tensor_tensor(y_lo[:, i, :], y_s[:], y_hi[:, i, :].bitcast(F32), ALU.subtract)\
                        .then_inc(yc_lo_ready, 1)

            def mv_evac(t):
                dve.wait_ge(mv_turned, t + 1)
                dst = (mv0, mv1)[t // 2][:, :, t % 2 * P:(t % 2 + 1) * P]
                dve.tensor_copy(dst, ps[:, 6, 0:NMEM].rearrange("p (m f) -> p m f", m=2))\
                    .then_inc(mv_ready, 1)

            for n in range(N_QM0, N_OUT0 + 1):
                if n == 2:
                    diagonal(V_MIX0)
                    dve.wait_ge(rstd_ready, 1)
                    l0_epilogue(0)
                if n >= 2:
                    l0_epilogue(n - 1)
                if n >= 1:
                    split(n + 1, KT * P)
                if n == 1:
                    variance(V_MIX0, EPS_A)
                if n == 3:
                    variance(V_MEM, EPS_A, 2)
                if n == 4:
                    diagonal(V_MEM, 2)
                    dve.wait_ge(rstd_ready, 2)
                    for k in range(KT):
                        dve.scalar_tensor_tensor(memx[:, k, :], memx[:, k, :], gains[:, G_MEM, k:k + 1],
                                                 rmem[:], ALU.mult, ALU.mult).then_inc(memx_ready, 1)
                    for k in range(KT):
                        dve.wait_ge(mem_hi_ready, k + 1)
                        dve.tensor_tensor(mem_lo[:, k, :], memx[:, k, :], mem_hi[:, k, :].bitcast(F32),
                                          ALU.subtract).then_inc(mem_lo_ready, 1)
                if N_MEMKV + 6 <= n <= N_MEMKV + 9:
                    mv_evac(n - N_MEMKV - 6)
                mem_step(0, n)

            def out_phase(n0, g, count):
                for m in range(KT):
                    residual(m, n0 + m, (n0 + m) % 2, g, 0)
                    operand(m, g, count + m + 1)
                    split(n0 + m + 2, KT * P)

            def ffn(layer, n0, v, q0):
                def body(i, first=False, last=False):
                    for j in range(2):
                        n = i * 4 + (n0 + 2 * j)
                        q = i * 4 + (q0 + 2 * j)
                        p = i * 2 + (FT * layer + j)
                        w = SLOT if last and j else KT * P
                        if first and j == 0:
                            diagonal(v)
                            split(n + 2, w, 0, 2)
                            dve.wait_ge(rstd_ready, v + 1)
                        scaled(n, 2 * j, tmp[:, 2 * j, :])
                        if not (first and j == 0):
                            split(n + 2, w, 0, (2 * j + 2) % 4)
                        scaled(n + 1, 2 * j + 1, tmp[:, 2 * j + 1, :])
                        dve.wait_ge(silu_ready, p + 1)
                        dve.wait_ge(lin_read, q + 2)
                        dve.tensor_tensor(tmp[:, 2 * j + 1, :], tmp[:, 2 * j, :], tmp[:, 2 * j + 1, :],
                                          ALU.mult).then_inc(gu_ready, 1)
                        dve.wait_ge(g_hi_ready, p + 1)
                        m = i * 2 + j
                        dve.tensor_tensor(g_lo[:, m, :], tmp[:, 2 * j + 1, :],
                                          g_hi[:, m, :].bitcast(F32), ALU.subtract)\
                            .then_inc(g_lo_ready, 1)
                        split(n + 3, w, 1, (2 * j + 3) % 4)
                variance(v, EPS_A)
                body(0, first=True)
                with dve.Fori(1, FT // 2 - 1, 1) as i:
                    body(i)
                body(FT // 2 - 1, last=True)

            def down(n0, g, count):
                def body(i, last=False):
                    for j in range(2):
                        n = i * 4 + (n0 + 2 * j)
                        m = i * 2 + j
                        w = KT * P if last and j else SLOT
                        split(n + 2, w, 0, (2 * j + 2) % 4)
                        residual(m, n + 1, j, g, 0)
                        operand(m, g, i * 2 + (count + j + 1))
                        split(n + 3, w, 1, (2 * j + 3) % 4)
                with dve.Fori(0, KT // 2 - 1, 1) as i:
                    body(i)
                body(KT // 2 - 1, last=True)

            out_phase(N_OUT0, G_FFN0, KT)
            dve.wait_ge(table_out, 16)
            dve.tensor_tensor(gains[:, G_PRE, :], gains[:, G_PRE, :], gains[:, G_FINAL, :], ALU.mult)\
                .then_inc(gain_ready, 1)
            ffn(0, N_FFN0, V_FFN0, out_index(N_FFN0))
            down(N_DOWN0, G_MIX1, 2 * KT)

            dve.wait_ge(small_in, 16 * 4)
            dve.tensor_scalar(nsink[:], sinks[:], -1.0, None, ALU.mult).then_inc(nsink_ready, 1)
            for k in range(KT):
                dve.wait_ge(kv_hi_ready, k + 1)
                dve.scalar_tensor_tensor(kv_lo[:, k, :], x[:, k, :], gains[:, G_KV, k:k + 1],
                                         kv_hi[:, k, :].bitcast(F32), ALU.mult, ALU.subtract)\
                    .then_inc(kv_lo_ready, 1)

            def sw_maxima(u):
                hp, b, s, keys, _ = sw_unit(u)
                h = 2 * hp + s
                lg = ps[:, 2 + 2 * (u % 2):4 + 2 * (u % 2), :].rearrange("p k (g m) -> p (k g) m", g=2)
                dve.wait_ge(sw_scores, u + 1)
                dve.tensor_tensor(s_sw[:, u % 2, :, 0:keys], lg[:, 0:GROUP, 0:keys],
                                  bias[:, GROUP * h:GROUP * h + GROUP, 256 - keys:256], ALU.add)\
                    .then_inc(sw_biased, 1)
                dve.wait_ge(sw_biased, u + 1)
                dve.tensor_reduce(nmx[:, u % 2, 0:GROUP], s_sw[:, u % 2, :, 0:keys], AX.X, ALU.max,
                                  negate=True).then_inc(sw_max, 1)
                dve.wait_ge(sw_max, u + 1)
                dve.wait_ge(nsink_ready, 1)
                dve.tensor_tensor(nmx[:, u % 2, 0:GROUP], nmx[:, u % 2, 0:GROUP],
                                  nsink[:, GROUP * h:GROUP * h + GROUP], ALU.min).then_inc(sw_sink, 1)
                dve.wait_ge(sw_sink, 2 * u + 1)
                dve.tensor_tensor(es[:, u % 2, 0:GROUP], nmx[:, u % 2, 0:GROUP],
                                  sinks[:, GROUP * h:GROUP * h + GROUP], ALU.add).then_inc(sw_sink, 1)

            def sw_normalise(u):
                keys = sw_unit(u)[3]
                dve.wait_ge(sw_exp, 4 * u + 4)
                dve.tensor_tensor(den[:, u % 2, 0:GROUP], den[:, u % 2, 0:GROUP],
                                  es[:, u % 2, 0:GROUP], ALU.add).then_inc(sw_den, 1)
                dve.wait_ge(sw_den, 2 * u + 1)
                dve.reciprocal(den[:, u % 2, 0:GROUP], den[:, u % 2, 0:GROUP]).then_inc(sw_den, 1)
                dve.wait_ge(sw_den, 2 * u + 2)
                dve.tensor_tensor(p_sw[:, u % 2, :, 0:keys], p_sw[:, u % 2, :, 0:keys],
                                  den[:, u % 2, 0:GROUP].unsqueeze(2).to_broadcast([P, GROUP, keys]),
                                  ALU.mult).then_inc(sw_probs, 1)

            def sw_evac(u):
                dve.wait_ge(sw_turned, 2 * u + (1 if sw_unit(u)[3] > P else 2))
                if u:
                    dve.wait_ge(sw_pv, u)
                dve.tensor_copy(pT_sw[:, 0, :], ps[:, 6, 0:GROUP * P]).then_inc(sw_pT0, 1)

            def sw_out(u):
                hp, b, s, _, _ = sw_unit(u)
                dve.wait_ge(ys_hi_ready, u // 2 + 1)
                dve.tensor_tensor(y_lo[:, GROUP * hp:GROUP * hp + GROUP, b * P:(b + 1) * P],
                                  ps[:, 1, 0:GROUP * P].rearrange("p (g t) -> p g t", g=GROUP),
                                  y_hi[:, GROUP * hp:GROUP * hp + GROUP, b * P:(b + 1) * P].bitcast(F32),
                                  ALU.subtract).then_inc(ys_lo_ready, 1)

            def sw_step(u):
                if u < NSW:
                    sw_maxima(u)
                if u:
                    sw_normalise(u - 1)
                    sw_evac(u - 1)
                if u and u % 2 == 0:
                    sw_out(u - 1)

            def l1_epilogue(n):
                if n < N_KV + 2:
                    scaled(n, bank_of(n), kT[:, n - N_KV, :])
                elif n < N_QM1:
                    if n > N_KV + 2:
                        dve.wait_ge(v_turned, 1)
                    scaled(n, bank_of(n), vT[:])
                elif n < N_Q:
                    scaled(n, bank_of(n), qm1[:, n - N_QM1, :], SCALE)
                else:
                    scaled(n, bank_of(n), qT[:, n - N_Q, :], SCALE)

            for n in range(N_KV, N_OUT1 + 1):
                if n == N_KV + 2:
                    diagonal(V_MIX1)
                    split(n + 1, KT * P)
                    dve.wait_ge(rstd_ready, V_MIX1 + 1)
                    l1_epilogue(N_KV)
                if n >= N_KV + 2:
                    l1_epilogue(n - 1)
                if n > N_KV and n != N_KV + 2:
                    split(n + 1, KT * P)
                if n == N_KV + 1:
                    variance(V_MIX1, EPS_A)
                if n in (N_KV + 4, N_KV + 5):
                    t = n - N_KV - 4
                    dve.wait_ge(v_turned, t + 1)
                    dve.tensor_copy(vn[:, :, t * P:(t + 1) * P],
                                    ps[:, 7, :].rearrange("p (b f) -> p b f", b=TB)).then_inc(vn_ready, 1)
                if n in (N_KV + 3, N_KV + 4):
                    for c in range(3 * (n - N_KV - 3), 3 * (n - N_KV - 3) + 3):
                        dve.wait_ge(flip_mm, c + 1)
                        dve.tensor_copy(bias[:].rearrange("p h j -> p (h j)")[:, c * S:(c + 1) * S],
                                        ps[:, 4 + c % 3, :]).then_inc(bias_ready, 1)
                mem_step(1, n)
                if SW_FIRST <= n < N_OUT1:
                    sw_step(n - SW_FIRST)
                if n == N_OUT1:
                    for u in range(n - SW_FIRST, NSW + 1):
                        sw_step(u)
            out_phase(N_OUT1, G_FFN1, 3 * KT)
            ffn(1, N_FFN1, V_FFN1, out_index(N_FFN1))
            dve.wait_ge(gain_ready, 1)
            down(N_DOWN1, G_PRE, 4 * KT)

            def rotate(n):
                kind, dst = ROPE[n]
                i = turned_before(n)[0]
                table_of = (rope_n, rope_r)[kind]
                src = strip_of(n)
                dve.wait_ge(rope_in, 16 * 2)
                dve.wait_ge(lin_read, out_index(n) + 1)
                dve.tensor_tensor(dst, src, table_of[:, 0, :], ALU.mult).then_inc(rope_mul, 1)
                dve.wait_ge(rope_mm, i + 1)
                dve.wait_ge(rope_mul, 2 * i + 1)
                dve.tensor_tensor(src, ps[:, turn_bank(n), :], table_of[:, 1, :], ALU.mult)\
                    .then_inc(rope_mul, 1)
                dve.wait_ge(rope_mul, 2 * i + 2)
                dve.tensor_tensor(dst, dst, src, ALU.add).then_inc(rope_ready, 1)

            def turn(n):
                dve.wait_ge(turn_mm, turned_before(n)[1] + 1)
                dve.tensor_copy(TURN[n], ps[:, turn_bank(n), :].rearrange("p (b f) -> p b f", b=TB))\
                    .then_inc(turn_ready, 1)

            def blocks_of(i):
                src = (kcr, vcr)[i][:].rearrange("p (c l) -> p l c", l=CSTRIDE)
                if i == 0:
                    dve.wait_ge(rope_ready, 1)
                else:
                    dve.wait_ge(lin_read, out_index(N_SECOND + 1) + 1)
                dve.wait_ge(bd_clear, 2)
                dve.wait_ge(small2_in, 16 * 6)
                for g in range(2):
                    r = slice(HD * g, HD * g + HD)
                    for w in range(2):
                        ls = slice(CSTRIDE * w, CSTRIDE * w + CSTRIDE)
                        dve.tensor_tensor(bd[i][r, ls, g * NCMP:(g + 1) * NCMP], src[r, :, w:w + NCMP],
                                          pe2[r, i, ls].unsqueeze(2).to_broadcast([HD, CSTRIDE, NCMP]),
                                          ALU.add).then_inc(bd_ready, 1)

            def cmp_maxima(g):
                s = ps[:, 7, 0:16 * NCMP].rearrange("p (k c) -> p k c", c=NCMP)
                dve.wait_ge(cm_scores, g + 1)
                dve.tensor_reduce(nm16[:], s, AX.X, ALU.max, negate=True).then_inc(cm_step, 1)
                dve.wait_ge(cm_step, 3 * g + 1)
                dve.tensor_scalar(nm16[:], nm16[:], -EMPTY, None, ALU.min).then_inc(cm_step, 1)
                dve.wait_ge(cm_step, 3 * g + 2)
                dve.tensor_tensor(p_c[:, g], s, nm16[:].unsqueeze(2).to_broadcast([P, 16, NCMP]), ALU.add)\
                    .then_inc(cm_step, 1)

            def cmp_normalise(g):
                dve.wait_ge(cm_exp, g + 1)
                dve.tensor_reduce(d16[:], p_c[:, g], AX.X, ALU.add).then_inc(cm_probs, 1)
                dve.wait_ge(cm_probs, 5 * g + 1)
                dve.tensor_scalar(d16[:], d16[:], TINY, None, ALU.max).then_inc(cm_probs, 1)
                dve.wait_ge(cm_probs, 5 * g + 2)
                dve.reciprocal(d16[:], d16[:]).then_inc(cm_probs, 1)
                dve.wait_ge(cm_probs, 5 * g + 3)
                dve.wait_ge(gate_ready, 1)
                w = d16[:].rearrange("p (b j) -> p b j", b=TB)
                dve.tensor_tensor(w, w, gate_n[:, :, 12 * g:12 * g + 12:3], ALU.mult).then_inc(cm_probs, 1)
                dve.wait_ge(cm_probs, 5 * g + 4)
                dve.tensor_tensor(p_c[:, g], p_c[:, g], d16[:].unsqueeze(2).to_broadcast([P, 16, NCMP]),
                                  ALU.mult).then_inc(cm_probs, 1)

            def ns_maxima(u):
                keys = ns_unit(u)[3]
                dve.wait_ge(ns_scores, u + 1)
                dve.tensor_reduce(nmx[:, u % 2, :], ps[:, 2:6, 0:keys], AX.X, ALU.max, negate=True)\
                    .then_inc(ns_max, 1)

            def ns_normalise(u):
                b, g, br, keys = ns_unit(u)
                dve.wait_ge(ns_exp, GH * u + GH)
                dve.reciprocal(den[:, u % 2, :], den[:, u % 2, :]).then_inc(ns_den, 1)
                dve.wait_ge(ns_den, 2 * u + 1)
                dve.wait_ge(gate_ready, 1)
                dve.tensor_tensor(den[:, u % 2, :], den[:, u % 2, :],
                                  gate_n[:, b, 12 * g + 1 + br:12 * g + 12:3], ALU.mult).then_inc(ns_den, 1)
                dve.wait_ge(ns_den, 2 * u + 2)
                dve.tensor_tensor(p_n[:, u % 2, :, 0:keys], p_n[:, u % 2, :, 0:keys],
                                  den[:, u % 2, :].unsqueeze(2).to_broadcast([P, GH, keys]), ALU.mult)\
                    .then_inc(ns_probs, 1)

            def ns_evac(u):
                b, g, br, keys = ns_unit(u)
                if u:
                    dve.wait_ge(ns_pv, u)
                for j in (0, 2):
                    dve.wait_ge(ns_turned, GH * u + j + 1)
                    dve.tensor_copy(pT_n[:, 0:b + 1, j * P:(j + 1) * P],
                                    ps[:, 6, 0:keys].rearrange("p (c t) -> p c t", t=P)).then_inc(ns_pTd, 1)
                if br:
                    dve.wait_ge(cm_turned, u // 2 + 1)
                    dve.tensor_copy(pT_c[:], ps[0:NCMP, 6, :]).then_inc(cm_pT, 1)

            def ret_mask(h):
                if h == 0:
                    dve.wait_ge(decay_in, 16)
                else:
                    dve.wait_ge(rt_out, h)
                dve.wait_ge(rt_scores, h + 1)
                for jc, (bank, c) in enumerate(((2, 0), (3, 0), (4, 0), (3, 3 * P))):
                    w = S - jc * P
                    dve.tensor_tensor(att[:, jc, 0:w], ps[:, bank, c:c + w], decay[:, h, 0:w], ALU.mult)\
                        .then_inc(rt_att, 1)

            def ret_bank(ic):
                return ps[:, (1, 5)[ic // 2], ic % 2 * RDV:(ic % 2 + 1) * RDV]

            def ret_norm(h):
                dve.wait_ge(rt_out, h + 1)
                for ic in range(TB):
                    dve.bn_stats(bn6[:, ic, :], ret_bank(ic)).then_inc(rt_stats, 1)
                for ic in range(TB):
                    dve.wait_ge(rt_stats, 8 * h + ic + 1)
                    dve.bn_aggr(bn2[:, h % 2, ic, :], bn6[:, ic, :]).then_inc(rt_stats, 1)
                dve.wait_ge(rt_stats, 8 * h + 8)
                dve.tensor_scalar(bn2[:, h % 2, :, 1], bn2[:, h % 2, :, 1], EPS_B, None, ALU.add)\
                    .then_inc(rt_var, 1)
                dve.wait_ge(rt_pow, h + 1)
                if h:
                    dve.wait_ge(rt_turned, 2 * h)
                for ic in range(TB):
                    dve.tensor_scalar(on[:, ic, :], ret_bank(ic), bn2[:, h % 2, ic, 0:1],
                                      bn2[:, h % 2, ic, 1:2], ALU.subtract, ALU.mult).then_inc(rt_norm, 1)

            def ret_evac(h):
                dve.wait_ge(rt_turned, 2 * h + 1)
                dve.tensor_copy(ob[h // 2][:, h % 2 * 2, :], ps[:, 6, :]).then_inc(rt_ob0, 1)

            def left_over(i, src, hi, lo):
                dve.wait_ge(zh_ready, i + 1)
                dve.tensor_tensor(lo, src, hi.bitcast(F32), ALU.subtract).then_inc(zl_ready, 1)

            def epilogue(n):
                bank, q = bank_of(n), out_index(n)
                e = gated_index(n)
                t = tmp[:, e % 4, :]
                if n == N_SECOND + 1:
                    scaled(n, bank, vcr[:])
                elif n == N_GATE:
                    dve.wait_ge(blk_done, n + 1)
                    dve.tensor_tensor(tmp[0:24, 2, :], ps[0:24, bank, :], rstd[0:24, :], ALU.mult)\
                        .then_inc(lin_read, 1)
                elif n < N_ZN:
                    head = (n - N_RET) % 4 if n >= N_RET else -1
                    factor = SCALE if N_SECOND + 4 <= n < N_SECOND + 8 else (P ** -0.5 if head == 1 else None)
                    scaled(n, bank, strip_of(n), factor)
                elif n < N_MA or N_ZR <= n < N_MB:
                    i = n - N_ZN if n < N_MA else n - N_ZR
                    scaled(n, bank, t)
                    if n < N_MA:
                        dve.wait_ge(oa_ready, TB)
                        o, hi, lo, k = oa[:, i, :], ya_hi, ya_lo, i
                    else:
                        dve.wait_ge(rt_ob1, RH)
                        o, hi, lo, k = ob[i // 4][:, i % 4, :], yb_hi, yb_lo, 4 + i
                    dve.wait_ge(gated, e + 1)
                    dve.tensor_tensor(t, t, o, ALU.mult).then_inc(prod_ready, 1)
                    left_over(k, t, hi[:, i, :], lo[:, i, :])
                elif n < N_ZR:
                    i = (n - N_MA) // 2
                    if (n - N_MA) % 2 == 0:
                        scaled(n, bank, t)
                    else:
                        dve.wait_ge(blk_done, n + 1)
                        dve.wait_ge(gated, e + 1)
                        dve.tensor_tensor(merged[:, i, :], t, ps[:, bank, :], ALU.mult).then_inc(lin_read, 1)
                elif n < N_FIN:
                    i = (n - N_MB) // 2
                    if (n - N_MB) % 2 == 0:
                        scaled(n, bank, t)
                    else:
                        dve.wait_ge(blk_done, n + 1)
                        dve.wait_ge(gated, e + 1)
                        dve.tensor_tensor(t, t, ps[:, bank, :], ALU.mult).then_inc(lin_read, 1)
                        dve.wait_ge(lin_read, q + 1)
                        dve.tensor_tensor(t, t, merged[:, i, :], ALU.add).then_inc(prod_ready, 1)
                        left_over(12 + i, t, mg_hi[:, i, :], mg_lo[:, i, :])

            for n in range(N_SECOND, N_END):
                if n == N_SECOND + 3:
                    dve.wait_ge(rstd_ready, V_LAST + 1)
                    epilogue(N_SECOND)
                    epilogue(N_SECOND + 1)
                if n >= N_SECOND + 3:
                    epilogue(n - 1)
                if N_SECOND < n < N_END - 1:
                    split(n + 1, width(n + 1))
                if n == N_SECOND + 1:
                    dve.wait_ge(norm_sum, V_PRE + 1)
                    variance(V_LAST, EPS_A)
                if n == N_SECOND + 2:
                    dve.wait_ge(norm_sum, V_PRE + 1)
                    dve.wait_ge(norm_pow, V_LAST + 1)
                    dve.tensor_tensor(rs3[:], rs[:], rs[:], ALU.mult).then_inc(pre_step, 1)
                    dve.wait_ge(pre_step, 1)
                    dve.tensor_tensor(rs3[:], rs3[:], ps[:, stat_bank, TB:2 * TB], ALU.mult)\
                        .then_inc(pre_step, 1)
                    dve.wait_ge(pre_step, 2)
                    dve.tensor_scalar(var[:], rs3[:], 1.0 / D, EPS_B, ALU.mult, ALU.add).then_inc(norm_var, 1)
                    dve.wait_ge(norm_pow, V_PRE + 1)
                    dve.tensor_tensor(rs2[:], rs2[:], rs[:], ALU.mult).then_inc(pre_step, 1)
                    dve.wait_ge(pre_step, 3)
                    diagonal(V_LAST, rs=rs2)
                if n == N_SECOND + 3:
                    dve.wait_ge(norm_spread, V_LAST + 1)
                    diagonal(V_PRE)
                for m in handled(n):
                    (rotate if m in ROPE else turn)(m)
                if N_SECOND + 4 <= n < N_SECOND + 12:
                    k = n - N_SECOND - 4
                    dve.wait_ge(rstd_ready, V_PRE + 1)
                    dve.scalar_tensor_tensor(x[:, k, :], x[:, k, :], gains[:, G_FINAL, k:k + 1], r1[:],
                                             ALU.mult, ALU.mult).then_inc(x1_ready, 1)
                if n == N_SECOND + 4:
                    blocks_of(0)
                if n == N_SECOND + 5:
                    blocks_of(1)
                if n == N_SECOND + 7:
                    dve.wait_ge(cmp_mm, 1)
                    dve.tensor_copy(kc[:], ps[:, 4, P:P + NCMP]).then_inc(cmp_ready, 1)
                if n == N_RET + 1:
                    dve.wait_ge(cmp_mm, 2)
                    dve.tensor_copy(vc[:], ps[0:NCMP, 1, P:2 * P].rearrange("p (g d) -> p g d", g=2))\
                        .then_inc(cmp_ready, 1)
                    dve.wait_ge(gate_mm, 1)
                    dve.tensor_copy(gate_n[:], ps[:, 6, 0:24 * TB].rearrange("p (b c) -> p b c", b=TB))\
                        .then_inc(gate_ready, 1)
                if NS_FIRST <= n < NS_FIRST + NS:
                    ns_maxima(n - NS_FIRST)
                if NS_FIRST <= n < NS_FIRST + 2:
                    cmp_maxima(n - NS_FIRST)
                if NS_FIRST < n <= NS_FIRST + NS:
                    ns_normalise(n - 1 - NS_FIRST)
                    if n <= NS_FIRST + 2:
                        cmp_normalise(n - 1 - NS_FIRST)
                    ns_evac(n - 1 - NS_FIRST)
                if RT_FIRST <= n < RT_FIRST + RH:
                    ret_mask(n - RT_FIRST)
                if RT_FIRST + 1 <= n < RT_FIRST + 1 + RH:
                    ret_norm(n - RT_FIRST - 1)
                if RT_FIRST + 2 <= n < RT_FIRST + 2 + RH:
                    ret_evac(n - RT_FIRST - 2)
            variance(V_POST, EPS_B)
            diagonal(V_POST)
            dve.wait_ge(rstd_ready, V_POST + 1)
            dve.wait_ge(fin_read, KT)
            dve.wait_ge(x1_ready, KT)
            for k in range(KT):
                dve.tensor_tensor(yg[:, k, :], yg[:, k, :], rstd[:], ALU.mult).then_inc(fin_gain, 1)
                dve.wait_ge(fin_gain, k + 1)
                dve.tensor_tensor(x[:, k, :], x[:, k, :], yg[:, k, :], ALU.add).then_inc(out_part, 1)

        @block.tensor
        def _(pe):
            def strip(n, hi, lo, bank, kt=KT, k0=0, cols=S, slot=None, start=True, stop=True,
                      ready=None, rows=P):
                slot = n % 2 if slot is None else slot
                pe.wait_ge(w_lo_ready, n + 1)
                o = ps[0:rows, bank, 0:cols]
                for k in range(kt):
                    if ready:
                        pe.wait_ge(ready[0], ready[1] + k + 1)
                    wh = w_hi[:, slot, k * rows:(k + 1) * rows]
                    wl = w_lo[:, slot, k * rows:(k + 1) * rows]
                    pe.matmul(o, wh, hi[:, k0 + k, 0:cols], start=start and k == 0, stop=False)
                    pe.matmul(o, wh, lo[:, k0 + k, 0:cols], start=False, stop=False)
                    ins = pe.matmul(o, wl, hi[:, k0 + k, 0:cols], start=False, stop=stop and k == kt - 1)
                ins.then_inc(blk_done, 1)

            def sums(v, tiles=TB):
                pe.wait_ge(acc_ready, SQUARES * (v + 1))
                for c in range(tiles):
                    ins = pe.matmul(ps[:, stat_bank, c:c + 1], acc[:, c * P:(c + 1) * P], ones[:, 0:1],
                                    start=True, stop=True)
                ins.then_inc(norm_sum, 1)

            def spread(v, tiles=TB):
                pe.wait_ge(norm_diag, v + 1)
                pe.matmul(ps[:, stat_bank, 0:tiles * P], ones[:],
                          diag[:, 0:tiles, :].rearrange("p b t -> p (b t)"),
                          start=True, stop=True).then_inc(norm_spread, 1)

            def mem_scores_of(layer, i):
                u, q, mk = 4 * layer + i, (qm0, qm1)[layer], (mk0, mk1)[layer]
                r, t = HD * (i % 2), i // 2
                if i:
                    pe.wait_ge(mem_exp, 4 * u)
                for b in range(TB):
                    ins = pe.matmul(ps[:, 2 + b // 2, b % 2 * NMEM:(b % 2 + 1) * NMEM],
                                    q[r:r + HD, t, b * P:(b + 1) * P], mk[r:r + HD, t, :],
                                    start=True, stop=True)
                ins.then_inc(mem_scores, 1)

            def mem_turn(layer, i):
                u, pm = 4 * layer + i, (pm0, pm1)[layer]
                pe.wait_ge(mem_probs, u + 1)
                for c in range(2):
                    for b in range(TB):
                        ins = pe.transpose(ps[:, 4 + c, b * P:(b + 1) * P],
                                           pm[:, u % 2, b, c * P:(c + 1) * P], ident[:])
                    ins.then_inc(mem_turned, 1)

            def mem_values(layer, i):
                u, pT, mv = 4 * layer + i, (pmT0, pmT1)[layer], (mv0, mv1)[layer]
                r, t = HD * (i % 2), i // 2
                pe.wait_ge(mem_pT0, u + 1)
                pe.wait_ge(mem_pT1, u + 1)
                for c in range(2):
                    ins = pe.matmul(ps[r:r + HD, 6 + t, :], mv[:, c, t * P + r:t * P + r + HD],
                                    pT[:, c, :], start=(c == 0), stop=(c == 1))
                ins.then_inc(mem_pv, 1)

            def mem_step(layer, n):
                if n in MEM_STEPS[layer]:
                    mem_scores_of(layer, MEM_STEPS[layer][n])
                if n - 1 in MEM_STEPS[layer]:
                    mem_turn(layer, MEM_STEPS[layer][n - 1])
                    mem_values(layer, MEM_STEPS[layer][n - 1])

            pe.wait_ge(ones_ready, 1)
            pe.wait_ge(half_ready, 1)
            for n in range(N_QM0, N_OUT0):
                if n == 1:
                    pe.wait_ge(small_in, 16 * 4)
                    pe.matmul(ps[0:12, 6, 0:NREL], rb[:], onehot[:], start=True, stop=True)\
                        .then_inc(table_mm, 1)
                    sums(V_MIX0)
                if n == 2:
                    spread(V_MIX0)
                if n == 3:
                    pe.wait_ge(rstd_ready, 1)
                    sums(V_MEM, 2)
                if n == 4:
                    spread(V_MEM, 2)
                if N_MEMKV + 6 <= n <= N_MEMKV + 9:
                    t = n - N_MEMKV - 6
                    pe.wait_ge(lin_read, n - 1)
                    if t:
                        pe.wait_ge(mv_ready, t)
                    else:
                        pe.wait_ge(table_ready, 1)
                    for m in range(2):
                        ins = pe.transpose(ps[:, 6, m * P:(m + 1) * P], mvt[:, m * P:(m + 1) * P], ident[:])
                    ins.then_inc(mv_turned, 1)
                if n == N_CONV + 1:
                    pe.wait_ge(lin_read, N_CONV)
                if n == N_CONV + 2:
                    pe.wait_ge(mv_ready, 4)
                mem_step(0, n)
                last = [m for m in range(n) if bank_of(m) == bank_of(n)]
                if last:
                    pe.wait_ge(lin_read, last[-1] + 1)
                if N_MEMKV <= n < N_CONV:
                    if n == N_MEMKV:
                        strip(n, mem_hi, mem_lo, bank_of(n), cols=NMEM, ready=(mem_lo_ready, 0))
                    else:
                        strip(n, mem_hi, mem_lo, bank_of(n), cols=NMEM)
                else:
                    strip(n, a_hi, a_lo, bank_of(n), ready=(a_lo_ready, 0) if n == 0 else None)

            def out_phase(n0):
                for m in range(KT):
                    n = n0 + m
                    pe.wait_ge(lin_read, out_index(n) - (1 if m else 0))
                    strip(n, y_hi, y_lo, n % 2)

            def ffn(n0, v, q0, count):
                def body(i, first=False):
                    for j in range(4):
                        n = i * 4 + (n0 + j)
                        if first and j == 1:
                            sums(v)
                        if first and j == 2:
                            spread(v)
                        if not first:
                            pe.wait_ge(lin_read, i * 4 + (q0 + j - 3))
                        strip(n, a_hi, a_lo, j, slot=j % 2,
                              ready=(a_lo_ready, count) if first and j == 0 else None)
                body(0, first=True)
                with pe.Fori(1, FT // 2, 1) as i:
                    body(i)

            def down(layer, n0, q0):
                with pe.Fori(0, KT // 2, 1) as i:
                    for j in range(2):
                        n = i * 4 + (n0 + 2 * j)
                        pe.wait_ge(lin_read, i * 2 + (q0 + j - 1))
                        pe.wait_ge(g_lo_ready, FT * layer + HALF)
                        strip(n, g_hi, g_lo, j, kt=HALF, slot=0, stop=False)
                        pe.wait_ge(g_lo_ready, FT * (layer + 1))
                        strip(n + 1, g_hi, g_lo, j, kt=HALF, k0=HALF, slot=1, start=False)

            pe.wait_ge(yc_lo_ready, CT)
            pe.wait_ge(ym_lo_ready, 2)
            out_phase(N_OUT0)
            ffn(N_FFN0, V_FFN0, out_index(N_FFN0), KT)
            down(0, N_DOWN0, out_index(N_DOWN0))

            def sw_scores_of(u):
                hp, b, s, keys, k0 = sw_unit(u)
                r = HD * s
                if u >= 2:
                    pe.wait_ge(sw_biased, u - 1)
                for g in range(GROUP):
                    ins = pe.matmul(ps[:, 2 + 2 * (u % 2) + g // 2, g % 2 * 256:g % 2 * 256 + keys],
                                    qT[r:r + HD, GROUP * hp + g, b * P:(b + 1) * P],
                                    kT[r:r + HD, hp, k0:k0 + keys], start=True, stop=True)
                ins.then_inc(sw_scores, 1)

            def sw_turn(u):
                hp, b, s, keys, k0 = sw_unit(u)
                pe.wait_ge(sw_probs, u + 1)
                for c in range(keys // P):
                    for g in range(GROUP):
                        ins = pe.transpose(ps[:, 6 + c, g * P:(g + 1) * P],
                                           p_sw[:, u % 2, g, c * P:(c + 1) * P], ident[:])
                        if g == GROUP - 1 or (keys == P and g == GROUP - 2):
                            ins.then_inc(sw_turned, 1)

            def sw_values(u):
                hp, b, s, keys, k0 = sw_unit(u)
                r, h = HD * s, 2 * hp + s
                pe.wait_ge(sw_pT0, u + 1)
                if keys > P:
                    pe.wait_ge(sw_pT1, sum(sw_unit(w)[3] > P for w in range(u + 1)))
                if s == 0 and u:
                    pe.wait_ge(ys_lo_ready, u // 2)
                for c in range(keys // P):
                    ins = pe.matmul(ps[r:r + HD, 1, 0:GROUP * P],
                                    vn[:, k0 // P + c, h * HD:(h + 1) * HD], pT_sw[:, c, :],
                                    start=(c == 0), stop=(c == keys // P - 1))
                ins.then_inc(sw_pv, 1)

            def sw_step(u):
                if u < NSW:
                    sw_scores_of(u)
                if u:
                    sw_turn(u - 1)
                    sw_values(u - 1)

            for n in range(N_KV, N_OUT1):
                if n == N_KV + 1:
                    sums(V_MIX1)
                if n == N_KV + 2:
                    spread(V_MIX1)
                if n in (N_KV + 3, N_KV + 4):
                    pe.wait_ge(band_in, 16 * 2)
                    for c in range(3 * (n - N_KV - 3), 3 * (n - N_KV - 3) + 3):
                        if c >= 3:
                            pe.wait_ge(bias_ready, c - 2)
                        pe.matmul(ps[:, 4 + c % 3, :], flip[:], band[:, c * S:(c + 1) * S],
                                  start=True, stop=True).then_inc(flip_mm, 1)
                if n in (N_KV + 4, N_KV + 5):
                    t = n - N_KV - 4
                    pe.wait_ge(lin_read, out_index(N_KV + 2 + t) + 1)
                    pe.wait_ge(vn_ready, t) if t else pe.wait_ge(rstd_ready, V_MIX1 + 1)
                    for b in range(TB):
                        ins = pe.transpose(ps[:, 7, b * P:(b + 1) * P], vT[:, b * P:(b + 1) * P], ident[:])
                    ins.then_inc(v_turned, 1)
                if n == N_Q:
                    pe.wait_ge(lin_read, out_index(N_Q))
                if n == N_Q + 1:
                    pe.wait_ge(vn_ready, 2)
                    pe.wait_ge(bias_ready, 6)
                mem_step(1, n)
                if n == SW_FIRST:
                    pe.wait_ge(ym_lo_ready, 4)
                if n >= SW_FIRST:
                    sw_step(n - SW_FIRST)
                last = [m for m in range(N_KV, n) if bank_of(m) == bank_of(n)]
                if last:
                    pe.wait_ge(lin_read, out_index(last[-1]) + 1)
                kv = n < N_QM1
                strip(n, kv_hi if kv else a_hi, kv_lo if kv else a_lo, bank_of(n),
                      ready=(kv_lo_ready, 0) if n == N_KV else None)
            for u in range(N_OUT1 - SW_FIRST, NSW + 1):
                sw_step(u)
            pe.wait_ge(ys_lo_ready, NSW // 2)
            out_phase(N_OUT1)
            ffn(N_FFN1, V_FFN1, out_index(N_FFN1), 3 * KT)
            down(1, N_DOWN1, out_index(N_DOWN1))

            def exchange(n):
                i = turned_before(n)[0]
                pe.wait_ge(lin_read, out_index(n) + 1)
                pe.matmul(ps[:, turn_bank(n), :], perm[:, ROPE[n][0], :], strip_of(n), start=True, stop=True)\
                    .then_inc(rope_mm, 1)

            def turn(n):
                pe.wait_ge(lin_read, out_index(n) + 1)
                for b in range(TB):
                    ins = pe.transpose(ps[:, turn_bank(n), b * P:(b + 1) * P],
                                       strip_of(n)[:, b * P:(b + 1) * P], ident[:])
                ins.then_inc(turn_mm, 1)

            def bank_read(n):
                if n in ROPE:
                    pe.wait_ge(rope_ready, read_of(n)[0])
                else:
                    pe.wait_ge(turn_ready, read_of(n)[1])

            def hidden(i):
                pe.wait_ge((w1k_in, w1v_in)[i], 16 * 2)
                pe.wait_ge(bd_ready, 4 * i + 4)
                bank = (4, 1)[i]
                for m in range(2):
                    for l in range(CLEN):
                        ins = pe.matmul(ps[:, bank, m * 2 * NCMP:(m + 1) * 2 * NCMP],
                                        w1[:, l, m * P:(m + 1) * P], bd[i][:, l, :],
                                        start=(l == 0), stop=(l == CLEN - 1))
                ins.then_inc(cmp_hidden, 1)

            def compressed(i):
                pe.wait_ge(cmp_gelu, i + 1)
                for g in range(2):
                    for m in range(2):
                        inner = hid[:, m, g * NCMP:(g + 1) * NCMP]
                        if i == 0:
                            o = ps[HD * g:HD * g + HD, 4, P:P + NCMP]
                            ins = pe.matmul(o, w2[:, 0, m, :], inner, start=(m == 0), stop=(m == 1))
                        else:
                            o = ps[0:NCMP, 1, P + g * HD:P + (g + 1) * HD]
                            ins = pe.matmul(o, inner, w2[:, 1, m, :], start=(m == 0), stop=(m == 1))
                ins.then_inc(cmp_mm, 1)

            def cmp_scores(g):
                if g == 0:
                    pe.wait_ge(cmp_ready, 1)
                else:
                    pe.wait_ge(cm_step, 3)
                pe.matmul(ps[:, 7, 0:16 * NCMP], ident_b, mask_c, start=True, stop=False)
                for k in range(16):
                    b, j = k // GH, k % GH
                    ins = pe.matmul(ps[:, 7, k * NCMP:(k + 1) * NCMP],
                                    qn[HD * g:HD * g + HD, j, b * P:(b + 1) * P], kc[HD * g:HD * g + HD, :],
                                    start=False, stop=(k == 15))
                ins.then_inc(cm_scores, 1)

            def ns_scores_of(u):
                b, g, br, keys = ns_unit(u)
                r = slice(HD * g, HD * g + HD)
                if u:
                    pe.wait_ge(ns_exp, GH * u)
                for j in range(GH):
                    pe.matmul(ps[:, 2 + j, 0:keys], qn[r, j, b * P:(b + 1) * P], (ks, kw)[br][r, 0:keys],
                              start=True, stop=False)
                    ins = pe.matmul(ps[:, 2 + j, b * P:keys], ident_b, causal, start=False, stop=True)
                ins.then_inc(ns_scores, 1)

            def ns_turn(u):
                b, g, br, keys = ns_unit(u)
                pe.wait_ge(ns_probs, u + 1)
                for j in range(GH):
                    if j >= 2:
                        pe.wait_ge((ns_pTd, ns_pTa)[j % 2], 2 * u + 1)
                    for c in range(b + 1):
                        ins = pe.transpose(ps[:, 6 + j % 2, c * P:(c + 1) * P],
                                           p_n[:, u % 2, j, c * P:(c + 1) * P], ident[:])
                    ins.then_inc(ns_turned, 1)
                if br:
                    pe.wait_ge(ns_pTd, 2 * u + 2)
                    pe.wait_ge(cm_probs, 5 * (g + 1))
                    for j in range(GH):
                        ins = pe.transpose(ps[0:NCMP, 6, j * P:(j + 1) * P], p_c[:, g, b * GH + j, :], ident[:])
                    ins.then_inc(cm_turned, 1)

            def ns_values(u):
                b, g, br, keys = ns_unit(u)
                pe.wait_ge(ns_pTd, 2 * u + 2)
                pe.wait_ge(ns_pTa, 2 * u + 2)
                if g == 0 and br == 0:
                    pe.wait_ge(oa_ready, b) if b else pe.wait_ge(cmp_ready, 2)
                o = ps[HD * g:HD * g + HD, 1, :]
                for c in range(b + 1):
                    ins = pe.matmul(o, (vs, vw)[br][:, c, g * HD:(g + 1) * HD], pT_n[:, c, :],
                                    start=(br == 0 and c == 0), stop=False)
                if br:
                    pe.wait_ge(cm_pT, u // 2 + 1)
                    ins = pe.matmul(o, vc[:, g, :], pT_c[:], start=False, stop=True)
                ins.then_inc(ns_pv, 1)

            def ret_scores(h):
                if h:
                    pe.wait_ge(rt_att, TB * h)
                for jc, (bank, c) in enumerate(((2, 0), (3, 0), (4, 0), (3, 3 * P))):
                    ins = pe.matmul(ps[:, bank, c:c + S - jc * P], kr[:, h, jc * P:(jc + 1) * P],
                                    qr[:, h, jc * P:S], start=True, stop=True)
                ins.then_inc(rt_scores, 1)

            def ret_values(h):
                pe.wait_ge(rt_att, TB * h + TB)
                if h:
                    pe.wait_ge(rt_norm, TB * h)
                for ic in range(TB):
                    for jc in range(ic + 1):
                        ins = pe.matmul(ps[:, (1, 5)[ic // 2], ic % 2 * RDV:(ic % 2 + 1) * RDV],
                                        att[:, jc, (ic - jc) * P:(ic - jc + 1) * P],
                                        vr[:, jc, h * RDV:(h + 1) * RDV], start=(jc == 0), stop=(jc == ic))
                ins.then_inc(rt_out, 1)

            def ret_turn(h):
                pe.wait_ge(rt_norm, TB * h + TB)
                if h:
                    pe.wait_ge(rt_ob0, h)
                    pe.wait_ge(rt_ob1, h)
                for f in range(2):
                    for ic in range(TB):
                        ins = pe.transpose(ps[:, 6 + f, ic * P:(ic + 1) * P], on[:, ic, f * P:(f + 1) * P],
                                           ident[:])
                    ins.then_inc(rt_turned, 1)

            for n in range(N_SECOND, N_END):
                if n == N_SECOND + 1:
                    sums(V_LAST)
                    pe.wait_ge(acc2_ready, 1 + KT)
                    for c in range(TB):
                        ins = pe.matmul(ps[:, stat_bank, TB + c:TB + c + 1], acc2[:, c * P:(c + 1) * P],
                                        ones[:, 0:1], start=True, stop=True)
                    ins.then_inc(norm_sum, 1)
                if n == N_SECOND + 3:
                    spread(V_LAST)
                if n == N_SECOND + 4:
                    pe.wait_ge(rstd_ready, V_LAST + 1)
                    spread(V_PRE)
                    pe.wait_ge(small2_in, 16 * 6)
                for m in handled(n):
                    if turned_before(m) != (0, 0):
                        order = [k for t in range(N_SECOND, N_END) for k in handled(t)]
                        same = [k for k in order[:order.index(m)] if turn_bank(k) == turn_bank(m)]
                        if same:
                            bank_read(same[-1])
                    (exchange if m in ROPE else turn)(m)
                if n == N_SECOND + 6:
                    hidden(0)
                if n == N_SECOND + 7:
                    compressed(0)
                if n == N_RET:
                    pe.wait_ge(lin_read, out_index(N_GATE) + 1)
                    hidden(1)
                if n == N_RET + 1:
                    compressed(1)
                    pe.wait_ge(gate_sig, 1)
                    bank_read(N_SECOND + 9)
                    for b in range(TB):
                        ins = pe.transpose(ps[:, 6, 24 * b:24 * b + 24], tmp[0:24, 2, b * P:(b + 1) * P],
                                           ident[0:24, 0:24])
                    ins.then_inc(gate_mm, 1)
                if n == N_RET + 1:
                    pe.wait_ge(gate_ready, 1)
                if n == N_RET:
                    bank_read(N_SECOND + 8)
                    bank_read(N_SECOND + 9)
                if NS_FIRST <= n < NS_FIRST + NS:
                    ns_scores_of(n - NS_FIRST)
                if NS_FIRST <= n < NS_FIRST + 2:
                    cmp_scores(n - NS_FIRST)
                if NS_FIRST < n <= NS_FIRST + NS:
                    if n == NS_FIRST + 1:
                        pe.wait_ge(cm_step, 6)
                    for m in handled(n):
                        bank_read(m)
                    ns_turn(n - 1 - NS_FIRST)
                    ns_values(n - 1 - NS_FIRST)
                if n == RT_FIRST:
                    pe.wait_ge(ns_exp, GH * NS)
                    pe.wait_ge(oa_ready, TB)
                    bank_read(N_ZN - 1)
                if RT_FIRST + 2 <= n < RT_FIRST + 2 + RH:
                    ret_turn(n - RT_FIRST - 2)
                if RT_FIRST + 1 <= n < RT_FIRST + 1 + RH:
                    ret_values(n - RT_FIRST - 1)
                if RT_FIRST <= n < RT_FIRST + RH:
                    ret_scores(n - RT_FIRST)
                last = [m for m in range(N_SECOND, n) if bank_of(m) == bank_of(n)]
                if n >= N_FIN + 2:
                    pe.wait_ge(fin_read, n - N_FIN - 1)
                elif last:
                    pe.wait_ge(lin_read, out_index(last[-1]) + 1)
                if n == N_MA + 1:
                    pe.wait_ge(zl_ready, GH)
                if n == N_MB + 1:
                    pe.wait_ge(zl_ready, GH + KT)
                if n == N_FIN:
                    strip(n, mg_hi, mg_lo, bank_of(n), ready=(zl_ready, GH + KT))
                elif n > N_FIN:
                    strip(n, mg_hi, mg_lo, bank_of(n))
                elif N_MA <= n < N_ZR and (n - N_MA) % 2:
                    strip(n, ya_hi, ya_lo, bank_of(n), kt=GH)
                elif n >= N_MB and (n - N_MB) % 2:
                    strip(n, yb_hi, yb_lo, bank_of(n))
                else:
                    strip(n, a_hi, a_lo, bank_of(n), ready=(a_lo_ready, 4 * KT) if n == N_SECOND else None,
                          rows=24 if n == N_GATE else P)
            sums(V_POST - 1)
            spread(V_POST)


def strips(w):
    k, n = w.shape
    return w.reshape(k // P, P, n // P, P).transpose(2, 1, 0, 3).reshape(n // P, P, -1)


LOW = [0, 1, 2, 6, 7, 8]
HIGH = [3, 4, 5, 9, 10, 11]


def head_order():
    return np.concatenate([np.arange(h * HD, (h + 1) * HD) for p in zip(LOW, HIGH) for h in p])


def relative_onehot():
    exact, count, far = 16, 32, 128
    dist = np.arange(2 * P - 1, 2 * P - 1 - NREL, -1)
    d = np.maximum(dist, 1).astype(np.float32)
    large = exact + (np.log(d / np.float32(exact)) / np.float32(math.log(far / exact))
                     * np.float32(count - exact)).astype(np.int32)
    bucket = np.where(np.maximum(dist, 0) < exact, np.maximum(dist, 0), np.minimum(large, count - 1))
    out = np.zeros((33, NREL), np.float32)
    inside = (dist >= 0) & (dist < P)
    out[bucket[inside], np.nonzero(inside)[0]] = 1.0
    out[32, ~inside] = 1.0
    return out


def exchanges():
    out = np.zeros((P, 2, P), np.float32)
    for d in range(P):
        if d % HD < 16:
            out[d ^ 8, 0, d] = 1.0
        out[d ^ 64, 1, d] = 1.0
    return out


def rotary_tables():
    pos = np.arange(S, dtype=np.float32)
    out = np.zeros((2, P, 2, S), np.float32)
    inv_n = np.float32(1.0) / (np.float32(500000.0) ** (np.arange(0, 16, 2, dtype=np.float32) / np.float32(16)))
    inv_r = np.float32(1.0) / (np.float32(10000.0) ** np.linspace(0.0, 1.0, 64, dtype=np.float32))
    out[0, :, 0, :] = 1.0
    for d in range(P):
        if d % HD < 16:
            ang = (pos * inv_n[d % 8]).astype(np.float32)
            out[0, d, 0], out[0, d, 1] = np.cos(ang), np.sin(ang) * (-1 if d % HD < 8 else 1)
        ang = (pos * inv_r[d % 64]).astype(np.float32)
        out[1, d, 0], out[1, d, 1] = np.cos(ang), np.sin(ang) * (-1 if d < 64 else 1)
    return out


def mask_table():
    q, k = np.arange(P)[:, None], np.arange(P)[None, :]
    causal = np.where(k <= q, 0.0, MASKED)
    t = np.arange(TB)[None, :, None, None] * P + np.arange(P)[:, None, None, None]
    end = np.arange(NCMP)[None, None, None, :] * CSTRIDE + CLEN - 1
    cmp = np.where(end <= t, 0.0, MASKED) + np.zeros((P, TB, GH, NCMP))
    return np.concatenate([np.eye(P), causal, cmp.reshape(P, -1)], 1).astype(mybir.dt.np(BF16))


def decays():
    log_g = np.log(np.float32(1.0) - np.float32(2.0) ** (np.float32(-5.0) - np.arange(RH, dtype=np.float32)))
    diff = (np.arange(S)[None, :] - np.arange(P)[:, None]).astype(np.float32)
    out = np.exp(np.maximum(diff, 0)[:, None, :] * log_g[None, :, None]) * (diff >= 0)[:, None, :]
    return out.astype(np.float32)


def feature_major(v):
    return v.T.reshape(v.shape[1] // P, P, -1).transpose(1, 0, 2)


def kernel(**inputs):
    from concourse import bacc
    from concourse.bass_utils import run_bass_kernel_spmd

    w = {k: np.asarray(v) for k, v in inputs.items()}
    nc = bacc.Bacc("TRN2", target_bir_lowering=False, num_devices=1)
    order = head_order()
    a_in = strips(w["a_w_in"][0])
    triple = [a_in[[i, 12 + i, 6 + i]] for i in range(CT)]
    mkv = [strips(w["w_mem_kv"][i]) for i in range(2)]
    b_in = strips(w["b_w_q"][0][:, np.concatenate([order, np.arange(768, 1024)])])
    b_out = strips(w["b_w_out"][0][np.concatenate([order, np.arange(768, 1024)])])

    def pairs(i):
        return np.stack([strips(w["w_gate"][i]), strips(w["w_up"][i])], 1).reshape(2 * FT, P, D)

    w2_in = w["w_in_2"]
    cuts = np.cumsum([512, 128, 128, 128, 128, 128, 128, 24, 512, 512, 512, 1024, 1024, 1024, 1024])[:-1]
    q_n, k_c, v_c, k_s, v_s, k_w, v_w, g_n, z_n, q_r, k_r, v_r, z_r, m_a, m_b = np.split(w2_in, cuts, axis=1)
    pairs_n = np.concatenate([np.arange(h * HD, (h + 1) * HD) for t in range(GH) for h in (t, GH + t)])
    q_r, k_r, v_r = strips(q_r), strips(k_r), strips(v_r)
    ret = np.concatenate([np.stack([q_r[h], k_r[h], v_r[2 * h], v_r[2 * h + 1]]) for h in range(RH)])
    mb_ret = np.stack([strips(m_b), strips(w["w_ret_o_2"])], 1).reshape(2 * KT, P, D)

    def cmp_first(v):
        return v.reshape(CLEN, HD, 256).transpose(1, 0, 2)

    arrays = {
        "w8b": np.concatenate([strips(k_c), strips(v_c), strips(v_s), strips(v_w), strips(q_n[:, pairs_n]),
                               strips(k_s), strips(k_w), ret, strips(z_n[:, pairs_n]), strips(m_a),
                               strips(z_r), mb_ret, strips(w["w_out_2"])]),
        "w_gates": g_n.reshape(KT, P, 24).transpose(1, 0, 2).reshape(P, KT * 24),
        "w_nsa_o": strips(w["w_nsa_o_2"][pairs_n]),
        "cmp_w1": np.stack([cmp_first(w["cmp_w1_k_2"]), cmp_first(w["cmp_w1_v_2"])]),
        "cmp_w2": np.stack([w["cmp_w2_k_2"].reshape(2, P, HD), w["cmp_w2_v_2"].reshape(2, P, HD)])
                    .transpose(2, 0, 1, 3),
        "cmp_pe": np.stack([w["cmp_pe_k_2"].T, w["cmp_pe_v_2"].T], 1),
        "gate_b": w["b_nsa_gate_2"].reshape(24, 1),
        "perm": exchanges(),
        "masks": mask_table(),
        "rope": rotary_tables(),
        "decay": decays(),
        "w8": np.concatenate([a_in[18:20], triple[0], mkv[0][:2], mkv[1][:2], mkv[0][2:], mkv[1][2:],
                              *triple[1:], strips(w["a_w_out"][0]), pairs(0), strips(w["w_kv"]),
                              b_in[6:8], b_in[:6], b_out, pairs(1)]),
        "w_down": np.concatenate([strips(w["w_down"][i]).reshape(KT, P, 2, SLOT).transpose(0, 2, 1, 3)
                                  .reshape(2 * KT, P, SLOT) for i in range(2)]),
        "xT": feature_major(w["x"][0]),
        "memT": feature_major(w["mem"][0]),
        "gains": np.stack([g.reshape(KT, P).T for g in (
            w["mem_norm"], w["norm_mix"][0], w["norm_ffn"][0], w["kv_norm"], w["norm_mix"][1],
            w["norm_ffn"][1], w["final_norm"], w["norm_pre_2"], w["norm_post_2"])], 1),
        "conv_w": w["a_conv_w"][0].reshape(3, CT, P).transpose(2, 1, 0),
        "sinks": w["b_sinks"][0],
        "rel_bias": w["rel_bias"],
        "onehot": relative_onehot(),
        "masked": np.full((1, 12), MASKED, np.float32),
        "ident": np.eye(P, dtype=np.float32),
        "flip": np.eye(P, dtype=np.float32)[::-1],
    }
    arrays = {k: np.ascontiguousarray(v) for k, v in arrays.items()}
    aps = {k: nc.dram_tensor(k, v.shape, mybir.dt.from_np(v.dtype), kind="ExternalInput").ap()
           for k, v in arrays.items()}
    out = nc.dram_tensor("out", (P, KT, S), F32, kind="ExternalOutput").ap()
    build(nc, aps, out)
    r = run_bass_kernel_spmd(nc, [arrays], core_ids=[0])
    y = r.results[0]["out"]
    return np.ascontiguousarray(y.transpose(2, 1, 0).reshape(1, S, D))
```

```python
import math

import concourse.bass as bass
import numpy as np
from concourse import mybir

F32 = mybir.dt.float32
R32 = mybir.dt.float32r
BF16 = mybir.dt.bfloat16
ACT = mybir.ActivationFunctionType
ALU = mybir.AluOpType
AX = mybir.AxisListType

P = 128
S = 512
D = 1024
KT = D // P
NMEM = 256
HD = 64
FF = 2816
FT = FF // P
HALF = FT // 2
TB = S // P
CT = 6
RAW = 4
SLOT = HALF * P
SCALE = HD ** -0.5
EPS_A = 1e-5
EPS_B = 1e-6
MASKED = -1.0e30
GROUP = 3
NREL = 383
(G_MEM, G_MIX0, G_FFN0, G_KV, G_MIX1, G_FFN1, G_FINAL, G_PRE, G_POST) = range(9)

N_QM0 = 0
N_CONV0 = 2
N_MEMKV = 5
N_CONV = 13
N_OUT0 = 28
N_FFN0 = 36
N_DOWN0 = 80
N_KV = 96
N_QM1 = 100
N_Q = 102
N_OUT1 = 108
N_FFN1 = 116
N_DOWN1 = 160
N_SECOND = 176
N_GATE = 186
N_RET = 187
N_ZN = 203
N_MA = 207
N_ZR = 223
N_MB = 231
N_FIN = 247
N_END = 255

V_MIX0, V_MEM, V_FFN0, V_MIX1, V_FFN1, V_LAST, V_PRE, V_POST = range(8)
SQUARES = 9


NCMP = 31
CLEN = 32
CSTRIDE = 16
GH = 4
RH = 4
RDV = 256
EMPTY = -1.0e29
TINY = float(np.finfo(np.float32).tiny)


def out_index(n):
    return n if n <= N_DOWN0 else n - 8 if n <= N_DOWN1 else n - 16


def build(nc, a, out):
    base = (nc.sbuf_base + 31) // 32 * 32
    top = [base]

    def at(name, shape, dtype, offset):
        return nc.alloc_sbuf_tensor_at(name, shape, dtype, offset=offset)

    def sb(name, shape, dtype=F32):
        size = int(np.prod(shape[1:])) * (2 if dtype == BF16 else 4)
        t = at(name, shape, dtype, top[0])
        top[0] += (size + 31) // 32 * 32
        return t

    x = sb("x", [P, KT, S])
    a_hi = sb("a_hi", [P, KT, S], R32)
    a_lo = sb("a_lo", [P, KT, S], R32)
    raw = sb("raw", [P, RAW, SLOT])
    w_hi = sb("w_hi", [P, 2, SLOT], R32)
    w_lo = sb("w_lo", [P, 2, SLOT], R32)
    tmp_at = top[0]
    tmp = sb("tmp", [P, 4, S])
    rstd = sb("rstd", [P, S])
    diag = sb("diag", [P, TB, P])
    acc = sb("acc", [P, S])
    mk1_at = top[0]
    mk1 = sb("mk1", [P, 2, NMEM])
    mv1 = sb("mv1", [P, 2, NMEM])
    ident = sb("ident", [P, P])
    ones = sb("ones", [P, P])
    gains = sb("gains", [P, 9, KT])
    conv_w = sb("conv_w", [P, CT, 3])
    sinks = sb("sinks", [P, 12])
    half = sb("half", [P, TB])
    acc2 = sb("acc2", [P, S])
    perm = sb("perm", [P, 2, P])
    w2 = sb("w2", [P, 2, 2, HD])
    pe2 = sb("pe2", [P, 2, CLEN // 2])
    masks = sb("masks", [P, 2 * P + TB * GH * NCMP], BF16)
    gate_n = sb("gate_n", [P, TB, 24])
    hid = sb("hid", [P, 2, 2 * NCMP])
    kc = sb("kc", [P, NCMP])
    vc = sb("vc", [NCMP, 2, HD])
    gate_b = sb("gate_b", [24, 1])
    rs2 = sb("rs2", [P, TB])
    rs3 = sb("rs3", [P, TB])
    nm16 = sb("nm16", [P, 16])
    d16 = sb("d16", [P, 16])
    bn6 = sb("bn6", [P, TB, 6])
    bn2 = sb("bn2", [P, 2, TB, 2])
    var = sb("var", [P, TB])
    rs = sb("rs", [P, TB])
    nmx = sb("nmx", [P, 2, TB])
    den = sb("den", [P, 2, TB])
    sq = at("sq", [P, 2, S], F32, tmp_at)
    sq2 = at("sq2", [P, 2, S], F32, tmp_at + 4096)
    g0 = top[0]
    K1 = 1024

    g_hi = at("g_hi", [P, FT, S], R32, g0)
    g_lo = at("g_lo", [P, FT, S], R32, g0 + FT * 2 * K1)
    assert g0 + 2 * FT * 2 * K1 <= nc.sbuf_base + 212800, g0
    y_hi = at("y_hi", [P, KT, S], R32, g0)
    y_lo = at("y_lo", [P, KT, S], R32, g0 + 16 * K1)
    memx = at("memx", [P, KT, NMEM], F32, g0 + 32 * K1)
    mem_hi = at("mem_hi", [P, KT, NMEM], R32, g0 + 40 * K1)
    mem_lo = at("mem_lo", [P, KT, NMEM], R32, g0 + 48 * K1)
    u_s = at("u_s", [P, S], F32, g0 + 56 * K1)
    v_s = at("v_s", [P, S], F32, g0 + 58 * K1)
    y_s = at("y_s", [P, S], F32, g0 + 60 * K1)
    qm0 = at("qm0", [P, 2, S], F32, g0 + 62 * K1)
    pm0 = at("pm0", [P, 2, TB, NMEM], F32, g0 + 66 * K1)
    pmT0 = at("pmT0", [P, 2, S], F32, g0 + 74 * K1)
    mk0 = at("mk0", [P, 2, NMEM], F32, g0 + 78 * K1)
    mv0 = at("mv0", [P, 2, NMEM], F32, g0 + 80 * K1)
    mvt = at("mvt", [P, NMEM], F32, g0 + 82 * K1)
    rmem = at("rmem", [P, NMEM], F32, g0 + 83 * K1)
    table = at("table", [12, NREL], F32, g0 + 84 * K1)
    rb = at("rb", [33, 12], F32, g0 + 86 * K1)
    onehot = at("onehot", [33, NREL], F32, g0 + 86 * K1 + 256)
    kv_hi = at("kv_hi", [P, KT, S], R32, g0)
    kv_lo = at("kv_lo", [P, KT, S], R32, g0 + 16 * K1)
    kT = at("kT", [P, 2, S], F32, g0 + 32 * K1)
    vn = at("vn", [P, TB, NMEM], F32, g0 + 36 * K1)
    vT = at("vT", [P, S], F32, g0 + 40 * K1)
    qT = at("qT", [P, CT, S], F32, g0 + 42 * K1)
    band = at("band", [P, 12 * 256], F32, g0 + 42 * K1)
    qm1 = at("qm1", [P, 2, S], F32, g0 + 54 * K1)
    pm1 = at("pm1", [P, 2, TB, NMEM], F32, g0 + 58 * K1)
    pmT1 = at("pmT1", [P, 2, S], F32, g0 + 66 * K1)
    s_sw = at("s_sw", [P, 2, GROUP, 257], F32, g0 + 58 * K1)
    p_sw = at("p_sw", [P, 2, GROUP, 257], F32, g0 + 64 * K1 + 256)
    pT_sw = at("pT_sw", [P, 2, GROUP * P], F32, g0 + 70 * K1 + 512)
    bias = at("bias", [P, 12, 256], F32, g0 + 73 * K1 + 512)
    flip = at("flip", [P, P], F32, g0 + 85 * K1 + 512)

    t2 = at("t2", [P, 2, S], F32, mk1_at)
    pT_n = at("pT_n", [P, TB, GH * P], F32, tmp_at)
    qn = at("qn", [P, GH, S], F32, g0)
    ks = at("ks", [P, S], F32, g0 + 8 * K1)
    kw = at("kw", [P, S], F32, g0 + 10 * K1)
    windows = [at(f"windows{i}", [P, CLEN // 2, 2 * NCMP], F32, g0 + (12 + 8 * i) * K1) for i in range(2)]
    p_n = at("p_n", [P, 2, GH, S], F32, g0 + 12 * K1)
    rope_n = at("rope_n", [P, 2, S], F32, g0 + 28 * K1)
    vs = at("vs", [P, TB, P], F32, g0 + 32 * K1)
    vw = at("vw", [P, TB, P], F32, g0 + 34 * K1)
    rope_r = at("rope_r", [P, 2, S], F32, g0 + 36 * K1)
    kcr = at("kcr", [P, S], F32, g0 + 40 * K1)
    vcr = at("vcr", [P, S], F32, g0 + 42 * K1)
    oa = at("oa", [P, GH, S], F32, g0 + 40 * K1)
    p_c = at("p_c", [P, 2, 16, NCMP], F32, g0 + 48 * K1)
    pT_c = at("pT_c", [NCMP, GH * P], F32, g0 + 52 * K1)
    r1 = at("r1", [P, S], F32, g0 + 54 * K1)
    w1 = at("w1", [P, 2, CLEN // 2, 256], F32, g0 + 56 * K1)
    qr = at("qr", [P, RH, S], F32, g0 + 56 * K1)
    kr = at("kr", [P, RH, S], F32, g0 + 64 * K1)
    vr = at("vr", [P, TB, RH * RDV], F32, g0 + 72 * K1)
    ya_hi = at("ya_hi", [P, GH, S], R32, g0)
    ya_lo = at("ya_lo", [P, GH, S], R32, g0 + 8 * K1)
    decay = at("decay", [P, RH, S], F32, g0 + 16 * K1)
    att = at("att", [P, TB, S], F32, g0 + 24 * K1)
    on = at("on", [P, TB, RDV], F32, g0 + 32 * K1)
    ob = [at("ob0", [P, 4, S], F32, g0 + 48 * K1), at("ob1", [P, 4, S], F32, g0 + 40 * K1)]
    merged = at("merged", [P, KT, S], F32, g0 + 16 * K1)
    yb_hi = at("yb_hi", [P, KT, S], R32, g0 + 56 * K1)
    yb_lo = at("yb_lo", [P, KT, S], R32, g0 + 72 * K1)
    mg_hi = at("mg_hi", [P, KT, S], R32, g0)
    mg_lo = at("mg_lo", [P, KT, S], R32, g0 + 32 * K1)
    yg = at("yg", [P, KT, S], F32, g0 + 16 * K1)
    ident_b = masks[:, 0:P]
    causal = masks[:, P:2 * P]
    mask_c = masks[:, 2 * P:]

    ps = nc.alloc_psum_tensor("ps", [P, 8, S], F32)

    def sem(name):
        return nc.alloc_semaphore(name)

    raw_in = [sem(f"raw_in{i}") for i in range(RAW)]
    x_in = [sem(f"x_in{i}") for i in range(4)]
    mem_in = sem("mem_in")
    gains_in = sem("gains_in")
    const_in = sem("const_in")
    first_in = sem("first_in")
    first_hi = sem("first_hi")
    first_lo = sem("first_lo")
    small_in = sem("small_in")
    w_hi_ready = sem("w_hi_ready")
    w_lo_ready = sem("w_lo_ready")
    blk_done = sem("blk_done")
    lin_read = sem("lin_read")
    ones_ready = sem("ones_ready")
    half_ready = sem("half_ready")
    sq_ready = sem("sq_ready")
    acc_ready = sem("acc_ready")
    norm_sum = sem("norm_sum")
    norm_var = sem("norm_var")
    norm_pow = sem("norm_pow")
    norm_diag = sem("norm_diag")
    norm_spread = sem("norm_spread")
    rstd_ready = sem("rstd_ready")
    a_hi_ready = sem("a_hi_ready")
    a_lo_ready = sem("a_lo_ready")
    mem_hi_ready = sem("mem_hi_ready")
    mem_lo_ready = sem("mem_lo_ready")
    conv_step = sem("conv_step")
    yc_hi_ready = sem("yc_hi_ready")
    yc_lo_ready = sem("yc_lo_ready")
    mv_turned = sem("mv_turned")
    mv_ready = sem("mv_ready")
    mem_scores = sem("mem_scores")
    mem_max = sem("mem_max")
    mem_exp = sem("mem_exp")
    mem_rden = sem("mem_rden")
    mem_probs = sem("mem_probs")
    mem_turned = sem("mem_turned")
    mem_pT0 = sem("mem_pT0")
    mem_pT1 = sem("mem_pT1")
    mem_pv = sem("mem_pv")
    ym_hi_ready = sem("ym_hi_ready")
    ym_lo_ready = sem("ym_lo_ready")
    silu_ready = sem("silu_ready")
    gu_ready = sem("gu_ready")
    g_hi_ready = sem("g_hi_ready")
    g_lo_ready = sem("g_lo_ready")
    table_mm = sem("table_mm")
    table_ready = sem("table_ready")
    table_out = sem("table_out")
    band_in = sem("band_in")
    flip_mm = sem("flip_mm")
    bias_ready = sem("bias_ready")
    kv_hi_ready = sem("kv_hi_ready")
    kv_lo_ready = sem("kv_lo_ready")
    v_turned = sem("v_turned")
    vn_ready = sem("vn_ready")
    sw_scores = sem("sw_scores")
    sw_biased = sem("sw_biased")
    sw_max = sem("sw_max")
    sw_sink = sem("sw_sink")
    sw_exp = sem("sw_exp")
    sw_den = sem("sw_den")
    sw_probs = sem("sw_probs")
    sw_turned = sem("sw_turned")
    sw_pT = sem("sw_pT")
    sw_pv = sem("sw_pv")
    ys_hi_ready = sem("ys_hi_ready")
    ys_lo_ready = sem("ys_lo_ready")
    out_done = sem("out_done")
    sq2_ready = sem("sq2_ready")
    acc2_ready = sem("acc2_ready")
    gain_ready = sem("gain_ready")
    pre_step = sem("pre_step")
    small2_in = sem("small2_in")
    rope_in = sem("rope_in")
    w1k_in = sem("w1k_in")
    w1v_in = sem("w1v_in")
    rope_mm = sem("rope_mm")
    rope_mul = sem("rope_mul")
    rope_ready = sem("rope_ready")
    turn_mm = sem("turn_mm")
    turn_ready = sem("turn_ready")
    swap_mm = sem("swap_mm")
    windows_ready = sem("windows_ready")
    cmp_hidden = sem("cmp_hidden")
    cmp_gelu = sem("cmp_gelu")
    cmp_mm = sem("cmp_mm")
    cmp_ready = sem("cmp_ready")
    x1_ready = sem("x1_ready")
    gate_sig = sem("gate_sig")
    gate_mm = sem("gate_mm")
    gate_ready = sem("gate_ready")
    cm_scores = sem("cm_scores")
    cm_step = sem("cm_step")
    cm_exp = sem("cm_exp")
    cm_probs = sem("cm_probs")
    cm_turned = sem("cm_turned")
    cm_pT = sem("cm_pT")
    ns_scores = sem("ns_scores")
    ns_max = sem("ns_max")
    ns_exp = sem("ns_exp")
    ns_den = sem("ns_den")
    ns_probs = sem("ns_probs")
    ns_turned = sem("ns_turned")
    ns_pTd = sem("ns_pTd")
    ns_pTa = sem("ns_pTa")
    ns_pv = sem("ns_pv")
    oa_ready = sem("oa_ready")
    decay_in = sem("decay_in")
    rt_scores = sem("rt_scores")
    rt_att = sem("rt_att")
    rt_out = sem("rt_out")
    rt_stats = sem("rt_stats")
    rt_var = sem("rt_var")
    rt_pow = sem("rt_pow")
    rt_norm = sem("rt_norm")
    rt_turned = sem("rt_turned")
    rt_ob0 = sem("rt_ob0")
    rt_ob1 = sem("rt_ob1")
    gated = sem("gated")
    prod_ready = sem("prod_ready")
    zh_ready = sem("zh_ready")
    zl_ready = sem("zl_ready")
    fin_read = sem("fin_read")
    fin_gain = sem("fin_gain")
    out_part = sem("out_part")

    scratch = nc.dram_tensor("rel_scratch", (12, NREL), F32, kind="Internal").ap()

    stat_bank = 7

    def sw_unit(u):
        hp, b, s = u // 8, u % 8 // 2, u % 2
        keys = 256 if b else P
        return hp, b, s, keys, (b - 1) * P if b else 0

    NSW = 16

    def sw_bank(u):
        return 1 - u // 2 % 2

    MEM_STEPS = {0: {N_CONV + 1: 0, N_CONV + 4: 1, N_CONV + 7: 2, N_CONV + 10: 3},
                 1: {N_Q: 0, N_Q + 1: 1, N_Q + 2: 2, N_Q + 3: 3}}
    SW_FIRST = N_Q + 4

    NS = 16
    NS_FIRST, RT_FIRST = N_RET, N_ZN + 2

    def ns_unit(u):
        return u // 4, u % 4 // 2, u % 2, (u // 4 + 1) * P

    def width(n):
        return 24 * KT if n == N_GATE else GH * P if N_MA <= n < N_ZR and (n - N_MA) % 2 else KT * P

    ROPE = {N_SECOND: (0, kcr[:]), **{N_SECOND + 4 + t: (0, qn[:, t, :]) for t in range(GH)},
            N_SECOND + 8: (0, ks[:]), N_SECOND + 9: (0, kw[:])}
    for _h in range(RH):
        ROPE[N_RET + 4 * _h] = (1, qr[:, _h, :])
        ROPE[N_RET + 4 * _h + 1] = (1, kr[:, _h, :])
    TURN = {N_SECOND + 2: vs[:], N_SECOND + 3: vw[:]}
    for _f in range(2 * RH):
        TURN[N_RET + 4 * (_f // 2) + 2 + _f % 2] = vr[:, :, _f * P:(_f + 1) * P]
    ROPES, TURNS = sorted(ROPE), sorted(TURN)

    def turn_step(n):
        return N_SECOND + 4 if n == N_SECOND else N_SECOND + 5 if n == N_SECOND + 2 else n + 2

    def handled(n):
        return [m for m in ROPES + TURNS if turn_step(m) == n]

    def turn_bank(n):
        return 7 if n >= N_RET else 5 + n % 2

    def strip_of(n):
        return tmp[:, n % 4, :] if n < N_RET else t2[:, n % 2, :]

    def turned_before(n):
        order = [m for t in range(N_SECOND, N_END) for m in handled(t)]
        i = order.index(n)
        return sum(m in ROPE for m in order[:i]), sum(m in TURN for m in order[:i])

    def read_of(n):
        r, t = turned_before(n)
        return r + (n in ROPE), t + (n in TURN)

    def gated_index(n):
        if n < N_MA:
            return n - N_ZN
        if n < N_ZR:
            return 4 + (n - N_MA) // 2
        return 12 + n - N_ZR if n < N_MB else 20 + (n - N_MB) // 2

    def bank_of(n):
        if n >= N_SECOND:
            if n < N_GATE:
                return n % 4
            return 0 if n < RT_FIRST + 6 else n % 2
        if n < N_CONV:
            return n % 6
        if n in (N_KV + 2, N_KV + 3):
            return n - N_KV
        return 0 if n == N_OUT1 - 1 else n % 2

    with nc.Block() as block:

        @block.sync
        def _(sp):
            def load(n, slot, src, w):
                sp.wait_ge(w_lo_ready, n - (RAW - 1))
                sp.dma_start(raw[:, slot, 0:w], src).then_inc(raw_in[slot], 16)

            mid = KT * P // 2
            sp.dma_start(raw[:, 0, 0:mid], a["w8"][0][:, 0:mid]).then_inc(first_in, 16)
            for j in (1, 3):
                sp.dma_start(x[:, 2 * j:2 * j + 2, :], a["xT"][:, 2 * j:2 * j + 2, :]).then_inc(x_in[j], 16)
                if j == 1:
                    sp.dma_start(raw[:, 0, mid:KT * P], a["w8"][0][:, mid:KT * P]).then_inc(raw_in[0], 16)
            for n in range(1, RAW):
                sp.dma_start(raw[:, n, 0:KT * P], a["w8"][n]).then_inc(raw_in[n], 16)
            sp.dma_start(ident[:], a["ident"]).then_inc(const_in, 16)
            sp.dma_start(conv_w[:], a["conv_w"]).then_inc(const_in, 16)
            sp.dma_start(memx[:], a["memT"]).then_inc(mem_in, 16)
            sp.dma_start(onehot[:], a["onehot"]).then_inc(small_in, 16)
            sp.dma_start(rb[0:32, :], a["rel_bias"]).then_inc(small_in, 16)
            sp.dma_start(rb[32:33, :], a["masked"]).then_inc(small_in, 16)
            sp.dma_start(sinks[:], a["sinks"].partition_broadcast(P)).then_inc(small_in, 16)
            for dst, src in ((perm, "perm"), (w2, "cmp_w2"), (masks, "masks"), (gate_b, "gate_b")):
                sp.dma_start(dst[:], a[src]).then_inc(small2_in, 16)
            sp.dma_start(pe2[:], a["cmp_pe"]).then_inc(small2_in, 16)
            with sp.Fori(1, N_DOWN0 // RAW, 1) as i:
                for j in range(RAW):
                    load(i * RAW + j, j, a["w8"][i * RAW + j], KT * P)
            with sp.Fori(0, 2 * KT // RAW, 1) as i:
                for j in range(RAW):
                    load(i * RAW + (N_DOWN0 + j), j, a["w_down"][i * RAW + j], SLOT)
            with sp.Fori(0, (N_DOWN1 - N_KV) // RAW, 1) as i:
                for j in range(RAW):
                    load(i * RAW + (N_KV + j), j, a["w8"][i * RAW + (N_DOWN0 + j)], KT * P)
            with sp.Fori(0, 2 * KT // RAW, 1) as i:
                for j in range(RAW):
                    load(i * RAW + (N_DOWN1 + j), j, a["w_down"][i * RAW + (2 * KT + j)], SLOT)
            def source(n):
                if n == N_GATE:
                    return a["w_gates"]
                if n < N_GATE:
                    return a["w8b"][n - N_SECOND]
                if n < N_MA:
                    return a["w8b"][n - N_SECOND - 1]
                if n < N_ZR:
                    i = (n - N_MA) // 2
                    return a["w_nsa_o"][i] if (n - N_MA) % 2 else a["w8b"][30 + i]
                return a["w8b"][38 + n - N_ZR]

            for n in range(N_SECOND, N_END):
                if n == N_SECOND + RAW:
                    sp.wait_ge(lin_read, out_index(N_SECOND))
                    sp.dma_start(w1[:, 0], a["cmp_w1"][0]).then_inc(w1k_in, 16)
                if n == N_SECOND + RAW + 2:
                    sp.dma_start(w1[:, 1], a["cmp_w1"][1]).then_inc(w1v_in, 16)
                load(n, n % RAW, source(n), width(n))
            for k in range(KT):
                sp.wait_ge(out_part, k + 1)
                sp.dma_start(out[:, k, :], x[:, k, :]).then_inc(out_done, 16)
            sp.wait_ge(out_done, 16 * KT)

        @block.gpsimd
        def _(pool):
            pool.memset(ones[:], 1.0).then_inc(ones_ready, 1)

            def clear(v):
                if v:
                    pool.wait_ge(norm_sum, v)
                pool.memset(acc[:], 0.0).then_inc(acc_ready, 1)
                pool.wait_ge(acc_ready, SQUARES * v + 1)

            def squares(v, cols=S):
                clear(v)
                for k in range(KT):
                    pool.wait_ge(sq_ready, KT * v + k + 1)
                    pool.wait_ge(acc_ready, SQUARES * v + 1 + k)
                    pool.tensor_tensor(acc[:, 0:cols], acc[:, 0:cols], sq[:, k % 2, 0:cols],
                                       ALU.add).then_inc(acc_ready, 1)

            def power(v, tiles=TB):
                pool.wait_ge(norm_var, v + 1)
                pool.wait_ge(half_ready, 1)
                pool.tensor_tensor(rs[:, 0:tiles], var[:, 0:tiles], half[:, 0:tiles], ALU.pow)\
                    .then_inc(norm_pow, 1)

            squares(V_MIX0)
            power(V_MIX0)
            squares(V_MEM, NMEM)
            power(V_MEM, 2)
            for v in (V_FFN0, V_MIX1):
                squares(v)
                power(v)
            pool.wait_ge(small_in, 16 * 4)
            pool.wait_ge(mem_turned, 16)
            for u in range(NSW):
                hp, b, s, _, _ = sw_unit(u)
                h = 2 * hp + s
                if u >= 2:
                    pool.wait_ge(sw_exp, GROUP * (u - 1))
                pool.tensor_copy(s_sw[:, u % 2, :, 0], sinks[:, GROUP * h:GROUP * h + GROUP])\
                    .then_inc(sw_sink, 1)
            squares(V_FFN1)
            power(V_FFN1)
            clear(V_LAST)
            pool.memset(acc2[:], 0.0).then_inc(acc2_ready, 1)
            for k in range(KT):
                pool.wait_ge(sq_ready, KT * V_LAST + k + 1)
                pool.wait_ge(acc_ready, SQUARES * V_LAST + 1 + k)
                pool.tensor_tensor(acc[:], acc[:], sq[:, k % 2, :], ALU.add).then_inc(acc_ready, 1)
                pool.wait_ge(sq2_ready, k + 1)
                pool.wait_ge(acc2_ready, k + 1)
                pool.tensor_tensor(acc2[:], acc2[:], sq2[:, k % 2, :], ALU.add).then_inc(acc2_ready, 1)
            power(V_LAST)
            pool.wait_ge(norm_var, V_PRE + 1)
            pool.tensor_tensor(rs2[:], var[:], half[:], ALU.pow).then_inc(norm_pow, 1)
            for h in range(RH):
                pool.wait_ge(rt_var, h + 1)
                pool.tensor_tensor(bn2[:, h % 2, :, 1], bn2[:, h % 2, :, 1], half[:], ALU.pow)\
                    .then_inc(rt_pow, 1)
            squares(V_POST - 1)
            power(V_POST)

        @block.scalar
        def _(act):
            act.dma_start(gains[:], a["gains"]).then_inc(gains_in, 16)
            for j in (0, 2):
                act.dma_start(x[:, 2 * j:2 * j + 2, :], a["xT"][:, 2 * j:2 * j + 2, :])\
                    .then_inc(x_in[j], 16)

            def split(n, w, slot=None, raw_slot=None, count=None):
                slot = n % 2 if slot is None else slot
                raw_slot = n % RAW if raw_slot is None else raw_slot
                act.wait_ge(raw_in[raw_slot], 16 * (n // RAW + 1) if count is None else count)
                if not isinstance(n, int) or n >= 2:
                    act.wait_ge(blk_done, n - 1)
                act.activation(w_hi[:, slot, 0:w], raw[:, raw_slot, 0:w], ACT.Copy)\
                    .then_inc(w_hi_ready, 1)

            def square(v, k, slot, src, cols=S, first=False):
                if v:
                    if first:
                        act.wait_ge(acc_ready, SQUARES * v)
                if not first:
                    act.wait_ge(acc_ready, k + SQUARES * v)
                act.activation(sq[:, slot, 0:cols], src, ACT.Square).then_inc(sq_ready, 1)

            def operand(k, g):
                act.activation(a_hi[:, k, :], x[:, k, :], ACT.Copy, scale=gains[:, g, bass.ds(k, 1)])\
                    .then_inc(a_hi_ready, 1)

            def spread(v, dst, cols=S):
                act.wait_ge(norm_spread, v + 1)
                act.activation(dst, ps[:, stat_bank, 0:cols], ACT.Copy).then_inc(rstd_ready, 1)

            def residual(k, q, v, g, slot, first=False):
                act.wait_ge(lin_read, q + 1)
                square(v, k, slot, x[:, k, :], first=first)
                if v == V_LAST:
                    if not first:
                        act.wait_ge(acc2_ready, k)
                    act.activation(sq2[:, slot, :], x[:, k, :], ACT.Square,
                                   scale=gains[:, G_FINAL, bass.ds(k, 1)]).then_inc(sq2_ready, 1)
                operand(k, g)

            def mem_exps(layer, i):
                u, pm = 4 * layer + i, (pm0, pm1)[layer]
                act.wait_ge(mem_max, u + 1)
                if i >= 2:
                    act.wait_ge(mem_turned, 2 * (u - 1))
                for b in range(TB):
                    act.activation(pm[:, u % 2, b, :], ps[:, 2 + b // 2, b % 2 * NMEM:(b % 2 + 1) * NMEM],
                                   ACT.Exp, bias=nmx[:, u % 2, b:b + 1],
                                   accum_out=den[:, u % 2, b:b + 1]).then_inc(mem_exp, 1)

            def mem_evac(layer, i):
                u, pT = 4 * layer + i, (pmT0, pmT1)[layer]
                act.wait_ge(mem_turned, 2 * u + 2)
                if i:
                    act.wait_ge(mem_pv, u)
                act.activation(pT[:, 1, :], ps[:, 5, :], ACT.Copy).then_inc(mem_pT1, 1)

            def mem_out(layer, t):
                act.wait_ge(mem_pv, 4 * layer + 2 * t + 2)
                act.activation(y_hi[:, CT + t, :], ps[:, 6 + t, :], ACT.Copy).then_inc(ym_hi_ready, 1)

            def mem_step(layer, n):
                if n - 1 in MEM_STEPS[layer]:
                    mem_evac(layer, MEM_STEPS[layer][n - 1])
                if n in MEM_STEPS[layer]:
                    mem_exps(layer, MEM_STEPS[layer][n])
                if n - 2 in MEM_STEPS[layer] and MEM_STEPS[layer][n - 2] % 2:
                    mem_out(layer, MEM_STEPS[layer][n - 2] // 2)

            act.wait_ge(ones_ready, 1)
            act.activation(half[:], ones[:, 0:TB], ACT.Copy, scale=-0.5).then_inc(half_ready, 1)
            mid = KT * P // 2
            act.wait_ge(first_in, 16)
            act.activation(w_hi[:, 0, 0:mid], raw[:, 0, 0:mid], ACT.Copy).then_inc(first_hi, 1)
            act.wait_ge(gains_in, 16)
            for k in range(KT):
                act.wait_ge(x_in[k // 2], 16)
                operand(k, G_MIX0)
                if k == 1:
                    act.wait_ge(raw_in[0], 16)
                    act.activation(w_hi[:, 0, mid:KT * P], raw[:, 0, mid:KT * P], ACT.Copy)\
                        .then_inc(w_hi_ready, 1)
                if k == 5:
                    split(1, KT * P)
            for k in range(KT):
                square(V_MIX0, k, k % 2, x[:, k, :], first=k < 2)
                if k == 3:
                    split(2, KT * P)

            def l0_strip(n):
                if N_CONV0 <= n < N_MEMKV:
                    return "ucb"[n - N_CONV0], 0
                if n >= N_CONV:
                    return "ucb"[(n - N_CONV) % 3], 1 + (n - N_CONV) // 3
                return "q" if n < N_CONV0 else "m", 0

            def conv_out(i):
                act.wait_ge(conv_step, 5 * i + 5)
                act.activation(y_hi[:, i, :], y_s[:], ACT.Copy).then_inc(yc_hi_ready, 1)

            for n in range(N_QM0, N_OUT0 + 1):
                if n:
                    kind, i = l0_strip(n - 1)
                    if kind == "b":
                        conv_out(i)
                if n >= 2:
                    split(n + 1, KT * P)
                if n == 1:
                    act.wait_ge(mem_in, 16)
                    for k in range(KT):
                        act.activation(mem_hi[:, k, :], memx[:, k, :], ACT.Copy,
                                       scale=gains[:, G_MEM, k:k + 1]).then_inc(mem_hi_ready, 1)
                if n == 2:
                    act.wait_ge(table_mm, 1)
                    act.activation(table[:], ps[0:12, 6, 0:NREL], ACT.Copy).then_inc(table_ready, 1)
                if n == 4:
                    spread(V_MIX0, rstd[:])
                    for k in range(KT):
                        square(V_MEM, k, k % 2, memx[:, k, :], NMEM, first=k < 2)
                if n == 7:
                    spread(V_MEM, rmem[:], NMEM)
                mem_step(0, n)
            act.wait_ge(table_ready, 1)
            act.dma_start(scratch, table[:]).then_inc(table_out, 16)

            def out_phase(n0, v, g):
                for n in range(n0 + 1, n0 + KT):
                    residual(n - 1 - n0, out_index(n - 1), v, g, (n - 1 - n0) % 2, first=n - 1 - n0 < 2)
                    split(n + 1, KT * P)
                residual(KT - 1, out_index(n0 + KT - 1), v, g, 1)
                split(n0 + KT + 1, KT * P)

            def ffn(layer, n0, v, q0, r0):
                def body(i, first=False, last=False):
                    for j in range(2):
                        n = i * 4 + (n0 + 2 * j)
                        q = i * 4 + (q0 + 2 * j)
                        p = i * 2 + (FT * layer + j)
                        w = SLOT if last and j else KT * P
                        count = (i + (r0 + 1 + j)) * 16
                        m = i * 2 + j
                        if first and j == 0:
                            split(n + 2, w, 0, 2, count)
                            spread(v, rstd[:])
                        act.wait_ge(lin_read, q + 1)
                        act.activation(tmp[:, 2 * j, :], tmp[:, 2 * j, :], ACT.Silu).then_inc(silu_ready, 1)
                        if not (first and j == 0):
                            split(n + 2, w, 0, (2 * j + 2) % 4, count)
                        act.wait_ge(gu_ready, p + 1)
                        act.activation(g_hi[:, m, :], tmp[:, 2 * j + 1, :], ACT.Copy).then_inc(g_hi_ready, 1)
                        split(n + 3, w, 1, (2 * j + 3) % 4, count)
                body(0, first=True)
                with act.Fori(1, FT // 2 - 1, 1) as i:
                    body(i)
                body(FT // 2 - 1, last=True)

            def down(n0, q0, v, g, r0):
                def body(i, first=False, last=False):
                    for j in range(2):
                        n = i * 4 + (n0 + 2 * j)
                        w = KT * P if last and j else SLOT
                        count = (i + (r0 + 1 + (1 if j else 0))) * 16
                        split(n + 2, w, 0, (2 * j + 2) % 4, count)
                        residual(i * 2 + j, i * 2 + (q0 + j), v, g, j, first=first)
                        split(n + 3, w, 1, (2 * j + 3) % 4, count)
                body(0, first=True)
                with act.Fori(1, KT // 2 - 1, 1) as i:
                    body(i)
                body(KT // 2 - 1, last=True)

            out_phase(N_OUT0, V_FFN0, G_FFN0)
            ffn(0, N_FFN0, V_FFN0, out_index(N_FFN0), N_FFN0 // RAW)
            down(N_DOWN0, N_DOWN0, V_MIX1, G_MIX1, N_DOWN0 // RAW)

            act.dma_start(flip[:], a["flip"]).then_inc(band_in, 16)
            act.wait_ge(table_out, 16)
            toeplitz = bass.AP(tensor=scratch.tensor, offset=scratch.offset,
                               ap=[[1, P], [NREL, 12], [1, 256]])
            act.dma_start(band[:].rearrange("p (h j) -> p h j", h=12), toeplitz).then_inc(band_in, 16)
            for k in range(KT):
                act.activation(kv_hi[:, k, :], x[:, k, :], ACT.Copy, scale=gains[:, G_KV, k:k + 1])\
                    .then_inc(kv_hi_ready, 1)

            def sw_exps(u):
                keys = sw_unit(u)[3]
                act.wait_ge(sw_max, u + 1)
                if u >= 2:
                    act.wait_ge(sw_turned, 2 * (u - 1))
                else:
                    act.wait_ge(mem_pv, 8)
                for g in range(GROUP):
                    act.activation(p_sw[:, u % 2, g, 0:1 + keys], s_sw[:, u % 2, g, 0:1 + keys], ACT.Exp,
                                   bias=nmx[:, u % 2, g:g + 1], accum_out=den[:, u % 2, g:g + 1])\
                        .then_inc(sw_exp, 1)

            def sw_evac(u):
                act.wait_ge(sw_turned, 2 * u + 2)
                if u:
                    act.wait_ge(sw_pv, u)
                tiles = sw_unit(u)[3] // P
                act.activation(pT_sw[:, 0:tiles, :], ps[:, 6:6 + tiles, 0:GROUP * P], ACT.Copy)\
                    .then_inc(sw_pT, 1)

            def sw_out(u):
                hp, b, s, _, _ = sw_unit(u)
                act.wait_ge(sw_pv, u + 1)
                act.activation(y_hi[:, GROUP * hp:GROUP * hp + GROUP, b * P:(b + 1) * P],
                               ps[:, sw_bank(u), 0:GROUP * P].rearrange("p (g t) -> p g t", g=GROUP),
                               ACT.Copy).then_inc(ys_hi_ready, 1)

            def sw_step(w):
                if 2 <= w < NSW + 2:
                    sw_evac(w - 2)
                if w < NSW:
                    sw_exps(w)
                if 2 <= w < NSW + 2 and w % 2:
                    sw_out(w - 2)

            for n in range(N_KV, N_OUT1 + 1):
                if n > N_KV:
                    split(n + 1, KT * P)
                if n == N_KV + 2:
                    spread(V_MIX1, rstd[:])
                mem_step(1, n)
                if SW_FIRST <= n < N_OUT1:
                    sw_step(n - SW_FIRST)
                if n == N_OUT1:
                    for w in range(n - SW_FIRST, NSW + 3):
                        sw_step(w)
            out_phase(N_OUT1, V_FFN1, G_FFN1)
            ffn(1, N_FFN1, V_FFN1, out_index(N_FFN1), N_FFN1 // RAW)
            act.wait_ge(gain_ready, 1)
            down(N_DOWN1, out_index(N_DOWN1), V_LAST, G_PRE, N_DOWN1 // RAW)

            act.wait_ge(lin_read, out_index(N_SECOND))
            act.dma_start(rope_n[:], a["rope"][0]).then_inc(rope_in, 16)
            act.dma_start(rope_r[:], a["rope"][1]).then_inc(rope_in, 16)

            def ns_exps(u):
                b, g, br, keys = ns_unit(u)
                act.wait_ge(ns_max, u + 1)
                if u >= 2:
                    act.wait_ge(ns_turned, GH * (u - 1))
                for j in range(GH):
                    act.activation(p_n[:, u % 2, j, 0:keys], ps[:, 2 + j, 0:keys], ACT.Exp,
                                   bias=nmx[:, u % 2, j:j + 1], accum_out=den[:, u % 2, j:j + 1])\
                        .then_inc(ns_exp, 1)

            def ns_evac(u):
                b, g, br, keys = ns_unit(u)
                if u:
                    act.wait_ge(ns_pv, u)
                for j in (1, 3):
                    act.wait_ge(ns_turned, GH * u + j + 1)
                    act.activation(pT_n[:, 0:b + 1, j * P:(j + 1) * P],
                                   ps[:, 7, 0:keys].rearrange("p (c t) -> p c t", t=P), ACT.Copy)\
                        .then_inc(ns_pTa, 1)

            def ns_out(u):
                b, g, br, keys = ns_unit(u)
                if g and br:
                    act.wait_ge(ns_pv, u + 1)
                    act.activation(oa[:, :, b * P:(b + 1) * P],
                                   ps[:, 1, :].rearrange("p (j t) -> p j t", j=GH), ACT.Copy)\
                        .then_inc(oa_ready, 1)

            def ret_evac(h):
                act.wait_ge(rt_turned, 2 * h + 2)
                act.activation(ob[h // 2][:, h % 2 * 2 + 1, :], ps[:, 7, :], ACT.Copy).then_inc(rt_ob1, 1)

            def gate_strip(n, func):
                e = gated_index(n)
                act.wait_ge(lin_read, out_index(n) + 1)
                act.activation(tmp[:, e % 4, :], tmp[:, e % 4, :], func).then_inc(gated, 1)

            def rounded(i, src, dst):
                act.wait_ge(prod_ready, i + 1)
                act.activation(dst, src, ACT.Copy).then_inc(zh_ready, 1)

            def epilogue(n):
                e = gated_index(n)
                if n < N_ZN:
                    return
                if n < N_MA:
                    gate_strip(n, ACT.Silu)
                    rounded(n - N_ZN, tmp[:, e % 4, :], ya_hi[:, n - N_ZN, :])
                elif n < N_ZR:
                    if (n - N_MA) % 2 == 0:
                        gate_strip(n, ACT.Sigmoid)
                elif n < N_MB:
                    gate_strip(n, ACT.Silu)
                    rounded(4 + n - N_ZR, tmp[:, e % 4, :], yb_hi[:, n - N_ZR, :])
                elif n < N_FIN:
                    i = (n - N_MB) // 2
                    if (n - N_MB) % 2 == 0:
                        gate_strip(n, ACT.Sigmoid)
                    else:
                        rounded(12 + i, tmp[:, e % 4, :], mg_hi[:, i, :])
                else:
                    i = n - N_FIN
                    act.wait_ge(blk_done, n + 1)
                    square(V_POST - 1, i, i % 2, ps[:, n % 2, :], first=i < 2)
                    act.activation(yg[:, i, :], ps[:, n % 2, :], ACT.Copy,
                                   scale=gains[:, G_POST, i:i + 1]).then_inc(fin_read, 1)

            for n in range(N_SECOND, N_END):
                if NS_FIRST < n <= NS_FIRST + NS:
                    ns_evac(n - 1 - NS_FIRST)
                if NS_FIRST + 2 <= n <= NS_FIRST + NS:
                    ns_out(n - 2 - NS_FIRST)
                if n == NS_FIRST + NS:
                    ns_out(NS - 1)
                if n > N_SECOND:
                    epilogue(n - 1)
                    if n + 1 < N_END:
                        split(n + 1, width(n + 1))
                if n == N_SECOND + 3:
                    spread(V_LAST, rstd[:])
                if n == N_SECOND + 4:
                    spread(V_PRE, r1[:])
                if n in (N_SECOND + 6, N_SECOND + 8):
                    i = (n - N_SECOND - 6) // 2
                    act.wait_ge(cmp_hidden, i + 1)
                    if i:
                        act.wait_ge(cmp_mm, 1)
                    act.activation(hid[:], ps[:, 7 if i else 4, 0:4 * NCMP].rearrange("p (m c) -> p m c", m=2),
                                   ACT.Gelu_apprx_tanh).then_inc(cmp_gelu, 1)
                if n == N_RET:
                    act.wait_ge(small2_in, 16 * 5)
                    act.wait_ge(lin_read, out_index(N_GATE) + 1)
                    act.activation(tmp[0:24, 2, :], tmp[0:24, 2, :], ACT.Sigmoid, bias=gate_b[:])\
                        .then_inc(gate_sig, 1)
                if NS_FIRST <= n < NS_FIRST + NS:
                    ns_exps(n - NS_FIRST)
                if NS_FIRST <= n < NS_FIRST + 2:
                    g = n - NS_FIRST
                    act.wait_ge(cm_step, 3 * g + 3)
                    act.activation(p_c[:, g], p_c[:, g], ACT.Exp).then_inc(cm_exp, 1)
                if n == RT_FIRST - 1:
                    act.wait_ge(ns_turned, GH * NS)
                    act.dma_start(decay[:], a["decay"]).then_inc(decay_in, 16)
                if RT_FIRST + 2 <= n < RT_FIRST + 2 + RH:
                    ret_evac(n - RT_FIRST - 2)
            epilogue(N_END - 1)
            spread(V_POST, rstd[:])

        @block.vector
        def _(dve):
            def split(n, w, slot=None, raw_slot=None):
                slot = n % 2 if slot is None else slot
                raw_slot = n % RAW if raw_slot is None else raw_slot
                dve.wait_ge(w_hi_ready, n + 1)
                dve.tensor_tensor(w_lo[:, slot, 0:w], raw[:, raw_slot, 0:w],
                                  w_hi[:, slot, 0:w].bitcast(F32), ALU.subtract).then_inc(w_lo_ready, 1)

            def operand(k, g, count):
                dve.wait_ge(a_hi_ready, count)
                dve.scalar_tensor_tensor(a_lo[:, k, :], x[:, k, :], gains[:, g, bass.ds(k, 1)],
                                         a_hi[:, k, :].bitcast(F32), ALU.mult, ALU.subtract)\
                    .then_inc(a_lo_ready, 1)

            def variance(v, eps, tiles=TB):
                dve.wait_ge(norm_sum, v + 1)
                dve.tensor_scalar(var[:, 0:tiles], ps[:, stat_bank, 0:tiles], 1.0 / D, eps,
                                  ALU.mult, ALU.add).then_inc(norm_var, 1)

            def diagonal(v, tiles=TB, rs=rs):
                dve.wait_ge(norm_pow, v + 1)
                dve.tensor_tensor(diag[:, 0:tiles, :],
                                  ident[:].unsqueeze(1).to_broadcast([P, tiles, P]),
                                  rs[:, 0:tiles].unsqueeze(2).to_broadcast([P, tiles, P]), ALU.mult)\
                    .then_inc(norm_diag, 1)

            def scaled(n, bank, dst, factor=None):
                dve.wait_ge(blk_done, n + 1)
                if factor is None:
                    ins = dve.tensor_tensor(dst, ps[:, bank, :], rstd[:], ALU.mult)
                else:
                    ins = dve.scalar_tensor_tensor(dst, ps[:, bank, :], factor, rstd[:], ALU.mult, ALU.mult)
                ins.then_inc(lin_read, 1)

            def memory_scaled(n, bank, dst):
                dve.wait_ge(blk_done, n + 1)
                dve.tensor_tensor(dst, ps[:, bank, 0:NMEM], rmem[:], ALU.mult).then_inc(lin_read, 1)

            def residual(k, n, bank, g, count):
                dve.wait_ge(blk_done, n + 1)
                dve.tensor_tensor(x[:, k, :], x[:, k, :], ps[:, bank, :], ALU.add).then_inc(lin_read, 1)

            def mem_maxima(layer, i):
                u = 4 * layer + i
                dve.wait_ge(mem_scores, u + 1)
                dve.tensor_reduce(nmx[:, u % 2, :], ps[:, 2:4, :].rearrange("p k (b m) -> p (k b) m", b=2),
                                  AX.X, ALU.max, negate=True).then_inc(mem_max, 1)

            def mem_normalise(layer, i):
                u, pm = 4 * layer + i, (pm0, pm1)[layer]
                dve.wait_ge(mem_exp, 4 * u + 4)
                dve.reciprocal(den[:, u % 2, :], den[:, u % 2, :]).then_inc(mem_rden, 1)
                dve.wait_ge(mem_rden, u + 1)
                dve.tensor_tensor(pm[:, u % 2], pm[:, u % 2],
                                  den[:, u % 2, :].unsqueeze(2).to_broadcast([P, TB, NMEM]), ALU.mult)\
                    .then_inc(mem_probs, 1)

            def mem_evac(layer, i):
                u, pT = 4 * layer + i, (pmT0, pmT1)[layer]
                dve.wait_ge(mem_turned, 2 * u + 1)
                if i:
                    dve.wait_ge(mem_pv, u)
                dve.tensor_copy(pT[:, 0, :], ps[:, 4, :]).then_inc(mem_pT0, 1)

            def mem_out(layer, t):
                dve.wait_ge(ym_hi_ready, 2 * layer + t + 1)
                dve.tensor_tensor(y_lo[:, CT + t, :], ps[:, 6 + t, :], y_hi[:, CT + t, :].bitcast(F32),
                                  ALU.subtract).then_inc(ym_lo_ready, 1)

            def mem_step(layer, n):
                if n - 1 in MEM_STEPS[layer]:
                    mem_evac(layer, MEM_STEPS[layer][n - 1])
                if n in MEM_STEPS[layer]:
                    mem_maxima(layer, MEM_STEPS[layer][n])
                if n - 2 in MEM_STEPS[layer] and MEM_STEPS[layer][n - 2] % 2:
                    mem_out(layer, MEM_STEPS[layer][n - 2] // 2)
                if n in MEM_STEPS[layer]:
                    mem_normalise(layer, MEM_STEPS[layer][n])

            mid = KT * P // 2
            dve.wait_ge(first_hi, 1)
            dve.tensor_tensor(w_lo[:, 0, 0:mid], raw[:, 0, 0:mid], w_hi[:, 0, 0:mid].bitcast(F32),
                              ALU.subtract).then_inc(first_lo, 1)
            for k in range(KT):
                operand(k, G_MIX0, k + 1)
                if k == 1:
                    dve.wait_ge(w_hi_ready, 1)
                    dve.tensor_tensor(w_lo[:, 0, mid:KT * P], raw[:, 0, mid:KT * P],
                                      w_hi[:, 0, mid:KT * P].bitcast(F32), ALU.subtract)\
                        .then_inc(w_lo_ready, 1)
                if k == 5:
                    split(1, KT * P)

            def l0_epilogue(n):
                bank = bank_of(n)
                if n < N_CONV0:
                    scaled(n, bank, qm0[:, n, :], SCALE)
                    return
                if N_MEMKV <= n < N_CONV:
                    t = n - N_MEMKV
                    if t < 4:
                        memory_scaled(n, bank, (mk0, mk1)[t // 2][:, t % 2, :])
                    else:
                        t -= 4
                        if t:
                            dve.wait_ge(mv_turned, t)
                        memory_scaled(n, bank, mvt[:])
                    return
                i = 0 if n < N_CONV else 1 + (n - N_CONV) // 3
                what = n - N_CONV0 if n < N_CONV else (n - N_CONV) % 3
                if what == 0:
                    scaled(n, bank, u_s[:])
                elif what == 1:
                    scaled(n, bank, v_s[:])
                    dve.wait_ge(lin_read, n + 1)
                    dve.tensor_tensor(v_s[:], v_s[:], u_s[:], ALU.mult).then_inc(conv_step, 1)
                    dve.wait_ge(conv_step, 5 * i + 1)
                    dve.tensor_scalar(y_s[:], v_s[:], conv_w[:, i, 2:3], None, ALU.mult)\
                        .then_inc(conv_step, 1)
                    for back in (1, 2):
                        dve.wait_ge(conv_step, 5 * i + 1 + back)
                        dve.scalar_tensor_tensor(y_s[:, back:S], v_s[:, 0:S - back],
                                                 conv_w[:, i, 2 - back:3 - back], y_s[:, back:S],
                                                 ALU.mult, ALU.add).then_inc(conv_step, 1)
                else:
                    scaled(n, bank, u_s[:])
                    dve.wait_ge(lin_read, n + 1)
                    dve.tensor_tensor(y_s[:], y_s[:], u_s[:], ALU.mult).then_inc(conv_step, 1)
                    dve.wait_ge(yc_hi_ready, i + 1)
                    dve.tensor_tensor(y_lo[:, i, :], y_s[:], y_hi[:, i, :].bitcast(F32), ALU.subtract)\
                        .then_inc(yc_lo_ready, 1)

            def mv_evac(t):
                dve.wait_ge(mv_turned, t + 1)
                dst = (mv0, mv1)[t // 2][:, :, t % 2 * P:(t % 2 + 1) * P]
                dve.tensor_copy(dst, ps[:, 6, 0:NMEM].rearrange("p (m f) -> p m f", m=2))\
                    .then_inc(mv_ready, 1)

            for n in range(N_QM0, N_OUT0 + 1):
                if n == 4:
                    dve.wait_ge(rstd_ready, 1)
                    for m in range(3):
                        l0_epilogue(m)
                if n == 7:
                    dve.wait_ge(rstd_ready, 2)
                    l0_epilogue(5)
                if n >= 4 and n != 6:
                    l0_epilogue(n - 1)
                if n >= 1:
                    split(n + 1, KT * P)
                if n == 1:
                    for k in range(KT):
                        dve.wait_ge(mem_hi_ready, k + 1)
                        dve.scalar_tensor_tensor(mem_lo[:, k, :], memx[:, k, :], gains[:, G_MEM, k:k + 1],
                                                 mem_hi[:, k, :].bitcast(F32), ALU.mult, ALU.subtract)\
                            .then_inc(mem_lo_ready, 1)
                if n == 3:
                    variance(V_MIX0, EPS_A)
                    dve.wait_ge(const_in, 16 * 2)
                    diagonal(V_MIX0)
                if n == 6:
                    variance(V_MEM, EPS_A, 2)
                    diagonal(V_MEM, 2)
                if N_MEMKV + 6 <= n <= N_MEMKV + 9:
                    mv_evac(n - N_MEMKV - 6)
                mem_step(0, n)

            def out_phase(n0, g, count):
                for m in range(KT):
                    residual(m, n0 + m, (n0 + m) % 2, g, 0)
                    operand(m, g, count + m + 1)
                    split(n0 + m + 2, KT * P)

            def ffn(layer, n0, v, q0):
                def body(i, first=False, last=False):
                    for j in range(2):
                        n = i * 4 + (n0 + 2 * j)
                        q = i * 4 + (q0 + 2 * j)
                        p = i * 2 + (FT * layer + j)
                        w = SLOT if last and j else KT * P
                        if first and j == 0:
                            diagonal(v)
                            split(n + 2, w, 0, 2)
                            dve.wait_ge(rstd_ready, v + 1)
                        scaled(n, 2 * j, tmp[:, 2 * j, :])
                        if not (first and j == 0):
                            split(n + 2, w, 0, (2 * j + 2) % 4)
                        scaled(n + 1, 2 * j + 1, tmp[:, 2 * j + 1, :])
                        dve.wait_ge(silu_ready, p + 1)
                        dve.wait_ge(lin_read, q + 2)
                        dve.tensor_tensor(tmp[:, 2 * j + 1, :], tmp[:, 2 * j, :], tmp[:, 2 * j + 1, :],
                                          ALU.mult).then_inc(gu_ready, 1)
                        dve.wait_ge(g_hi_ready, p + 1)
                        m = i * 2 + j
                        dve.tensor_tensor(g_lo[:, m, :], tmp[:, 2 * j + 1, :],
                                          g_hi[:, m, :].bitcast(F32), ALU.subtract)\
                            .then_inc(g_lo_ready, 1)
                        split(n + 3, w, 1, (2 * j + 3) % 4)
                variance(v, EPS_A)
                body(0, first=True)
                with dve.Fori(1, FT // 2 - 1, 1) as i:
                    body(i)
                body(FT // 2 - 1, last=True)

            def down(n0, g, count):
                def body(i, last=False):
                    for j in range(2):
                        n = i * 4 + (n0 + 2 * j)
                        m = i * 2 + j
                        w = KT * P if last and j else SLOT
                        split(n + 2, w, 0, (2 * j + 2) % 4)
                        residual(m, n + 1, j, g, 0)
                        operand(m, g, i * 2 + (count + j + 1))
                        split(n + 3, w, 1, (2 * j + 3) % 4)
                with dve.Fori(0, KT // 2 - 1, 1) as i:
                    body(i)
                body(KT // 2 - 1, last=True)

            out_phase(N_OUT0, G_FFN0, KT)
            dve.wait_ge(table_out, 16)
            dve.tensor_tensor(gains[:, G_PRE, :], gains[:, G_PRE, :], gains[:, G_FINAL, :], ALU.mult)\
                .then_inc(gain_ready, 1)
            ffn(0, N_FFN0, V_FFN0, out_index(N_FFN0))
            down(N_DOWN0, G_MIX1, 2 * KT)

            for k in range(KT):
                dve.wait_ge(kv_hi_ready, k + 1)
                dve.scalar_tensor_tensor(kv_lo[:, k, :], x[:, k, :], gains[:, G_KV, k:k + 1],
                                         kv_hi[:, k, :].bitcast(F32), ALU.mult, ALU.subtract)\
                    .then_inc(kv_lo_ready, 1)

            def sw_maxima(u):
                hp, b, s, keys, _ = sw_unit(u)
                h = 2 * hp + s
                lg = ps[:, 2 + 2 * (u % 2):4 + 2 * (u % 2), :].rearrange("p k (g m) -> p (k g) m", g=2)
                dve.wait_ge(sw_scores, u + 1)
                if u >= 2:
                    dve.wait_ge(sw_exp, GROUP * (u - 1))
                else:
                    dve.wait_ge(mem_turned, 16)
                dve.tensor_tensor(s_sw[:, u % 2, :, 1:1 + keys], lg[:, 0:GROUP, 0:keys],
                                  bias[:, GROUP * h:GROUP * h + GROUP, 256 - keys:256], ALU.add)\
                    .then_inc(sw_biased, 1)
                dve.wait_ge(sw_biased, u + 1)
                dve.wait_ge(sw_sink, u + 1)
                dve.tensor_reduce(nmx[:, u % 2, 0:GROUP], s_sw[:, u % 2, :, 0:1 + keys], AX.X, ALU.max,
                                  negate=True).then_inc(sw_max, 1)

            def sw_normalise(u):
                keys = sw_unit(u)[3]
                dve.wait_ge(sw_exp, GROUP * (u + 1))
                dve.reciprocal(den[:, u % 2, 0:GROUP], den[:, u % 2, 0:GROUP]).then_inc(sw_den, 1)
                dve.wait_ge(sw_den, u + 1)
                dve.tensor_tensor(p_sw[:, u % 2, :, 1:1 + keys], p_sw[:, u % 2, :, 1:1 + keys],
                                  den[:, u % 2, 0:GROUP].unsqueeze(2).to_broadcast([P, GROUP, keys]),
                                  ALU.mult).then_inc(sw_probs, 1)

            def sw_out(u):
                hp, b, s, _, _ = sw_unit(u)
                dve.wait_ge(ys_hi_ready, u // 2 + 1)
                dve.tensor_tensor(y_lo[:, GROUP * hp:GROUP * hp + GROUP, b * P:(b + 1) * P],
                                  ps[:, sw_bank(u), 0:GROUP * P].rearrange("p (g t) -> p g t", g=GROUP),
                                  y_hi[:, GROUP * hp:GROUP * hp + GROUP, b * P:(b + 1) * P].bitcast(F32),
                                  ALU.subtract).then_inc(ys_lo_ready, 1)

            def sw_step(w):
                if w < NSW:
                    sw_maxima(w)
                if 1 <= w < NSW + 1:
                    sw_normalise(w - 1)
                if 3 <= w < NSW + 3 and w % 2 == 0:
                    sw_out(w - 3)

            def l1_epilogue(n):
                if n < N_KV + 2:
                    scaled(n, bank_of(n), kT[:, n - N_KV, :])
                elif n < N_QM1:
                    if n > N_KV + 2:
                        dve.wait_ge(v_turned, 1)
                    scaled(n, bank_of(n), vT[:])
                elif n < N_Q:
                    scaled(n, bank_of(n), qm1[:, n - N_QM1, :], SCALE)
                else:
                    scaled(n, bank_of(n), qT[:, n - N_Q, :], SCALE)

            for n in range(N_KV, N_OUT1 + 1):
                if n == N_KV + 2:
                    diagonal(V_MIX1)
                    split(n + 1, KT * P)
                    dve.wait_ge(rstd_ready, V_MIX1 + 1)
                    l1_epilogue(N_KV)
                if n >= N_KV + 2:
                    l1_epilogue(n - 1)
                if n > N_KV and n != N_KV + 2:
                    split(n + 1, KT * P)
                if n == N_KV + 1:
                    variance(V_MIX1, EPS_A)
                if n in (N_KV + 4, N_KV + 5):
                    t = n - N_KV - 4
                    dve.wait_ge(v_turned, t + 1)
                    dve.tensor_copy(vn[:, :, t * P:(t + 1) * P],
                                    ps[:, 7, :].rearrange("p (b f) -> p b f", b=TB)).then_inc(vn_ready, 1)
                if n in (N_KV + 3, N_KV + 4):
                    for c in range(3 * (n - N_KV - 3), 3 * (n - N_KV - 3) + 3):
                        dve.wait_ge(flip_mm, c + 1)
                        dve.tensor_copy(bias[:].rearrange("p h j -> p (h j)")[:, c * S:(c + 1) * S],
                                        ps[:, 4 + c % 3, :]).then_inc(bias_ready, 1)
                mem_step(1, n)
                if SW_FIRST <= n < N_OUT1:
                    sw_step(n - SW_FIRST)
                if n == N_OUT1:
                    for w in range(n - SW_FIRST, NSW + 3):
                        sw_step(w)
            out_phase(N_OUT1, G_FFN1, 3 * KT)
            ffn(1, N_FFN1, V_FFN1, out_index(N_FFN1))
            dve.wait_ge(gain_ready, 1)
            down(N_DOWN1, G_PRE, 4 * KT)

            def rotate(n):
                kind, dst = ROPE[n]
                i = turned_before(n)[0]
                table_of = (rope_n, rope_r)[kind]
                src = strip_of(n)
                dve.wait_ge(rope_in, 16 * 2)
                dve.wait_ge(lin_read, out_index(n) + 1)
                dve.tensor_tensor(dst, src, table_of[:, 0, :], ALU.mult).then_inc(rope_mul, 1)
                dve.wait_ge(rope_mm, i + 1)
                dve.wait_ge(rope_mul, 2 * i + 1)
                dve.tensor_tensor(src, ps[:, turn_bank(n), :], table_of[:, 1, :], ALU.mult)\
                    .then_inc(rope_mul, 1)
                dve.wait_ge(rope_mul, 2 * i + 2)
                dve.tensor_tensor(dst, dst, src, ALU.add).then_inc(rope_ready, 1)

            def turn(n):
                dve.wait_ge(turn_mm, turned_before(n)[1] + 1)
                dve.tensor_copy(TURN[n], ps[:, turn_bank(n), :].rearrange("p (b f) -> p b f", b=TB))\
                    .then_inc(turn_ready, 1)

            def windows_of(i):
                straight, swapped = (kcr, vcr)[i][:], ps[:, (4, 7)[i], :]
                dve.wait_ge(swap_mm, i + 1)
                dve.wait_ge(small2_in, 16 * 5)
                for g in range(2):
                    for odd in range(2):
                        r = slice(HD * odd, HD * odd + HD)
                        src = (straight if g == odd else swapped)[r].rearrange(
                            "p (c l o) -> p l c o", l=CSTRIDE // 2, o=2)
                        for w in range(2):
                            ls = slice(CSTRIDE // 2 * w, CSTRIDE // 2 * (w + 1))
                            dve.tensor_tensor(windows[i][r, ls, g * NCMP:(g + 1) * NCMP],
                                              src[:, :, w:w + NCMP, odd],
                                              pe2[r, i, ls].unsqueeze(2).to_broadcast([HD, CSTRIDE // 2, NCMP]),
                                              ALU.add).then_inc(windows_ready, 1)

            def cmp_maxima(g):
                s = ps[:, 7, 0:16 * NCMP].rearrange("p (k c) -> p k c", c=NCMP)
                dve.wait_ge(cm_scores, g + 1)
                dve.tensor_reduce(nm16[:], s, AX.X, ALU.max, negate=True).then_inc(cm_step, 1)
                dve.wait_ge(cm_step, 3 * g + 1)
                dve.tensor_scalar(nm16[:], nm16[:], -EMPTY, None, ALU.min).then_inc(cm_step, 1)
                dve.wait_ge(cm_step, 3 * g + 2)
                dve.tensor_tensor(p_c[:, g], s, nm16[:].unsqueeze(2).to_broadcast([P, 16, NCMP]), ALU.add)\
                    .then_inc(cm_step, 1)

            def cmp_normalise(g):
                dve.wait_ge(cm_exp, g + 1)
                dve.tensor_reduce(d16[:], p_c[:, g], AX.X, ALU.add).then_inc(cm_probs, 1)
                dve.wait_ge(cm_probs, 5 * g + 1)
                dve.tensor_scalar(d16[:], d16[:], TINY, None, ALU.max).then_inc(cm_probs, 1)
                dve.wait_ge(cm_probs, 5 * g + 2)
                dve.reciprocal(d16[:], d16[:]).then_inc(cm_probs, 1)
                dve.wait_ge(cm_probs, 5 * g + 3)
                dve.wait_ge(gate_ready, 1)
                w = d16[:].rearrange("p (b j) -> p b j", b=TB)
                dve.tensor_tensor(w, w, gate_n[:, :, 12 * g:12 * g + 12:3], ALU.mult).then_inc(cm_probs, 1)
                dve.wait_ge(cm_probs, 5 * g + 4)
                dve.tensor_tensor(p_c[:, g], p_c[:, g], d16[:].unsqueeze(2).to_broadcast([P, 16, NCMP]),
                                  ALU.mult).then_inc(cm_probs, 1)

            def ns_maxima(u):
                keys = ns_unit(u)[3]
                dve.wait_ge(ns_scores, u + 1)
                dve.tensor_reduce(nmx[:, u % 2, :], ps[:, 2:6, 0:keys], AX.X, ALU.max, negate=True)\
                    .then_inc(ns_max, 1)

            def ns_normalise(u):
                b, g, br, keys = ns_unit(u)
                dve.wait_ge(ns_exp, GH * u + GH)
                dve.reciprocal(den[:, u % 2, :], den[:, u % 2, :]).then_inc(ns_den, 1)
                dve.wait_ge(ns_den, 2 * u + 1)
                dve.wait_ge(gate_ready, 1)
                dve.tensor_tensor(den[:, u % 2, :], den[:, u % 2, :],
                                  gate_n[:, b, 12 * g + 1 + br:12 * g + 12:3], ALU.mult).then_inc(ns_den, 1)
                dve.wait_ge(ns_den, 2 * u + 2)
                dve.tensor_tensor(p_n[:, u % 2, :, 0:keys], p_n[:, u % 2, :, 0:keys],
                                  den[:, u % 2, :].unsqueeze(2).to_broadcast([P, GH, keys]), ALU.mult)\
                    .then_inc(ns_probs, 1)

            def ns_evac(u):
                b, g, br, keys = ns_unit(u)
                if u:
                    dve.wait_ge(ns_pv, u)
                for j in (0, 2):
                    dve.wait_ge(ns_turned, GH * u + j + 1)
                    dve.tensor_copy(pT_n[:, 0:b + 1, j * P:(j + 1) * P],
                                    ps[:, 6, 0:keys].rearrange("p (c t) -> p c t", t=P)).then_inc(ns_pTd, 1)
                if br:
                    dve.wait_ge(cm_turned, u // 2 + 1)
                    dve.tensor_copy(pT_c[:], ps[0:NCMP, 6, :]).then_inc(cm_pT, 1)

            def ret_mask(h):
                if h == 0:
                    dve.wait_ge(decay_in, 16)
                else:
                    dve.wait_ge(rt_out, h)
                dve.wait_ge(rt_scores, h + 1)
                for jc, (bank, c) in enumerate(((2, 0), (3, 0), (4, 0), (3, 3 * P))):
                    w = S - jc * P
                    dve.tensor_tensor(att[:, jc, 0:w], ps[:, bank, c:c + w], decay[:, h, 0:w], ALU.mult)\
                        .then_inc(rt_att, 1)

            def ret_bank(ic):
                return ps[:, (1, 5)[ic // 2], ic % 2 * RDV:(ic % 2 + 1) * RDV]

            def ret_norm(h):
                dve.wait_ge(rt_out, h + 1)
                for ic in range(TB):
                    dve.bn_stats(bn6[:, ic, :], ret_bank(ic)).then_inc(rt_stats, 1)
                for ic in range(TB):
                    dve.wait_ge(rt_stats, 8 * h + ic + 1)
                    dve.bn_aggr(bn2[:, h % 2, ic, :], bn6[:, ic, :]).then_inc(rt_stats, 1)
                dve.wait_ge(rt_stats, 8 * h + 8)
                dve.tensor_scalar(bn2[:, h % 2, :, 1], bn2[:, h % 2, :, 1], EPS_B, None, ALU.add)\
                    .then_inc(rt_var, 1)
                dve.wait_ge(rt_pow, h + 1)
                if h:
                    dve.wait_ge(rt_turned, 2 * h)
                for ic in range(TB):
                    dve.tensor_scalar(on[:, ic, :], ret_bank(ic), bn2[:, h % 2, ic, 0:1],
                                      bn2[:, h % 2, ic, 1:2], ALU.subtract, ALU.mult).then_inc(rt_norm, 1)

            def ret_evac(h):
                dve.wait_ge(rt_turned, 2 * h + 1)
                dve.tensor_copy(ob[h // 2][:, h % 2 * 2, :], ps[:, 6, :]).then_inc(rt_ob0, 1)

            def left_over(i, src, hi, lo):
                dve.wait_ge(zh_ready, i + 1)
                dve.tensor_tensor(lo, src, hi.bitcast(F32), ALU.subtract).then_inc(zl_ready, 1)

            def epilogue(n):
                bank, q = bank_of(n), out_index(n)
                e = gated_index(n)
                t = tmp[:, e % 4, :]
                if n == N_SECOND + 1:
                    scaled(n, bank, vcr[:])
                elif n == N_GATE:
                    dve.wait_ge(blk_done, n + 1)
                    dve.tensor_tensor(tmp[0:24, 2, :], ps[0:24, bank, :], rstd[0:24, :], ALU.mult)\
                        .then_inc(lin_read, 1)
                elif n < N_ZN:
                    head = (n - N_RET) % 4 if n >= N_RET else -1
                    before = n - 4 if n < N_RET else n - 2
                    if before in ROPE and (n < N_RET or before >= N_RET):
                        dve.wait_ge(rope_ready, read_of(before)[0])
                    if before in TURN and (n < N_RET or before >= N_RET):
                        dve.wait_ge(turn_ready, read_of(before)[1])
                    factor = SCALE if N_SECOND + 4 <= n < N_SECOND + 8 else (P ** -0.5 if head == 1 else None)
                    scaled(n, bank, strip_of(n), factor)
                elif n < N_MA or N_ZR <= n < N_MB:
                    i = n - N_ZN if n < N_MA else n - N_ZR
                    scaled(n, bank, t)
                    if n < N_MA:
                        dve.wait_ge(oa_ready, TB)
                        o, hi, lo, k = oa[:, i, :], ya_hi, ya_lo, i
                    else:
                        dve.wait_ge(rt_ob1, RH)
                        o, hi, lo, k = ob[i // 4][:, i % 4, :], yb_hi, yb_lo, 4 + i
                    dve.wait_ge(gated, e + 1)
                    dve.tensor_tensor(t, t, o, ALU.mult).then_inc(prod_ready, 1)
                    left_over(k, t, hi[:, i, :], lo[:, i, :])
                elif n < N_ZR:
                    i = (n - N_MA) // 2
                    if (n - N_MA) % 2 == 0:
                        scaled(n, bank, t)
                    else:
                        dve.wait_ge(blk_done, n + 1)
                        dve.wait_ge(gated, e + 1)
                        dve.tensor_tensor(merged[:, i, :], t, ps[:, bank, :], ALU.mult).then_inc(lin_read, 1)
                elif n < N_FIN:
                    i = (n - N_MB) // 2
                    if (n - N_MB) % 2 == 0:
                        scaled(n, bank, t)
                    else:
                        dve.wait_ge(blk_done, n + 1)
                        dve.wait_ge(gated, e + 1)
                        dve.tensor_tensor(t, t, ps[:, bank, :], ALU.mult).then_inc(lin_read, 1)
                        dve.wait_ge(lin_read, q + 1)
                        dve.tensor_tensor(t, t, merged[:, i, :], ALU.add).then_inc(prod_ready, 1)
                        left_over(12 + i, t, mg_hi[:, i, :], mg_lo[:, i, :])

            for n in range(N_SECOND, N_END):
                if n == N_SECOND + 3:
                    dve.wait_ge(rstd_ready, V_LAST + 1)
                    epilogue(N_SECOND)
                    epilogue(N_SECOND + 1)
                if n == N_RET + 1:
                    dve.wait_ge(gate_mm, 1)
                    dve.tensor_copy(gate_n[:], ps[:, 6, 0:24 * TB].rearrange("p (b c) -> p b c", b=TB))\
                        .then_inc(gate_ready, 1)
                    ns_normalise(0)
                if n >= N_SECOND + 3:
                    epilogue(n - 1)
                if NS_FIRST < n <= NS_FIRST + NS:
                    ns_evac(n - 1 - NS_FIRST)
                if N_SECOND < n < N_END - 1:
                    split(n + 1, width(n + 1))
                if NS_FIRST <= n < NS_FIRST + NS:
                    ns_maxima(n - NS_FIRST)
                if n == N_SECOND + 1:
                    dve.wait_ge(norm_sum, V_PRE + 1)
                    variance(V_LAST, EPS_A)
                if n == N_SECOND + 2:
                    dve.wait_ge(norm_sum, V_PRE + 1)
                    dve.wait_ge(norm_pow, V_LAST + 1)
                    dve.tensor_tensor(rs3[:], rs[:], rs[:], ALU.mult).then_inc(pre_step, 1)
                    dve.wait_ge(pre_step, 1)
                    dve.tensor_tensor(rs3[:], rs3[:], ps[:, stat_bank, TB:2 * TB], ALU.mult)\
                        .then_inc(pre_step, 1)
                    dve.wait_ge(pre_step, 2)
                    dve.tensor_scalar(var[:], rs3[:], 1.0 / D, EPS_B, ALU.mult, ALU.add).then_inc(norm_var, 1)
                    dve.wait_ge(norm_pow, V_PRE + 1)
                    dve.tensor_tensor(rs2[:], rs2[:], rs[:], ALU.mult).then_inc(pre_step, 1)
                    dve.wait_ge(pre_step, 3)
                    diagonal(V_LAST, rs=rs2)
                if n == N_SECOND + 3:
                    dve.wait_ge(norm_spread, V_LAST + 1)
                    diagonal(V_PRE)
                for m in handled(n):
                    (rotate if m in ROPE else turn)(m)
                if N_SECOND + 4 <= n < N_SECOND + 12:
                    k = n - N_SECOND - 4
                    dve.wait_ge(rstd_ready, V_PRE + 1)
                    dve.scalar_tensor_tensor(x[:, k, :], x[:, k, :], gains[:, G_FINAL, k:k + 1], r1[:],
                                             ALU.mult, ALU.mult).then_inc(x1_ready, 1)
                if n in (N_SECOND + 5, N_SECOND + 6):
                    windows_of(n - N_SECOND - 5)
                if n == N_SECOND + 7:
                    dve.wait_ge(cmp_mm, 1)
                    dve.tensor_copy(kc[:], ps[:, 4, P:P + NCMP]).then_inc(cmp_ready, 1)
                if n == N_SECOND + 9:
                    dve.wait_ge(cmp_mm, 2)
                    dve.tensor_copy(vc[:], ps[0:NCMP, 7, P:2 * P].rearrange("p (g d) -> p g d", g=2))\
                        .then_inc(cmp_ready, 1)
                if NS_FIRST <= n < NS_FIRST + 2:
                    cmp_maxima(n - NS_FIRST)
                if NS_FIRST < n <= NS_FIRST + 2:
                    cmp_normalise(n - 1 - NS_FIRST)
                if NS_FIRST < n < NS_FIRST + NS:
                    ns_normalise(n - NS_FIRST)
                if RT_FIRST <= n < RT_FIRST + RH:
                    ret_mask(n - RT_FIRST)
                if RT_FIRST + 1 <= n < RT_FIRST + 1 + RH:
                    ret_norm(n - RT_FIRST - 1)
                if RT_FIRST + 2 <= n < RT_FIRST + 2 + RH:
                    ret_evac(n - RT_FIRST - 2)
            variance(V_POST, EPS_B)
            diagonal(V_POST)
            dve.wait_ge(rstd_ready, V_POST + 1)
            dve.wait_ge(fin_read, KT)
            dve.wait_ge(x1_ready, KT)
            for k in range(KT):
                dve.tensor_tensor(yg[:, k, :], yg[:, k, :], rstd[:], ALU.mult).then_inc(fin_gain, 1)
                dve.wait_ge(fin_gain, k + 1)
                dve.tensor_tensor(x[:, k, :], x[:, k, :], yg[:, k, :], ALU.add).then_inc(out_part, 1)

        @block.tensor
        def _(pe):
            def strip(n, hi, lo, bank, kt=KT, k0=0, cols=S, slot=None, start=True, stop=True,
                      ready=None, rows=P):
                slot = n % 2 if slot is None else slot
                if isinstance(n, int) and n == 0:
                    pe.wait_ge(first_lo, 1)
                else:
                    pe.wait_ge(w_lo_ready, n + 1)
                o = ps[0:rows, bank, 0:cols]
                for k in range(kt):
                    if isinstance(n, int) and n == 0 and k == kt // 2:
                        pe.wait_ge(w_lo_ready, 1)
                    if ready:
                        pe.wait_ge(ready[0], ready[1] + k + 1)
                    wh = w_hi[:, slot, k * rows:(k + 1) * rows]
                    wl = w_lo[:, slot, k * rows:(k + 1) * rows]
                    pe.matmul(o, wh, hi[:, k0 + k, 0:cols], start=start and k == 0, stop=False)
                    pe.matmul(o, wh, lo[:, k0 + k, 0:cols], start=False, stop=False)
                    ins = pe.matmul(o, wl, hi[:, k0 + k, 0:cols], start=False, stop=stop and k == kt - 1)
                ins.then_inc(blk_done, 1)

            def sums(v, tiles=TB):
                pe.wait_ge(acc_ready, SQUARES * (v + 1))
                for c in range(tiles):
                    ins = pe.matmul(ps[:, stat_bank, c:c + 1], acc[:, c * P:(c + 1) * P], ones[:, 0:1],
                                    start=True, stop=True)
                ins.then_inc(norm_sum, 1)

            def spread(v, tiles=TB):
                pe.wait_ge(norm_diag, v + 1)
                pe.matmul(ps[:, stat_bank, 0:tiles * P], ones[:],
                          diag[:, 0:tiles, :].rearrange("p b t -> p (b t)"),
                          start=True, stop=True).then_inc(norm_spread, 1)

            def mem_scores_of(layer, i):
                u, q, mk = 4 * layer + i, (qm0, qm1)[layer], (mk0, mk1)[layer]
                r, t = HD * (i % 2), i // 2
                if i:
                    pe.wait_ge(mem_exp, 4 * u)
                for b in range(TB):
                    ins = pe.matmul(ps[:, 2 + b // 2, b % 2 * NMEM:(b % 2 + 1) * NMEM],
                                    q[r:r + HD, t, b * P:(b + 1) * P], mk[r:r + HD, t, :],
                                    start=True, stop=True)
                ins.then_inc(mem_scores, 1)

            def mem_turn(layer, i):
                u, pm = 4 * layer + i, (pm0, pm1)[layer]
                pe.wait_ge(mem_probs, u + 1)
                for c in range(2):
                    for b in range(TB):
                        ins = pe.transpose(ps[:, 4 + c, b * P:(b + 1) * P],
                                           pm[:, u % 2, b, c * P:(c + 1) * P], ident[:])
                    ins.then_inc(mem_turned, 1)

            def mem_values(layer, i):
                u, pT, mv = 4 * layer + i, (pmT0, pmT1)[layer], (mv0, mv1)[layer]
                r, t = HD * (i % 2), i // 2
                pe.wait_ge(mem_pT0, u + 1)
                pe.wait_ge(mem_pT1, u + 1)
                for c in range(2):
                    ins = pe.matmul(ps[r:r + HD, 6 + t, :], mv[:, c, t * P + r:t * P + r + HD],
                                    pT[:, c, :], start=(c == 0), stop=(c == 1))
                ins.then_inc(mem_pv, 1)

            def mem_step(layer, n):
                if n - 2 in MEM_STEPS[layer]:
                    mem_values(layer, MEM_STEPS[layer][n - 2])
                if n - 1 in MEM_STEPS[layer]:
                    mem_turn(layer, MEM_STEPS[layer][n - 1])
                if n in MEM_STEPS[layer]:
                    mem_scores_of(layer, MEM_STEPS[layer][n])

            pe.wait_ge(ones_ready, 1)
            pe.wait_ge(half_ready, 1)
            for n in range(N_QM0, N_OUT0):
                if n == 1:
                    pe.wait_ge(small_in, 16 * 4)
                    pe.matmul(ps[0:12, 6, 0:NREL], rb[:], onehot[:], start=True, stop=True)\
                        .then_inc(table_mm, 1)
                if n == 3:
                    sums(V_MIX0)
                if n == 4:
                    spread(V_MIX0)
                if n == 6:
                    pe.wait_ge(rstd_ready, 1)
                    sums(V_MEM, 2)
                if n == 7:
                    spread(V_MEM, 2)
                if N_MEMKV + 6 <= n <= N_MEMKV + 9:
                    t = n - N_MEMKV - 6
                    pe.wait_ge(lin_read, n - 1)
                    if t:
                        pe.wait_ge(mv_ready, t)
                    else:
                        pe.wait_ge(table_ready, 1)
                    for m in range(2):
                        ins = pe.transpose(ps[:, 6, m * P:(m + 1) * P], mvt[:, m * P:(m + 1) * P], ident[:])
                    ins.then_inc(mv_turned, 1)
                if n == N_CONV + 1:
                    pe.wait_ge(lin_read, N_CONV)
                if n == N_CONV + 2:
                    pe.wait_ge(mv_ready, 4)
                mem_step(0, n)
                last = [m for m in range(n) if bank_of(m) == bank_of(n)]
                if last:
                    pe.wait_ge(lin_read, last[-1] + 1)
                if N_MEMKV <= n < N_CONV:
                    if n == N_MEMKV:
                        strip(n, mem_hi, mem_lo, bank_of(n), cols=NMEM, ready=(mem_lo_ready, 0))
                    else:
                        strip(n, mem_hi, mem_lo, bank_of(n), cols=NMEM)
                else:
                    strip(n, a_hi, a_lo, bank_of(n), ready=(a_lo_ready, 0) if n == 0 else None)

            def out_phase(n0):
                for m in range(KT):
                    n = n0 + m
                    pe.wait_ge(lin_read, out_index(n) - (1 if m else 0))
                    strip(n, y_hi, y_lo, n % 2)

            def ffn(n0, v, q0, count):
                def body(i, first=False):
                    for j in range(4):
                        n = i * 4 + (n0 + j)
                        if first and j == 1:
                            sums(v)
                        if first and j == 2:
                            spread(v)
                        if not first:
                            pe.wait_ge(lin_read, i * 4 + (q0 + j - 3))
                        strip(n, a_hi, a_lo, j, slot=j % 2,
                              ready=(a_lo_ready, count) if first and j == 0 else None)
                body(0, first=True)
                with pe.Fori(1, FT // 2, 1) as i:
                    body(i)

            def down(layer, n0, q0):
                with pe.Fori(0, KT // 2, 1) as i:
                    for j in range(2):
                        n = i * 4 + (n0 + 2 * j)
                        pe.wait_ge(lin_read, i * 2 + (q0 + j - 1))
                        pe.wait_ge(g_lo_ready, FT * layer + HALF)
                        strip(n, g_hi, g_lo, j, kt=HALF, slot=0, stop=False)
                        pe.wait_ge(g_lo_ready, FT * (layer + 1))
                        strip(n + 1, g_hi, g_lo, j, kt=HALF, k0=HALF, slot=1, start=False)

            pe.wait_ge(yc_lo_ready, CT)
            pe.wait_ge(ym_lo_ready, 2)
            out_phase(N_OUT0)
            ffn(N_FFN0, V_FFN0, out_index(N_FFN0), KT)
            down(0, N_DOWN0, out_index(N_DOWN0))

            def sw_scores_of(u):
                hp, b, s, keys, k0 = sw_unit(u)
                r = HD * s
                if u >= 2:
                    pe.wait_ge(sw_biased, u - 1)
                elif u:
                    pe.wait_ge(mem_pT0, 8)
                    pe.wait_ge(mem_pT1, 8)
                else:
                    pe.wait_ge(mem_exp, 32)
                for g in range(GROUP):
                    ins = pe.matmul(ps[:, 2 + 2 * (u % 2) + g // 2, g % 2 * 256:g % 2 * 256 + keys],
                                    qT[r:r + HD, GROUP * hp + g, b * P:(b + 1) * P],
                                    kT[r:r + HD, hp, k0:k0 + keys], start=True, stop=True)
                ins.then_inc(sw_scores, 1)

            def sw_turn(u):
                hp, b, s, keys, k0 = sw_unit(u)
                pe.wait_ge(sw_probs, u + 1)
                if u:
                    pe.wait_ge(sw_pT, u)
                else:
                    pe.wait_ge(ym_lo_ready, 4)
                for c in range(keys // P):
                    for g in range(GROUP):
                        ins = pe.transpose(ps[:, 6 + c, g * P:(g + 1) * P],
                                           p_sw[:, u % 2, g, 1 + c * P:1 + (c + 1) * P], ident[:])
                        if g == GROUP - 1 or (keys == P and g == GROUP - 2):
                            ins.then_inc(sw_turned, 1)

            def sw_values(u):
                hp, b, s, keys, k0 = sw_unit(u)
                r, h = HD * s, 2 * hp + s
                pe.wait_ge(sw_pT, u + 1)
                if s == 0 and u >= 4:
                    pe.wait_ge(ys_lo_ready, u // 2 - 1)
                elif s == 0 and u:
                    pe.wait_ge(lin_read, out_index(N_OUT1 - 1) + 1)
                for c in range(keys // P):
                    ins = pe.matmul(ps[r:r + HD, sw_bank(u), 0:GROUP * P],
                                    vn[:, k0 // P + c, h * HD:(h + 1) * HD], pT_sw[:, c, :],
                                    start=(c == 0), stop=(c == keys // P - 1))
                ins.then_inc(sw_pv, 1)

            def sw_step(v):
                if 3 <= v < NSW + 3:
                    sw_turn(v - 3)
                if v < NSW:
                    sw_scores_of(v)
                if 3 <= v < NSW + 3:
                    sw_values(v - 3)

            for n in range(N_KV, N_OUT1):
                if n == N_KV + 1:
                    sums(V_MIX1)
                if n == N_KV + 2:
                    spread(V_MIX1)
                if n in (N_KV + 3, N_KV + 4):
                    pe.wait_ge(band_in, 16 * 2)
                    for c in range(3 * (n - N_KV - 3), 3 * (n - N_KV - 3) + 3):
                        if c >= 3:
                            pe.wait_ge(bias_ready, c - 2)
                        pe.matmul(ps[:, 4 + c % 3, :], flip[:], band[:, c * S:(c + 1) * S],
                                  start=True, stop=True).then_inc(flip_mm, 1)
                if n in (N_KV + 4, N_KV + 5):
                    t = n - N_KV - 4
                    pe.wait_ge(lin_read, out_index(N_KV + 2 + t) + 1)
                    pe.wait_ge(vn_ready, t) if t else pe.wait_ge(rstd_ready, V_MIX1 + 1)
                    for b in range(TB):
                        ins = pe.transpose(ps[:, 7, b * P:(b + 1) * P], vT[:, b * P:(b + 1) * P], ident[:])
                    ins.then_inc(v_turned, 1)
                if n == N_Q:
                    pe.wait_ge(lin_read, out_index(N_Q))
                if n == N_Q + 1:
                    pe.wait_ge(vn_ready, 2)
                    pe.wait_ge(bias_ready, 6)
                mem_step(1, n)
                if n >= SW_FIRST:
                    sw_step(n - SW_FIRST)
                last = [m for m in range(N_KV, n) if bank_of(m) == bank_of(n)]
                if last:
                    pe.wait_ge(lin_read, out_index(last[-1]) + 1)
                kv = n < N_QM1
                strip(n, kv_hi if kv else a_hi, kv_lo if kv else a_lo, bank_of(n),
                      ready=(kv_lo_ready, 0) if n == N_KV else None)
            for v in range(N_OUT1 - SW_FIRST, NSW + 3):
                sw_step(v)
            pe.wait_ge(ym_lo_ready, 4)
            pe.wait_ge(ys_lo_ready, NSW // 2)
            out_phase(N_OUT1)
            ffn(N_FFN1, V_FFN1, out_index(N_FFN1), 3 * KT)
            down(1, N_DOWN1, out_index(N_DOWN1))

            def exchange(n):
                i = turned_before(n)[0]
                pe.wait_ge(lin_read, out_index(n) + 1)
                pe.matmul(ps[:, turn_bank(n), :], perm[:, ROPE[n][0], :], strip_of(n), start=True, stop=True)\
                    .then_inc(rope_mm, 1)

            def turn(n):
                pe.wait_ge(lin_read, out_index(n) + 1)
                for b in range(TB):
                    ins = pe.transpose(ps[:, turn_bank(n), b * P:(b + 1) * P],
                                       strip_of(n)[:, b * P:(b + 1) * P], ident[:])
                ins.then_inc(turn_mm, 1)

            def bank_read(n):
                if n in ROPE:
                    pe.wait_ge(rope_ready, read_of(n)[0])
                else:
                    pe.wait_ge(turn_ready, read_of(n)[1])

            def swap(i):
                if i:
                    pe.wait_ge(rstd_ready, V_PRE + 1)
                    pe.wait_ge(lin_read, out_index(N_SECOND + 1) + 1)
                else:
                    pe.wait_ge(rope_ready, 1)
                pe.matmul(ps[:, (4, 7)[i], :], perm[:, 1, :], (kcr, vcr)[i][:], start=True, stop=True)\
                    .then_inc(swap_mm, 1)

            def hidden(i):
                pe.wait_ge((w1k_in, w1v_in)[i], 16)
                pe.wait_ge(windows_ready, 8 * (i + 1))
                for m in range(2):
                    for l in range(CLEN // 2):
                        ins = pe.matmul(ps[:, (4, 7)[i], m * 2 * NCMP:(m + 1) * 2 * NCMP],
                                        w1[:, i, l, m * P:(m + 1) * P], windows[i][:, l, :],
                                        start=(l == 0), stop=(l == CLEN // 2 - 1))
                ins.then_inc(cmp_hidden, 1)

            def compressed(i):
                pe.wait_ge(cmp_gelu, i + 1)
                for g in range(2):
                    for m in range(2):
                        inner = hid[:, m, g * NCMP:(g + 1) * NCMP]
                        if i == 0:
                            o = ps[HD * g:HD * g + HD, 4, P:P + NCMP]
                            ins = pe.matmul(o, w2[:, 0, m, :], inner, start=(m == 0), stop=(m == 1))
                        else:
                            o = ps[0:NCMP, 7, P + g * HD:P + (g + 1) * HD]
                            ins = pe.matmul(o, inner, w2[:, 1, m, :], start=(m == 0), stop=(m == 1))
                ins.then_inc(cmp_mm, 1)

            def cmp_scores(g):
                if g == 0:
                    pe.wait_ge(cmp_ready, 1)
                else:
                    pe.wait_ge(cm_step, 3)
                pe.matmul(ps[:, 7, 0:16 * NCMP], ident_b, mask_c, start=True, stop=False)
                for k in range(16):
                    b, j = k // GH, k % GH
                    ins = pe.matmul(ps[:, 7, k * NCMP:(k + 1) * NCMP],
                                    qn[HD * g:HD * g + HD, j, b * P:(b + 1) * P], kc[HD * g:HD * g + HD, :],
                                    start=False, stop=(k == 15))
                ins.then_inc(cm_scores, 1)

            def ns_scores_of(u):
                b, g, br, keys = ns_unit(u)
                r = slice(HD * g, HD * g + HD)
                if u:
                    pe.wait_ge(ns_exp, GH * u)
                for j in range(GH):
                    pe.matmul(ps[:, 2 + j, 0:keys], qn[r, j, b * P:(b + 1) * P], (ks, kw)[br][r, 0:keys],
                              start=True, stop=False)
                    ins = pe.matmul(ps[:, 2 + j, b * P:keys], ident_b, causal, start=False, stop=True)
                ins.then_inc(ns_scores, 1)

            def ns_turn(u, js):
                b, g, br, keys = ns_unit(u)
                pe.wait_ge(ns_probs, u + 1)
                for j in js:
                    if j >= 2:
                        pe.wait_ge((ns_pTd, ns_pTa)[j % 2], 2 * u + 1)
                    for c in range(b + 1):
                        ins = pe.transpose(ps[:, 6 + j % 2, c * P:(c + 1) * P],
                                           p_n[:, u % 2, j, c * P:(c + 1) * P], ident[:])
                    ins.then_inc(ns_turned, 1)

            def cmp_turn(u):
                b, g, br, keys = ns_unit(u)
                pe.wait_ge(ns_pTd, 2 * u + 2)
                pe.wait_ge(cm_probs, 5 * (g + 1))
                for j in range(GH):
                    ins = pe.transpose(ps[0:NCMP, 6, j * P:(j + 1) * P], p_c[:, g, b * GH + j, :], ident[:])
                ins.then_inc(cm_turned, 1)

            def ns_values(u):
                b, g, br, keys = ns_unit(u)
                pe.wait_ge(ns_pTd, 2 * u + 2)
                pe.wait_ge(ns_pTa, 2 * u + 2)
                if g == 0 and br == 0:
                    pe.wait_ge(oa_ready, b) if b else pe.wait_ge(cmp_ready, 2)
                o = ps[HD * g:HD * g + HD, 1, :]
                for c in range(b + 1):
                    ins = pe.matmul(o, (vs, vw)[br][:, c, g * HD:(g + 1) * HD], pT_n[:, c, :],
                                    start=(br == 0 and c == 0), stop=False)
                if br:
                    pe.wait_ge(cm_pT, u // 2 + 1)
                    ins = pe.matmul(o, vc[:, g, :], pT_c[:], start=False, stop=True)
                ins.then_inc(ns_pv, 1)

            def ret_scores(h):
                if h:
                    pe.wait_ge(rt_att, TB * h)
                for jc, (bank, c) in enumerate(((2, 0), (3, 0), (4, 0), (3, 3 * P))):
                    ins = pe.matmul(ps[:, bank, c:c + S - jc * P], kr[:, h, jc * P:(jc + 1) * P],
                                    qr[:, h, jc * P:S], start=True, stop=True)
                ins.then_inc(rt_scores, 1)

            def ret_values(h):
                pe.wait_ge(rt_att, TB * h + TB)
                if h:
                    pe.wait_ge(rt_norm, TB * h)
                for ic in range(TB):
                    for jc in range(ic + 1):
                        ins = pe.matmul(ps[:, (1, 5)[ic // 2], ic % 2 * RDV:(ic % 2 + 1) * RDV],
                                        att[:, jc, (ic - jc) * P:(ic - jc + 1) * P],
                                        vr[:, jc, h * RDV:(h + 1) * RDV], start=(jc == 0), stop=(jc == ic))
                ins.then_inc(rt_out, 1)

            def ret_turn(h):
                pe.wait_ge(rt_norm, TB * h + TB)
                if h:
                    pe.wait_ge(rt_ob0, h)
                    pe.wait_ge(rt_ob1, h)
                for f in range(2):
                    for ic in range(TB):
                        ins = pe.transpose(ps[:, 6 + f, ic * P:(ic + 1) * P], on[:, ic, f * P:(f + 1) * P],
                                           ident[:])
                    ins.then_inc(rt_turned, 1)

            for n in range(N_SECOND, N_END):
                if n == N_SECOND + 1:
                    sums(V_LAST)
                    pe.wait_ge(acc2_ready, 1 + KT)
                    for c in range(TB):
                        ins = pe.matmul(ps[:, stat_bank, TB + c:TB + c + 1], acc2[:, c * P:(c + 1) * P],
                                        ones[:, 0:1], start=True, stop=True)
                    ins.then_inc(norm_sum, 1)
                if n == N_SECOND + 3:
                    spread(V_LAST)
                if n == N_SECOND + 4:
                    pe.wait_ge(rstd_ready, V_LAST + 1)
                    spread(V_PRE)
                    pe.wait_ge(small2_in, 16 * 5)
                if NS_FIRST + 2 <= n <= NS_FIRST + NS:
                    ns_values(n - 2 - NS_FIRST)
                if n == N_RET + 1:
                    pe.wait_ge(gate_sig, 1)
                    bank_read(N_SECOND + 9)
                    for b in range(TB):
                        ins = pe.transpose(ps[:, 6, 24 * b:24 * b + 24], tmp[0:24, 2, b * P:(b + 1) * P],
                                           ident[0:24, 0:24])
                    ins.then_inc(gate_mm, 1)
                if NS_FIRST < n <= NS_FIRST + NS:
                    u = n - 1 - NS_FIRST
                    if u == 0:
                        pe.wait_ge(gate_ready, 1)
                        pe.wait_ge(cm_step, 3)
                        ns_scores_of(1)
                        ns_turn(0, (0, 1))
                    else:
                        if u == 1:
                            pe.wait_ge(cm_step, 6)
                        if ns_unit(u - 1)[2]:
                            pe.wait_ge(cm_pT, u // 2)
                        for m in handled(n - 1):
                            bank_read(m)
                        ns_turn(u, (0, 1))
                        if u < NS - 1:
                            ns_scores_of(u + 1)
                    ns_turn(u, (2, 3))
                    if ns_unit(u)[2]:
                        cmp_turn(u)
                    pe.wait_ge(ns_pTa, 2 * u + 2)
                if n == NS_FIRST + NS:
                    ns_values(NS - 1)
                if n == NS_FIRST:
                    pe.wait_ge(lin_read, out_index(N_GATE) + 1)
                    pe.wait_ge(cmp_ready, 2)
                    bank_read(N_SECOND + 8)
                    ns_scores_of(0)
                if NS_FIRST <= n < NS_FIRST + 2:
                    cmp_scores(n - NS_FIRST)
                for m in handled(n):
                    if turned_before(m) != (0, 0):
                        order = [k for t in range(N_SECOND, N_END) for k in handled(t)]
                        same = [k for k in order[:order.index(m)] if turn_bank(k) == turn_bank(m)]
                        if same:
                            bank_read(same[-1])
                    (exchange if m in ROPE else turn)(m)
                if n == N_SECOND + 5:
                    swap(0)
                    swap(1)
                if n == N_SECOND + 6:
                    hidden(0)
                if n == N_SECOND + 7:
                    compressed(0)
                if n == N_SECOND + 8:
                    hidden(1)
                if n == N_SECOND + 9:
                    compressed(1)
                if n == RT_FIRST:
                    pe.wait_ge(ns_exp, GH * NS)
                    pe.wait_ge(oa_ready, TB)
                    bank_read(N_ZN - 1)
                if RT_FIRST + 2 <= n < RT_FIRST + 2 + RH:
                    ret_turn(n - RT_FIRST - 2)
                if RT_FIRST + 1 <= n < RT_FIRST + 1 + RH:
                    ret_values(n - RT_FIRST - 1)
                if RT_FIRST <= n < RT_FIRST + RH:
                    ret_scores(n - RT_FIRST)
                last = [m for m in range(N_SECOND, n) if bank_of(m) == bank_of(n)]
                if n >= N_FIN + 2:
                    pe.wait_ge(fin_read, n - N_FIN - 1)
                elif last:
                    pe.wait_ge(lin_read, out_index(last[-1]) + 1)
                if n == N_MA + 1:
                    pe.wait_ge(zl_ready, GH)
                if n == N_MB + 1:
                    pe.wait_ge(zl_ready, GH + KT)
                if n == N_FIN:
                    strip(n, mg_hi, mg_lo, bank_of(n), ready=(zl_ready, GH + KT))
                elif n > N_FIN:
                    strip(n, mg_hi, mg_lo, bank_of(n))
                elif N_MA <= n < N_ZR and (n - N_MA) % 2:
                    strip(n, ya_hi, ya_lo, bank_of(n), kt=GH)
                elif n >= N_MB and (n - N_MB) % 2:
                    strip(n, yb_hi, yb_lo, bank_of(n))
                else:
                    strip(n, a_hi, a_lo, bank_of(n), ready=(a_lo_ready, 4 * KT) if n == N_SECOND else None,
                          rows=24 if n == N_GATE else P)
            sums(V_POST - 1)
            spread(V_POST)


def strips(w):
    k, n = w.shape
    return w.reshape(k // P, P, n // P, P).transpose(2, 1, 0, 3).reshape(n // P, P, -1)


LOW = [0, 1, 2, 6, 7, 8]
HIGH = [3, 4, 5, 9, 10, 11]


def head_order():
    return np.concatenate([np.arange(h * HD, (h + 1) * HD) for p in zip(LOW, HIGH) for h in p])


def relative_onehot():
    exact, count, far = 16, 32, 128
    dist = np.arange(2 * P - 1, 2 * P - 1 - NREL, -1)
    d = np.maximum(dist, 1).astype(np.float32)
    large = exact + (np.log(d / np.float32(exact)) / np.float32(math.log(far / exact))
                     * np.float32(count - exact)).astype(np.int32)
    bucket = np.where(np.maximum(dist, 0) < exact, np.maximum(dist, 0), np.minimum(large, count - 1))
    out = np.zeros((33, NREL), np.float32)
    inside = (dist >= 0) & (dist < P)
    out[bucket[inside], np.nonzero(inside)[0]] = 1.0
    out[32, ~inside] = 1.0
    return out


def exchanges():
    out = np.zeros((P, 2, P), np.float32)
    for d in range(P):
        if d % HD < 16:
            out[d ^ 8, 0, d] = 1.0
        out[d ^ 64, 1, d] = 1.0
    return out


def rotary_tables():
    pos = np.arange(S, dtype=np.float32)
    out = np.zeros((2, P, 2, S), np.float32)
    inv_n = np.float32(1.0) / (np.float32(500000.0) ** (np.arange(0, 16, 2, dtype=np.float32) / np.float32(16)))
    inv_r = np.float32(1.0) / (np.float32(10000.0) ** np.linspace(0.0, 1.0, 64, dtype=np.float32))
    out[0, :, 0, :] = 1.0
    for d in range(P):
        if d % HD < 16:
            ang = (pos * inv_n[d % 8]).astype(np.float32)
            out[0, d, 0], out[0, d, 1] = np.cos(ang), np.sin(ang) * (-1 if d % HD < 8 else 1)
        ang = (pos * inv_r[d % 64]).astype(np.float32)
        out[1, d, 0], out[1, d, 1] = np.cos(ang), np.sin(ang) * (-1 if d < 64 else 1)
    return out


def mask_table():
    q, k = np.arange(P)[:, None], np.arange(P)[None, :]
    causal = np.where(k <= q, 0.0, MASKED)
    t = np.arange(TB)[None, :, None, None] * P + np.arange(P)[:, None, None, None]
    end = np.arange(NCMP)[None, None, None, :] * CSTRIDE + CLEN - 1
    cmp = np.where(end <= t, 0.0, MASKED) + np.zeros((P, TB, GH, NCMP))
    return np.concatenate([np.eye(P), causal, cmp.reshape(P, -1)], 1).astype(mybir.dt.np(BF16))


def decays():
    log_g = np.log(np.float32(1.0) - np.float32(2.0) ** (np.float32(-5.0) - np.arange(RH, dtype=np.float32)))
    diff = (np.arange(S)[None, :] - np.arange(P)[:, None]).astype(np.float32)
    out = np.exp(np.maximum(diff, 0)[:, None, :] * log_g[None, :, None]) * (diff >= 0)[:, None, :]
    return out.astype(np.float32)


def feature_major(v):
    return v.T.reshape(v.shape[1] // P, P, -1).transpose(1, 0, 2)


def kernel(**inputs):
    from concourse import bacc
    from concourse.bass_utils import run_bass_kernel_spmd

    w = {k: np.asarray(v) for k, v in inputs.items()}
    nc = bacc.Bacc("TRN2", target_bir_lowering=False, num_devices=1)
    order = head_order()
    a_in = strips(w["a_w_in"][0])
    triple = [a_in[[i, 12 + i, 6 + i]] for i in range(CT)]
    mkv = [strips(w["w_mem_kv"][i]) for i in range(2)]
    b_in = strips(w["b_w_q"][0][:, np.concatenate([order, np.arange(768, 1024)])])
    b_out = strips(w["b_w_out"][0][np.concatenate([order, np.arange(768, 1024)])])

    def pairs(i):
        return np.stack([strips(w["w_gate"][i]), strips(w["w_up"][i])], 1).reshape(2 * FT, P, D)

    w2_in = w["w_in_2"]
    cuts = np.cumsum([512, 128, 128, 128, 128, 128, 128, 24, 512, 512, 512, 1024, 1024, 1024, 1024])[:-1]
    q_n, k_c, v_c, k_s, v_s, k_w, v_w, g_n, z_n, q_r, k_r, v_r, z_r, m_a, m_b = np.split(w2_in, cuts, axis=1)
    pairs_n = np.concatenate([np.arange(h * HD, (h + 1) * HD) for t in range(GH) for h in (t, GH + t)])
    q_r, k_r, v_r = strips(q_r), strips(k_r), strips(v_r)
    ret = np.concatenate([np.stack([q_r[h], k_r[h], v_r[2 * h], v_r[2 * h + 1]]) for h in range(RH)])
    mb_ret = np.stack([strips(m_b), strips(w["w_ret_o_2"])], 1).reshape(2 * KT, P, D)

    def cmp_first(v):
        return v.reshape(CLEN // 2, 2, HD, 256).transpose(1, 2, 0, 3).reshape(P, CLEN // 2, 256)

    def cmp_places(v):
        return v.reshape(CLEN // 2, 2, HD).transpose(1, 2, 0).reshape(P, CLEN // 2)

    arrays = {
        "w8b": np.concatenate([strips(k_c), strips(v_c), strips(v_s), strips(v_w), strips(q_n[:, pairs_n]),
                               strips(k_s), strips(k_w), ret, strips(z_n[:, pairs_n]), strips(m_a),
                               strips(z_r), mb_ret, strips(w["w_out_2"])]),
        "w_gates": g_n.reshape(KT, P, 24).transpose(1, 0, 2).reshape(P, KT * 24),
        "w_nsa_o": strips(w["w_nsa_o_2"][pairs_n]),
        "cmp_w1": np.stack([cmp_first(w["cmp_w1_k_2"]), cmp_first(w["cmp_w1_v_2"])]),
        "cmp_w2": np.stack([w["cmp_w2_k_2"].reshape(2, P, HD), w["cmp_w2_v_2"].reshape(2, P, HD)])
                    .transpose(2, 0, 1, 3),
        "cmp_pe": np.stack([cmp_places(w["cmp_pe_k_2"]), cmp_places(w["cmp_pe_v_2"])], 1),
        "gate_b": w["b_nsa_gate_2"].reshape(24, 1),
        "perm": exchanges(),
        "masks": mask_table(),
        "rope": rotary_tables(),
        "decay": decays(),
        "w8": np.concatenate([a_in[18:20], triple[0], mkv[0][:2], mkv[1][:2], mkv[0][2:], mkv[1][2:],
                              *triple[1:], strips(w["a_w_out"][0]), pairs(0), strips(w["w_kv"]),
                              b_in[6:8], b_in[:6], b_out, pairs(1)]),
        "w_down": np.concatenate([strips(w["w_down"][i]).reshape(KT, P, 2, SLOT).transpose(0, 2, 1, 3)
                                  .reshape(2 * KT, P, SLOT) for i in range(2)]),
        "xT": feature_major(w["x"][0]),
        "memT": feature_major(w["mem"][0]),
        "gains": np.stack([g.reshape(KT, P).T for g in (
            w["mem_norm"], w["norm_mix"][0], w["norm_ffn"][0], w["kv_norm"], w["norm_mix"][1],
            w["norm_ffn"][1], w["final_norm"], w["norm_pre_2"], w["norm_post_2"])], 1),
        "conv_w": w["a_conv_w"][0].reshape(3, CT, P).transpose(2, 1, 0),
        "sinks": w["b_sinks"][0],
        "rel_bias": w["rel_bias"],
        "onehot": relative_onehot(),
        "masked": np.full((1, 12), MASKED, np.float32),
        "ident": np.eye(P, dtype=np.float32),
        "flip": np.eye(P, dtype=np.float32)[::-1],
    }
    arrays = {k: np.ascontiguousarray(v) for k, v in arrays.items()}
    aps = {k: nc.dram_tensor(k, v.shape, mybir.dt.from_np(v.dtype), kind="ExternalInput").ap()
           for k, v in arrays.items()}
    out = nc.dram_tensor("out", (P, KT, S), F32, kind="ExternalOutput").ap()
    build(nc, aps, out)
    r = run_bass_kernel_spmd(nc, [arrays], core_ids=[0])
    y = r.results[0]["out"]
    return np.ascontiguousarray(y.transpose(2, 1, 0).reshape(1, S, D))
```

```python
import math

import concourse.bass as bass
import numpy as np
from concourse import mybir

F32 = mybir.dt.float32
R32 = mybir.dt.float32r
BF16 = mybir.dt.bfloat16
ACT = mybir.ActivationFunctionType
ALU = mybir.AluOpType
AX = mybir.AxisListType

P = 128
S = 512
D = 1024
KT = D // P
NMEM = 256
HD = 64
FF = 2816
FT = FF // P
HALF = FT // 2
TB = S // P
CT = 6
RAW = 4
SLOT = HALF * P
SCALE = HD ** -0.5
EPS_A = 1e-5
EPS_B = 1e-6
MASKED = -1.0e30
GROUP = 3
NREL = 383
(G_MEM, G_MIX0, G_FFN0, G_KV, G_MIX1, G_FFN1, G_FINAL, G_PRE, G_POST) = range(9)

N_QM0 = 0
N_CONV0 = 2
N_MEMKV = 5
N_CONV = 13
N_OUT0 = 28
N_FFN0 = 36
N_DOWN0 = 80
N_QM1 = 96
N_KV = 98
N_Q = 102
N_OUT1 = 108
N_FFN1 = 116
N_DOWN1 = 160
N_SECOND = 176
N_GATE = 186
N_RET = 187
N_ZN = 203
N_MA = 207
N_ZR = 223
N_MB = 231
N_FIN = 247
N_END = 255
B_MA = N_MA - N_SECOND - 1

V_MIX0, V_MEM, V_FFN0, V_MIX1, V_FFN1, V_LAST, V_PRE, V_POST = range(8)
SQUARES = 9


LAST_DVE = 6
NCMP = 31
CLEN = 32
CSTRIDE = 16
GH = 4
RH = 4
RDV = 256
EMPTY = -1.0e29
TINY = float(np.finfo(np.float32).tiny)


def out_index(n):
    return n if n <= N_DOWN0 else n - 8 if n <= N_DOWN1 else n - 16


def build(nc, a, out):
    base = (nc.sbuf_base + 31) // 32 * 32
    top = [base]

    def at(name, shape, dtype, offset):
        return nc.alloc_sbuf_tensor_at(name, shape, dtype, offset=offset)

    def sb(name, shape, dtype=F32):
        size = int(np.prod(shape[1:])) * (2 if dtype == BF16 else 4)
        t = at(name, shape, dtype, top[0])
        top[0] += (size + 31) // 32 * 32
        return t

    x = sb("x", [P, KT, S])
    a_hi = sb("a_hi", [P, KT, S], R32)
    a_lo = sb("a_lo", [P, KT, S], R32)
    raw = sb("raw", [P, RAW, SLOT])
    w_hi = sb("w_hi", [P, 2, SLOT], R32)
    w_lo = sb("w_lo", [P, 2, SLOT], R32)
    tmp_at = top[0]
    tmp = sb("tmp", [P, 4, S])
    rstd = sb("rstd", [P, S])
    diag = sb("diag", [P, TB, P])
    acc = sb("acc", [P, S])
    mk1_at = top[0]
    mk1 = sb("mk1", [P, 2, NMEM])
    mv1 = sb("mv1", [P, 2, NMEM])
    ident = sb("ident", [P, P])
    ones = sb("ones", [P, P])
    gains = sb("gains", [P, 9, KT])
    conv_w = sb("conv_w", [P, CT, 3])
    sinks = sb("sinks", [P, 12])
    half = sb("half", [P, TB])
    acc2 = sb("acc2", [P, S])
    perm = sb("perm", [P, 2, P])
    w2 = sb("w2", [P, 2, 2, HD])
    pe2 = sb("pe2", [P, 2, 2, CLEN // 2])
    masks = sb("masks", [P, 2 * P + TB * GH * NCMP], BF16)
    gate_n = sb("gate_n", [P, TB, 24])
    hid = sb("hid", [P, 2, 2 * NCMP])
    kc = sb("kc", [P, NCMP])
    vc = sb("vc", [NCMP, 2, HD])
    gate_b = sb("gate_b", [24, 1])
    rs2 = sb("rs2", [P, TB])
    rs3 = sb("rs3", [P, TB])
    nm16 = sb("nm16", [P, 16])
    d16 = sb("d16", [P, 16])
    bn6 = sb("bn6", [P, TB, 6])
    bn2 = sb("bn2", [P, 2, TB, 2])
    var = sb("var", [P, TB])
    rs = sb("rs", [P, TB])
    nmx = sb("nmx", [P, 2, TB])
    den = sb("den", [P, 2, TB])
    sq = at("sq", [P, 2, S], F32, tmp_at)
    sq2 = at("sq2", [P, 2, S], F32, tmp_at + 4096)
    g0 = top[0]
    K1 = 1024

    g_hi = at("g_hi", [P, FT, S], R32, g0)
    g_lo = at("g_lo", [P, FT, S], R32, g0 + FT * 2 * K1)
    assert g0 + 2 * FT * 2 * K1 <= nc.sbuf_base + 212800, g0
    y_hi = at("y_hi", [P, KT, S], R32, g0)
    y_lo = at("y_lo", [P, KT, S], R32, g0 + 16 * K1)
    memx = at("memx", [P, KT, NMEM], F32, g0 + 32 * K1)
    mem_hi = at("mem_hi", [P, KT, NMEM], R32, g0 + 40 * K1)
    mem_lo = at("mem_lo", [P, KT, NMEM], R32, g0 + 48 * K1)
    u_s = at("u_s", [P, S], F32, g0 + 56 * K1)
    v_s = at("v_s", [P, S], F32, g0 + 58 * K1)
    y_s = at("y_s", [P, S], F32, g0 + 60 * K1)
    qm0 = at("qm0", [P, 2, S], F32, g0 + 62 * K1)
    pm0 = at("pm0", [P, 2, TB, NMEM], F32, g0 + 66 * K1)
    pmT0 = at("pmT0", [P, 2, S], F32, g0 + 74 * K1)
    mk0 = at("mk0", [P, 2, NMEM], F32, g0 + 78 * K1)
    mv0 = at("mv0", [P, 2, NMEM], F32, g0 + 80 * K1)
    mvt = at("mvt", [P, NMEM], F32, g0 + 82 * K1)
    rmem = at("rmem", [P, NMEM], F32, g0 + 83 * K1)
    table = at("table", [12, NREL], F32, g0 + 84 * K1)
    rb = at("rb", [33, 12], F32, g0 + 86 * K1)
    onehot = at("onehot", [33, NREL], F32, g0 + 86 * K1 + 256)
    kv_hi = at("kv_hi", [P, KT, S], R32, g0)
    kv_lo = at("kv_lo", [P, KT, S], R32, g0 + 16 * K1)
    kT = at("kT", [P, 2, S], F32, g0 + 32 * K1)
    vn = at("vn", [P, TB, NMEM], F32, g0 + 36 * K1)
    vT = at("vT", [P, S], F32, g0 + 40 * K1)
    qT = at("qT", [P, CT, S], F32, g0 + 42 * K1)
    qm1 = at("qm1", [P, 2, S], F32, g0 + 54 * K1)
    pm1 = at("pm1", [P, 2, TB, NMEM], F32, g0 + 58 * K1)
    pmT1 = at("pmT1", [P, 2, S], F32, g0 + 66 * K1)
    s_sw = at("s_sw", [P, 2, GROUP, 257], F32, g0 + 58 * K1)
    p_sw = at("p_sw", [P, 2, GROUP, 257], F32, g0 + 64 * K1 + 256)
    pT_sw = at("pT_sw", [P, 2, GROUP * P], F32, g0 + 70 * K1 + 512)
    bias = at("bias", [P, 12, 256], F32, g0 + 73 * K1 + 512)

    t2 = at("t2", [P, 2, S], F32, mk1_at)
    pT_n = at("pT_n", [P, TB, GH * P], F32, tmp_at)
    qn = at("qn", [P, GH, S], F32, g0)
    ks = at("ks", [P, S], F32, g0 + 8 * K1)
    kw = at("kw", [P, S], F32, g0 + 10 * K1)
    windows = [at(f"windows{i}", [P, CLEN // 2, 2 * NCMP], F32, g0 + (12 + 8 * i) * K1) for i in range(2)]
    p_n = at("p_n", [P, 2, GH, S], F32, g0 + 12 * K1)
    rope_n = at("rope_n", [P, 2, S], F32, g0 + 28 * K1)
    rot_r = at("rot_r", [P, 2, S], F32, g0 + 28 * K1)
    vs = at("vs", [P, TB, P], F32, g0 + 32 * K1)
    vw = at("vw", [P, TB, P], F32, g0 + 34 * K1)
    rope_r = at("rope_r", [P, 2, S], F32, g0 + 36 * K1)
    kcr = at("kcr", [P, S], F32, g0 + 40 * K1)
    vcr = at("vcr", [P, S], F32, g0 + 42 * K1)
    oa = at("oa", [P, GH, S], F32, g0 + 40 * K1)
    p_c = at("p_c", [P, 2, 16, NCMP], F32, g0 + 48 * K1)
    pT_c = at("pT_c", [NCMP, GH * P], F32, g0 + 52 * K1)
    r1 = at("r1", [P, S], F32, g0 + 54 * K1)
    w1 = at("w1", [P, 2, CLEN // 2, 256], F32, g0 + 56 * K1)
    qr = at("qr", [P, RH, S], F32, g0 + 56 * K1)
    kr = at("kr", [P, RH, S], F32, g0 + 64 * K1)
    vr = at("vr", [P, TB, RH * RDV], F32, g0 + 72 * K1)
    ya_hi = at("ya_hi", [P, GH, S], R32, g0)
    ya_lo = at("ya_lo", [P, GH, S], R32, g0 + 8 * K1)
    decay = at("decay", [P, RH, S], F32, g0 + 16 * K1)
    att = at("att", [P, TB, S], F32, g0 + 24 * K1)
    on = at("on", [P, TB, RDV], F32, g0 + 32 * K1)
    ob = [at("ob0", [P, 4, S], F32, g0 + 48 * K1), at("ob1", [P, 4, S], F32, g0 + 40 * K1)]
    merged = at("merged", [P, KT, S], F32, g0 + 16 * K1)
    yb_hi = at("yb_hi", [P, KT, S], R32, g0 + 56 * K1)
    yb_lo = at("yb_lo", [P, KT, S], R32, g0 + 72 * K1)
    mg_hi = at("mg_hi", [P, KT, S], R32, g0)
    mg_lo = at("mg_lo", [P, KT, S], R32, g0 + 32 * K1)
    yg = at("yg", [P, KT, S], F32, g0 + 16 * K1)
    ident_b = masks[:, 0:P]
    causal = masks[:, P:2 * P]
    mask_c = masks[:, 2 * P:]

    ps = nc.alloc_psum_tensor("ps", [P, 8, S], F32)

    def sem(name):
        return nc.alloc_semaphore(name)

    raw_in = [sem(f"raw_in{i}") for i in range(RAW)]
    x_in = [sem(f"x_in{i}") for i in range(4)]
    mem_in = sem("mem_in")
    gains_in = sem("gains_in")
    const_in = sem("const_in")
    first_in = sem("first_in")
    first_hi = sem("first_hi")
    first_lo = sem("first_lo")
    small_in = sem("small_in")
    w_hi_ready = sem("w_hi_ready")
    w_lo_ready = sem("w_lo_ready")
    blk_done = sem("blk_done")
    lin_read = sem("lin_read")
    ones_ready = sem("ones_ready")
    half_ready = sem("half_ready")
    sq_ready = sem("sq_ready")
    acc_ready = sem("acc_ready")
    norm_sum = sem("norm_sum")
    norm_var = sem("norm_var")
    norm_pow = sem("norm_pow")
    norm_diag = sem("norm_diag")
    norm_spread = sem("norm_spread")
    rstd_ready = sem("rstd_ready")
    a_hi_ready = sem("a_hi_ready")
    a_lo_ready = sem("a_lo_ready")
    mem_hi_ready = sem("mem_hi_ready")
    mem_lo_ready = sem("mem_lo_ready")
    conv_step = sem("conv_step")
    yc_hi_ready = sem("yc_hi_ready")
    yc_lo_ready = sem("yc_lo_ready")
    mv_turned = sem("mv_turned")
    mv_ready = sem("mv_ready")
    mem_scores = sem("mem_scores")
    mem_max = sem("mem_max")
    mem_exp = sem("mem_exp")
    mem_rden = sem("mem_rden")
    mem_probs = sem("mem_probs")
    mem_turned = sem("mem_turned")
    mem_pT0 = sem("mem_pT0")
    mem_pT1 = sem("mem_pT1")
    mem_pv = sem("mem_pv")
    ym_hi_ready = sem("ym_hi_ready")
    ym_lo_ready = sem("ym_lo_ready")
    silu_ready = sem("silu_ready")
    gu_ready = sem("gu_ready")
    g_hi_ready = sem("g_hi_ready")
    g_lo_ready = sem("g_lo_ready")
    table_mm = sem("table_mm")
    table_ready = sem("table_ready")
    table_out = sem("table_out")
    bias_in = sem("bias_in")
    kv_hi_ready = sem("kv_hi_ready")
    kv_lo_ready = sem("kv_lo_ready")
    v_turned = sem("v_turned")
    vn_ready = sem("vn_ready")
    sw_scores = sem("sw_scores")
    sw_biased = sem("sw_biased")
    sw_max = sem("sw_max")
    sw_sink = sem("sw_sink")
    sw_exp = sem("sw_exp")
    sw_den = sem("sw_den")
    sw_probs = sem("sw_probs")
    sw_probs_p = sem("sw_probs_p")
    sw_turned = sem("sw_turned")
    sw_pT = sem("sw_pT")
    sw_pv = sem("sw_pv")
    ys_hi_ready = sem("ys_hi_ready")
    ys_lo_ready = sem("ys_lo_ready")
    out_done = sem("out_done")
    sq2_ready = sem("sq2_ready")
    acc2_ready = sem("acc2_ready")
    gain_ready = sem("gain_ready")
    pre_step = sem("pre_step")
    small2_in = sem("small2_in")
    rope_in = sem("rope_in")
    w1k_in = sem("w1k_in")
    w1v_in = sem("w1v_in")
    rope_mm = sem("rope_mm")
    rope_cos = sem("rope_cos")
    rope_sin = sem("rope_sin")
    rope_ready = sem("rope_ready")
    turn_mm = sem("turn_mm")
    turn_ready = sem("turn_ready")
    windows_ready = sem("windows_ready")
    cmp_hidden = sem("cmp_hidden")
    cmp_gelu = sem("cmp_gelu")
    cmp_mm = sem("cmp_mm")
    cmp_ready = sem("cmp_ready")
    x1_ready = sem("x1_ready")
    gate_sig = sem("gate_sig")
    gate_mm = sem("gate_mm")
    gate_ready = sem("gate_ready")
    cm_scores = sem("cm_scores")
    cm_step = sem("cm_step")
    cm_exp = sem("cm_exp")
    cm_probs = sem("cm_probs")
    cm_turned = sem("cm_turned")
    cm_pT = sem("cm_pT")
    ns_scores = sem("ns_scores")
    ns_max = sem("ns_max")
    ns_exp = sem("ns_exp")
    ns_den = sem("ns_den")
    ns_probs_d = sem("ns_probs_d")
    ns_probs_a = sem("ns_probs_a")
    ns_turned = sem("ns_turned")
    ns_pTd = sem("ns_pTd")
    ns_pTa = sem("ns_pTa")
    ns_pv = sem("ns_pv")
    oa_ready = sem("oa_ready")
    decay_in = sem("decay_in")
    rt_scores = sem("rt_scores")
    rt_att = sem("rt_att")
    rt_out = sem("rt_out")
    rt_stats = sem("rt_stats")
    rt_var = sem("rt_var")
    rt_pow = sem("rt_pow")
    rt_norm = sem("rt_norm")
    rt_turned = sem("rt_turned")
    rt_ob0 = sem("rt_ob0")
    rt_ob1 = sem("rt_ob1")
    gated = sem("gated")
    prod_ready = sem("prod_ready")
    zh_ready = sem("zh_ready")
    zl_ready = sem("zl_ready")
    fin_read = sem("fin_read")
    post_sq = sem("post_sq")
    post_sum = sem("post_sum")
    fin_gain = sem("fin_gain")
    out_part = sem("out_part")
    fin_gain2 = sem("fin_gain2")
    out_part2 = sem("out_part2")

    scratch = nc.dram_tensor("rel_scratch", (12, P, NREL), F32, kind="Internal").ap()

    stat_bank = 7

    def sw_unit(u):
        hp, b, s = u // 8, u % 8 // 2, u % 2
        keys = 256 if b else P
        return hp, b, s, keys, (b - 1) * P if b else 0

    NSW = 16

    def sw_bank(u):
        return 1 - u // 2 % 2

    MEM_STEPS = {0: {N_CONV + 1: 0, N_CONV + 4: 1, N_CONV + 7: 2, N_CONV + 10: 3},
                 1: {N_Q - 1: 0, N_Q: 1, N_Q + 1: 2, N_Q + 2: 3}}
    SW_FIRST = N_Q + 3

    NS = 16
    NS_FIRST, RT_FIRST = N_RET, N_ZN + 2

    def ns_unit(u):
        return u // 4, u % 4 // 2, u % 2, (u // 4 + 1) * P

    def short(n):
        return N_MA <= n < N_ZR and (n - N_MA) % 2 == 1

    def width(n):
        return 24 * KT if n == N_GATE else GH * P if N_MA <= n < N_ZR and (n - N_MA) % 2 else KT * P

    ROPE = {N_SECOND: (0, kcr[:]), **{N_SECOND + 4 + t: (0, qn[:, t, :]) for t in range(GH)},
            N_SECOND + 8: (0, ks[:]), N_SECOND + 9: (0, kw[:])}
    for h in range(RH):
        ROPE[N_RET + 4 * h] = (1, qr[:, h, :])
        ROPE[N_RET + 4 * h + 1] = (1, kr[:, h, :])
    TURN = {N_SECOND + 2: vs[:], N_SECOND + 3: vw[:]}
    for f in range(2 * RH):
        TURN[N_RET + 4 * (f // 2) + 2 + f % 2] = vr[:, :, f * P:(f + 1) * P]
    ROPES, TURNS = sorted(ROPE), sorted(TURN)

    def turn_step(n):
        return N_SECOND + 4 if n == N_SECOND else N_SECOND + 5 if n == N_SECOND + 2 else n + 2

    def handled(n):
        return [m for m in ROPES + TURNS if turn_step(m) == n]

    def on_tensor(n):
        return [m for m in handled(n) if m in TURN or ROPE[m][0] == 0]

    def turn_bank(n):
        return 7 if n >= N_RET else 5 + n % 2

    def strip_of(n):
        return tmp[:, n % 4, :] if n < N_RET else t2[:, n % 2, :]

    def turned_before(n):
        order = [m for t in range(N_SECOND, N_END) for m in handled(t)]
        i = order.index(n)
        return sum(m in ROPE for m in order[:i]), sum(m in TURN for m in order[:i])

    def read_of(n):
        r, t = turned_before(n)
        return r + (n in ROPE), t + (n in TURN)

    def gated_index(n):
        if n < N_MA:
            return n - N_ZN
        if n < N_ZR:
            return 4 + (n - N_MA) // 2
        return 12 + n - N_ZR if n < N_MB else 20 + (n - N_MB) // 2

    def out_bank(n):
        return n % 2 if n < N_OUT1 else (1, 4)[n % 2]

    def bank_of(n):
        if n >= N_SECOND:
            if n < N_GATE:
                return n % 4
            return 0 if n < RT_FIRST + 6 else n % 2
        if n < N_CONV:
            return n % 6
        if n in (N_KV, N_KV + 1):
            return 2 + n - N_KV
        return 0 if n == N_OUT1 - 1 else n % 2

    with nc.Block() as block:

        @block.sync
        def _(sp):
            def load(n, slot, src, w):
                sp.wait_ge(w_lo_ready, n - (RAW - 1))
                sp.dma_start(raw[:, slot, 0:w], src).then_inc(raw_in[slot], 16)

            mid = KT * P // 2
            sp.dma_start(raw[:, 0, 0:mid], a["w8"][0][:, 0:mid]).then_inc(first_in, 16)
            for j in (1, 3):
                sp.dma_start(x[:, 2 * j:2 * j + 2, :], a["xT"][:, 2 * j:2 * j + 2, :]).then_inc(x_in[j], 16)
                if j == 1:
                    sp.dma_start(raw[:, 0, mid:KT * P], a["w8"][0][:, mid:KT * P]).then_inc(raw_in[0], 16)
            for n in range(1, RAW):
                sp.dma_start(raw[:, n, 0:KT * P], a["w8"][n]).then_inc(raw_in[n], 16)
            sp.dma_start(ident[:], a["ident"]).then_inc(const_in, 16)
            sp.dma_start(conv_w[:], a["conv_w"]).then_inc(const_in, 16)
            sp.dma_start(memx[:], a["memT"]).then_inc(mem_in, 16)
            sp.dma_start(onehot[:], a["onehot"]).then_inc(small_in, 16)
            sp.dma_start(rb[0:32, :], a["rel_bias"]).then_inc(small_in, 16)
            sp.dma_start(rb[32:33, :], a["masked"]).then_inc(small_in, 16)
            sp.dma_start(sinks[:], a["sinks"].partition_broadcast(P)).then_inc(small_in, 16)
            for dst, src in ((perm, "perm"), (w2, "cmp_w2"), (masks, "masks"), (gate_b, "gate_b")):
                sp.dma_start(dst[:], a[src]).then_inc(small2_in, 16)
            sp.dma_start(pe2[:], a["cmp_pe"]).then_inc(small2_in, 16)
            with sp.Fori(1, N_DOWN0 // RAW, 1) as i:
                for j in range(RAW):
                    load(i * RAW + j, j, a["w8"][i * RAW + j], KT * P)
            with sp.Fori(0, 2 * KT // RAW, 1) as i:
                for j in range(RAW):
                    load(i * RAW + (N_DOWN0 + j), j, a["w_down"][i * RAW + j], SLOT)
            with sp.Fori(0, (N_DOWN1 - N_QM1) // RAW, 1) as i:
                for j in range(RAW):
                    load(i * RAW + (N_QM1 + j), j, a["w8"][i * RAW + (N_DOWN0 + j)], KT * P)
            with sp.Fori(0, 2 * KT // RAW, 1) as i:
                for j in range(RAW):
                    load(i * RAW + (N_DOWN1 + j), j, a["w_down"][i * RAW + (2 * KT + j)], SLOT)

            for n in range(N_SECOND, N_GATE):
                if n == N_SECOND + RAW:
                    sp.wait_ge(lin_read, out_index(N_SECOND))
                    sp.dma_start(w1[:, 0], a["cmp_w1"][0]).then_inc(w1k_in, 16)
                if n == N_SECOND + RAW + 2:
                    sp.dma_start(w1[:, 1], a["cmp_w1"][1]).then_inc(w1v_in, 16)
                load(n, n % RAW, a["w8b"][n - N_SECOND], KT * P)
            load(N_GATE, N_GATE % RAW, a["w_gates"], 24 * KT)
            with sp.Fori(0, (N_MA - N_RET) // RAW, 1) as i:
                for j in range(RAW):
                    load(i * RAW + (N_RET + j), (N_RET + j) % RAW, a["w8b"][i * RAW + (N_GATE - N_SECOND + j)],
                         KT * P)
            with sp.Fori(0, (N_ZR - N_MA) // RAW, 1) as i:
                for j in (0, 2):
                    load(i * RAW + (N_MA + j), (N_MA + j) % RAW, a["w8b"][i * 2 + (B_MA + j // 2)], KT * P)
                    load(i * RAW + (N_MA + j + 1), (N_MA + j + 1) % RAW, a["w_nsa_o"][i * 2 + j // 2], GH * P)
            with sp.Fori(0, (N_END - N_ZR) // RAW, 1) as i:
                for j in range(RAW):
                    load(i * RAW + (N_ZR + j), (N_ZR + j) % RAW, a["w8b"][i * RAW + (B_MA + KT + j)], KT * P)
            for k in (0, 1, LAST_DVE, 2, 3, LAST_DVE + 1, *range(4, LAST_DVE)):
                if k < LAST_DVE:
                    sp.wait_ge(out_part, k + 1)
                else:
                    sp.wait_ge(out_part2, k - LAST_DVE + 1)
                sp.dma_start(out[:, k, :], x[:, k, :]).then_inc(out_done, 16)
            sp.wait_ge(out_done, 16 * KT)

        @block.gpsimd
        def _(pool):
            pool.memset(ones[:], 1.0).then_inc(ones_ready, 1)

            def clear(v):
                if v:
                    pool.wait_ge(norm_sum, v)
                pool.memset(acc[:], 0.0).then_inc(acc_ready, 1)
                pool.wait_ge(acc_ready, SQUARES * v + 1)

            def squares(v, cols=S):
                clear(v)
                for k in range(KT):
                    pool.wait_ge(sq_ready, KT * v + k + 1)
                    pool.wait_ge(acc_ready, SQUARES * v + 1 + k)
                    pool.tensor_tensor(acc[:, 0:cols], acc[:, 0:cols], sq[:, k % 2, 0:cols],
                                       ALU.add).then_inc(acc_ready, 1)

            def power(v, tiles=TB):
                pool.wait_ge(norm_var, v + 1)
                pool.wait_ge(half_ready, 1)
                pool.tensor_tensor(rs[:, 0:tiles], var[:, 0:tiles], half[:, 0:tiles], ALU.pow)\
                    .then_inc(norm_pow, 1)

            squares(V_MIX0)
            power(V_MIX0)
            squares(V_MEM, NMEM)
            power(V_MEM, 2)
            for v in (V_FFN0, V_MIX1):
                squares(v)
                power(v)
            def sw_last_head(u):
                keys = sw_unit(u)[3]
                pool.wait_ge(sw_den, u + 1)
                pool.wait_ge(sw_exp, GROUP * (u + 1))
                pool.tensor_tensor(p_sw[:, u % 2, GROUP - 1, 1:1 + keys], p_sw[:, u % 2, GROUP - 1, 1:1 + keys],
                                   den[:, u % 2, GROUP - 1:GROUP].to_broadcast([P, keys]), ALU.mult)\
                    .then_inc(sw_probs_p, 1)

            pool.wait_ge(small_in, 16 * 4)
            pool.wait_ge(mem_turned, 16)
            for u in range(NSW):
                hp, b, s, _, _ = sw_unit(u)
                h = 2 * hp + s
                if u >= 2:
                    pool.wait_ge(sw_exp, GROUP * (u - 1))
                pool.tensor_copy(s_sw[:, u % 2, :, 0], sinks[:, GROUP * h:GROUP * h + GROUP])\
                    .then_inc(sw_sink, 1)
                if u:
                    sw_last_head(u - 1)
            sw_last_head(NSW - 1)
            squares(V_FFN1)
            power(V_FFN1)
            clear(V_LAST)
            pool.memset(acc2[:], 0.0).then_inc(acc2_ready, 1)
            for k in range(KT):
                pool.wait_ge(sq_ready, KT * V_LAST + k + 1)
                pool.wait_ge(acc_ready, SQUARES * V_LAST + 1 + k)
                pool.tensor_tensor(acc[:], acc[:], sq[:, k % 2, :], ALU.add).then_inc(acc_ready, 1)
                pool.wait_ge(sq2_ready, k + 1)
                pool.wait_ge(acc2_ready, k + 1)
                pool.tensor_tensor(acc2[:], acc2[:], sq2[:, k % 2, :], ALU.add).then_inc(acc2_ready, 1)
            power(V_LAST)
            pool.wait_ge(norm_var, V_PRE + 1)
            pool.tensor_tensor(rs2[:], var[:], half[:], ALU.pow).then_inc(norm_pow, 1)
            for i, n in enumerate(m for t in range(N_SECOND, N_END) for m in handled(t) if m in ROPE):
                kind, dst = ROPE[n]
                pool.wait_ge(rope_in, 16 * 2)
                pool.wait_ge(lin_read, out_index(n) + 1)
                pool.tensor_tensor(dst, strip_of(n), (rope_n, rope_r)[kind][:, 0, :], ALU.mult)\
                    .then_inc(rope_cos, 1)
                pool.wait_ge(rope_sin, i + 1)
                pool.wait_ge(rope_cos, i + 1)
                turned = rot_r[:, i % 2, :] if kind else strip_of(n)
                pool.tensor_tensor(dst, dst, turned, ALU.add).then_inc(rope_ready, 1)
            for h in range(RH):
                pool.wait_ge(rt_var, h + 1)
                pool.tensor_tensor(bn2[:, h % 2, :, 1], bn2[:, h % 2, :, 1], half[:], ALU.pow)\
                    .then_inc(rt_pow, 1)
            power(V_POST)
            pool.wait_ge(rstd_ready, V_POST + 1)
            pool.wait_ge(x1_ready, KT)
            for k in range(LAST_DVE, KT):
                pool.tensor_tensor(yg[:, k, :], yg[:, k, :], rstd[:], ALU.mult).then_inc(fin_gain2, 1)
                pool.wait_ge(fin_gain2, k - LAST_DVE + 1)
                pool.tensor_tensor(x[:, k, :], x[:, k, :], yg[:, k, :], ALU.add).then_inc(out_part2, 1)

        @block.scalar
        def _(act):
            act.dma_start(gains[:], a["gains"]).then_inc(gains_in, 16)
            for j in (0, 2):
                act.dma_start(x[:, 2 * j:2 * j + 2, :], a["xT"][:, 2 * j:2 * j + 2, :])\
                    .then_inc(x_in[j], 16)

            def split(n, w, slot=None, raw_slot=None, count=None):
                slot = n % 2 if slot is None else slot
                raw_slot = n % RAW if raw_slot is None else raw_slot
                act.wait_ge(raw_in[raw_slot], 16 * (n // RAW + 1) if count is None else count)
                if not isinstance(n, int) or n >= 2:
                    act.wait_ge(blk_done, n - 1)
                act.activation(w_hi[:, slot, 0:w], raw[:, raw_slot, 0:w], ACT.Copy)\
                    .then_inc(w_hi_ready, 1)

            def square(v, k, slot, src, cols=S, first=False):
                if v:
                    if first:
                        act.wait_ge(acc_ready, SQUARES * v)
                if not first:
                    act.wait_ge(acc_ready, k + SQUARES * v)
                act.activation(sq[:, slot, 0:cols], src, ACT.Square).then_inc(sq_ready, 1)

            def operand(k, g):
                act.activation(a_hi[:, k, :], x[:, k, :], ACT.Copy, scale=gains[:, g, bass.ds(k, 1)])\
                    .then_inc(a_hi_ready, 1)

            def spread(v, dst, cols=S):
                act.wait_ge(norm_spread, v + 1)
                act.activation(dst, ps[:, stat_bank, 0:cols], ACT.Copy).then_inc(rstd_ready, 1)

            def residual(k, q, v, g, slot, first=False):
                act.wait_ge(lin_read, q + 1)
                square(v, k, slot, x[:, k, :], first=first)
                if v == V_LAST:
                    if not first:
                        act.wait_ge(acc2_ready, k)
                    act.activation(sq2[:, slot, :], x[:, k, :], ACT.Square,
                                   scale=gains[:, G_FINAL, bass.ds(k, 1)]).then_inc(sq2_ready, 1)
                operand(k, g)

            def mem_exps(layer, i):
                u, pm = 4 * layer + i, (pm0, pm1)[layer]
                act.wait_ge(mem_max, u + 1)
                if i >= 2:
                    act.wait_ge(mem_turned, 2 * (u - 1))
                for b in range(TB):
                    act.activation(pm[:, u % 2, b, :], ps[:, 2 + b // 2, b % 2 * NMEM:(b % 2 + 1) * NMEM],
                                   ACT.Exp, bias=nmx[:, u % 2, b:b + 1],
                                   accum_out=den[:, u % 2, b:b + 1]).then_inc(mem_exp, 1)

            def mem_evac(layer, i):
                u, pT = 4 * layer + i, (pmT0, pmT1)[layer]
                act.wait_ge(mem_turned, 2 * u + 2)
                if i:
                    act.wait_ge(mem_pv, u)
                act.activation(pT[:, 1, :], ps[:, 5, :], ACT.Copy).then_inc(mem_pT1, 1)

            def mem_out(layer, t):
                act.wait_ge(mem_pv, 4 * layer + 2 * t + 2)
                act.activation(y_hi[:, CT + t, :], ps[:, 6 + t, :], ACT.Copy).then_inc(ym_hi_ready, 1)

            def mem_step(layer, n):
                if n - 1 in MEM_STEPS[layer]:
                    mem_evac(layer, MEM_STEPS[layer][n - 1])
                if n in MEM_STEPS[layer]:
                    mem_exps(layer, MEM_STEPS[layer][n])
                if n - 2 in MEM_STEPS[layer] and MEM_STEPS[layer][n - 2] % 2:
                    mem_out(layer, MEM_STEPS[layer][n - 2] // 2)

            act.wait_ge(ones_ready, 1)
            act.activation(half[:], ones[:, 0:TB], ACT.Copy, scale=-0.5).then_inc(half_ready, 1)
            mid = KT * P // 2
            act.wait_ge(first_in, 16)
            act.activation(w_hi[:, 0, 0:mid], raw[:, 0, 0:mid], ACT.Copy).then_inc(first_hi, 1)
            act.wait_ge(gains_in, 16)
            for k in range(KT):
                act.wait_ge(x_in[k // 2], 16)
                operand(k, G_MIX0)
                if k == 1:
                    act.wait_ge(raw_in[0], 16)
                    act.activation(w_hi[:, 0, mid:KT * P], raw[:, 0, mid:KT * P], ACT.Copy)\
                        .then_inc(w_hi_ready, 1)
                if k == 5:
                    split(1, KT * P)
            for k in range(KT):
                square(V_MIX0, k, k % 2, x[:, k, :], first=k < 2)
                if k == 3:
                    split(2, KT * P)

            def l0_strip(n):
                if N_CONV0 <= n < N_MEMKV:
                    return "ucb"[n - N_CONV0], 0
                if n >= N_CONV:
                    return "ucb"[(n - N_CONV) % 3], 1 + (n - N_CONV) // 3
                return "q" if n < N_CONV0 else "m", 0

            def conv_out(i):
                act.wait_ge(conv_step, 5 * i + 5)
                act.activation(y_hi[:, i, :], y_s[:], ACT.Copy).then_inc(yc_hi_ready, 1)

            for n in range(N_QM0, N_OUT0 + 1):
                kind, i = l0_strip(n - 1) if n else ("", 0)
                if kind == "b" and i:
                    conv_out(i)
                if n >= 2:
                    split(n + 1, KT * P)
                if kind == "b" and i == 0:
                    conv_out(i)
                if n in (1, 2):
                    act.wait_ge(mem_in, 16)
                    for k in range((n - 1) * KT // 2, n * KT // 2):
                        act.activation(mem_hi[:, k, :], memx[:, k, :], ACT.Copy,
                                       scale=gains[:, G_MEM, k:k + 1]).then_inc(mem_hi_ready, 1)
                if n == 4:
                    act.wait_ge(table_mm, 1)
                    act.activation(table[:], ps[0:12, 6, 0:NREL], ACT.Copy).then_inc(table_ready, 1)
                if n == 4:
                    spread(V_MIX0, rstd[:])
                if n in (4, 5, 6, 7):
                    for k in range(2 * n - 8, 2 * n - 6):
                        square(V_MEM, k, k % 2, memx[:, k, :], NMEM, first=k < 2)
                if n == 9:
                    spread(V_MEM, rmem[:], NMEM)
                mem_step(0, n)
            act.wait_ge(table_ready, 1)
            act.dma_start(scratch, table[:].unsqueeze(1).to_broadcast([12, P, NREL])).then_inc(table_out, 16)

            def out_phase(n0, v, g):
                for n in range(n0 + 1, n0 + KT):
                    residual(n - 1 - n0, out_index(n - 1), v, g, (n - 1 - n0) % 2, first=n - 1 - n0 < 2)
                    split(n + 1, KT * P)
                residual(KT - 1, out_index(n0 + KT - 1), v, g, 1)
                split(n0 + KT + 1, KT * P)

            def ffn(layer, n0, v, q0, r0):
                def body(i, first=False, last=False):
                    for j in range(2):
                        n = i * 4 + (n0 + 2 * j)
                        q = i * 4 + (q0 + 2 * j)
                        p = i * 2 + (FT * layer + j)
                        w = SLOT if last and j else KT * P
                        count = (i + (r0 + 1 + j)) * 16
                        m = i * 2 + j
                        if first and j == 0:
                            split(n + 2, w, 0, 2, count)
                            spread(v, rstd[:])
                        act.wait_ge(lin_read, q + 1)
                        act.activation(tmp[:, 2 * j, :], tmp[:, 2 * j, :], ACT.Silu).then_inc(silu_ready, 1)
                        if not (first and j == 0):
                            split(n + 2, w, 0, (2 * j + 2) % 4, count)
                        act.wait_ge(gu_ready, p + 1)
                        act.activation(g_hi[:, m, :], tmp[:, 2 * j + 1, :], ACT.Copy).then_inc(g_hi_ready, 1)
                        split(n + 3, w, 1, (2 * j + 3) % 4, count)
                body(0, first=True)
                with act.Fori(1, FT // 2 - 1, 1) as i:
                    body(i)
                body(FT // 2 - 1, last=True)

            def down(n0, q0, v, g, r0):
                def body(i, first=False, last=False):
                    for j in range(2):
                        n = i * 4 + (n0 + 2 * j)
                        w = KT * P if last and j else SLOT
                        count = (i + (r0 + 1 + (1 if j else 0))) * 16
                        split(n + 2, w, 0, (2 * j + 2) % 4, count)
                        residual(i * 2 + j, i * 2 + (q0 + j), v, g, j, first=first)
                        split(n + 3, w, 1, (2 * j + 3) % 4, count)
                body(0, first=True)
                with act.Fori(1, KT // 2 - 1, 1) as i:
                    body(i)
                body(KT // 2 - 1, last=True)

            out_phase(N_OUT0, V_FFN0, G_FFN0)
            ffn(0, N_FFN0, V_FFN0, out_index(N_FFN0), N_FFN0 // RAW)
            down(N_DOWN0, N_DOWN0, V_MIX1, G_MIX1, N_DOWN0 // RAW)

            act.wait_ge(lin_read, out_index(N_QM1))
            act.wait_ge(table_out, 16)
            rows = bass.AP(tensor=scratch.tensor, offset=scratch.offset + P - 1,
                           ap=[[NREL - 1, P], [P * NREL, 12], [1, 256]])
            act.dma_start(bias[:], rows).then_inc(bias_in, 16)
            for k in range(KT):
                act.activation(kv_hi[:, k, :], x[:, k, :], ACT.Copy, scale=gains[:, G_KV, k:k + 1])\
                    .then_inc(kv_hi_ready, 1)

            def sw_exps(u):
                keys = sw_unit(u)[3]
                act.wait_ge(sw_max, u + 1)
                if u >= 2:
                    act.wait_ge(sw_turned, 2 * (u - 1))
                else:
                    act.wait_ge(mem_pv, 8)
                for g in range(GROUP):
                    act.activation(p_sw[:, u % 2, g, 0:1 + keys], s_sw[:, u % 2, g, 0:1 + keys], ACT.Exp,
                                   bias=nmx[:, u % 2, g:g + 1], accum_out=den[:, u % 2, g:g + 1])\
                        .then_inc(sw_exp, 1)

            def sw_evac(u):
                act.wait_ge(sw_turned, 2 * u + 2)
                if u:
                    act.wait_ge(sw_pv, u)
                tiles = sw_unit(u)[3] // P
                act.activation(pT_sw[:, 0:tiles, :], ps[:, 6:6 + tiles, 0:GROUP * P], ACT.Copy)\
                    .then_inc(sw_pT, 1)

            def sw_out(u):
                hp, b, s, _, _ = sw_unit(u)
                act.wait_ge(sw_pv, u + 1)
                act.activation(y_hi[:, GROUP * hp:GROUP * hp + GROUP, b * P:(b + 1) * P],
                               ps[:, sw_bank(u), 0:GROUP * P].rearrange("p (g t) -> p g t", g=GROUP),
                               ACT.Copy).then_inc(ys_hi_ready, 1)

            def sw_step(w):
                if 2 <= w < NSW + 2:
                    sw_evac(w - 2)
                if w < NSW:
                    sw_exps(w)
                if 2 <= w < NSW + 2 and w % 2:
                    sw_out(w - 2)

            for n in range(N_QM1, N_OUT1 + 1):
                if n > N_QM1:
                    split(n + 1, KT * P)
                if n == N_QM1 + 2:
                    spread(V_MIX1, rstd[:])
                mem_step(1, n)
                if SW_FIRST <= n < N_OUT1:
                    for w in ((0,), (1,), (2, 3))[n - SW_FIRST]:
                        sw_step(w)
                if n == N_OUT1:
                    for w in range(4, NSW + 3):
                        sw_step(w)
            out_phase(N_OUT1, V_FFN1, G_FFN1)
            ffn(1, N_FFN1, V_FFN1, out_index(N_FFN1), N_FFN1 // RAW)
            act.wait_ge(gain_ready, 1)
            down(N_DOWN1, out_index(N_DOWN1), V_LAST, G_PRE, N_DOWN1 // RAW)

            act.wait_ge(lin_read, out_index(N_SECOND))
            act.dma_start(rope_n[:], a["rope"][0]).then_inc(rope_in, 16)
            act.dma_start(rope_r[:], a["rope"][1]).then_inc(rope_in, 16)

            def ns_exps(u):
                b, g, br, keys = ns_unit(u)
                act.wait_ge(ns_max, u + 1)
                if u >= 2:
                    act.wait_ge(ns_turned, GH * (u - 1))
                for j in range(GH):
                    act.activation(p_n[:, u % 2, j, 0:keys], ps[:, 2 + j, 0:keys], ACT.Exp,
                                   bias=nmx[:, u % 2, j:j + 1], accum_out=den[:, u % 2, j:j + 1])\
                        .then_inc(ns_exp, 1)

            def ns_normalise(u):
                keys = ns_unit(u)[3]
                act.wait_ge(ns_den, 2 * u + 2)
                act.wait_ge(ns_exp, GH * u + GH)
                for j in (2, 3):
                    act.activation(p_n[:, u % 2, j, 0:keys], p_n[:, u % 2, j, 0:keys], ACT.Copy,
                                   scale=den[:, u % 2, j:j + 1]).then_inc(ns_probs_a, 1)

            def ns_evac(u, js):
                b, g, br, keys = ns_unit(u)
                if u:
                    act.wait_ge(ns_pv, u)
                for j in js:
                    act.wait_ge(ns_turned, GH * u + j + 1)
                    act.activation(pT_n[:, 0:b + 1, j * P:(j + 1) * P],
                                   ps[:, 6 + j % 2, 0:keys].rearrange("p (c t) -> p c t", t=P), ACT.Copy)\
                        .then_inc(ns_pTa, 1)

            def ns_out(u):
                b, g, br, keys = ns_unit(u)
                if g and br:
                    act.wait_ge(ns_pv, u + 1)
                    act.activation(oa[:, :, b * P:(b + 1) * P],
                                   ps[:, 1, :].rearrange("p (j t) -> p j t", j=GH), ACT.Copy)\
                        .then_inc(oa_ready, 1)

            def ret_evac(h):
                act.wait_ge(rt_turned, 2 * h + 2)
                act.activation(ob[h // 2][:, h % 2 * 2 + 1, :], ps[:, 7, :], ACT.Copy).then_inc(rt_ob1, 1)

            def gate_strip(n, func):
                e = gated_index(n)
                act.wait_ge(lin_read, out_index(n) + 1)
                act.activation(tmp[:, e % 4, :], tmp[:, e % 4, :], func).then_inc(gated, 1)

            def rounded(i, src, dst):
                act.wait_ge(prod_ready, i + 1)
                act.activation(dst, src, ACT.Copy).then_inc(zh_ready, 1)

            def epilogue(n):
                e = gated_index(n)
                if n < N_ZN:
                    return
                if n < N_MA:
                    gate_strip(n, ACT.Silu)
                    rounded(n - N_ZN, tmp[:, e % 4, :], ya_hi[:, n - N_ZN, :])
                elif n < N_ZR:
                    if (n - N_MA) % 2 == 0:
                        gate_strip(n, ACT.Sigmoid)
                elif n < N_MB:
                    gate_strip(n, ACT.Silu)
                    rounded(4 + n - N_ZR, tmp[:, e % 4, :], yb_hi[:, n - N_ZR, :])
                elif n < N_FIN:
                    i = (n - N_MB) // 2
                    if (n - N_MB) % 2 == 0:
                        gate_strip(n, ACT.Sigmoid)
                    else:
                        rounded(12 + i, tmp[:, e % 4, :], mg_hi[:, i, :])
                else:
                    i = n - N_FIN
                    act.wait_ge(blk_done, n + 1)
                    if i >= 2:
                        act.wait_ge(post_sum, i - 1)
                    act.activation(sq[:, i % 2, :], ps[:, n % 2, :], ACT.Square).then_inc(post_sq, 1)
                    act.activation(yg[:, i, :], ps[:, n % 2, :], ACT.Copy,
                                   scale=gains[:, G_POST, i:i + 1]).then_inc(fin_read, 1)

            for n in range(N_SECOND, N_END):
                if n == NS_FIRST + 1:
                    ns_normalise(0)
                if NS_FIRST < n <= NS_FIRST + NS:
                    ns_evac(n - 1 - NS_FIRST, (1,))
                if NS_FIRST + 2 <= n <= NS_FIRST + NS:
                    ns_out(n - 2 - NS_FIRST)
                if n > N_SECOND:
                    if not short(n):
                        epilogue(n - 1)
                    if n + 1 < N_END:
                        split(n + 1, width(n + 1))
                    if short(n):
                        epilogue(n - 1)
                if NS_FIRST < n <= NS_FIRST + NS:
                    ns_evac(n - 1 - NS_FIRST, (2, 3))
                if n == NS_FIRST + NS:
                    ns_out(NS - 1)
                if n == N_SECOND + 3:
                    spread(V_LAST, rstd[:])
                if n == N_SECOND + 4:
                    spread(V_PRE, r1[:])
                if n in (N_SECOND + 6, N_SECOND + 8):
                    i = (n - N_SECOND - 6) // 2
                    act.wait_ge(cmp_hidden, i + 1)
                    if i:
                        act.wait_ge(cmp_mm, 1)
                    act.activation(hid[:], ps[:, 7 if i else 4, 0:4 * NCMP].rearrange("p (m c) -> p m c", m=2),
                                   ACT.Gelu_apprx_tanh).then_inc(cmp_gelu, 1)
                if n == N_RET:
                    act.wait_ge(small2_in, 16 * 5)
                    act.wait_ge(lin_read, out_index(N_GATE) + 1)
                    act.activation(tmp[0:24, 2, :], tmp[0:24, 2, :], ACT.Sigmoid, bias=gate_b[:])\
                        .then_inc(gate_sig, 1)
                if NS_FIRST <= n < NS_FIRST + NS:
                    ns_exps(n - NS_FIRST)
                if NS_FIRST <= n < NS_FIRST + 2:
                    g = n - NS_FIRST
                    act.wait_ge(cm_step, 3 * g + 3)
                    act.activation(p_c[:, g], p_c[:, g], ACT.Exp).then_inc(cm_exp, 1)
                if NS_FIRST < n < NS_FIRST + NS:
                    ns_normalise(n - NS_FIRST)
                if n == RT_FIRST - 1:
                    act.wait_ge(ns_turned, GH * NS)
                    act.dma_start(decay[:], a["decay"]).then_inc(decay_in, 16)
                if RT_FIRST + 2 <= n < RT_FIRST + 2 + RH:
                    ret_evac(n - RT_FIRST - 2)
            epilogue(N_END - 1)
            spread(V_POST, rstd[:])

        @block.vector
        def _(dve):
            def split(n, w, slot=None, raw_slot=None):
                slot = n % 2 if slot is None else slot
                raw_slot = n % RAW if raw_slot is None else raw_slot
                dve.wait_ge(w_hi_ready, n + 1)
                dve.tensor_tensor(w_lo[:, slot, 0:w], raw[:, raw_slot, 0:w],
                                  w_hi[:, slot, 0:w].bitcast(F32), ALU.subtract).then_inc(w_lo_ready, 1)

            def operand(k, g, count):
                dve.wait_ge(a_hi_ready, count)
                dve.scalar_tensor_tensor(a_lo[:, k, :], x[:, k, :], gains[:, g, bass.ds(k, 1)],
                                         a_hi[:, k, :].bitcast(F32), ALU.mult, ALU.subtract)\
                    .then_inc(a_lo_ready, 1)

            def variance(v, eps, tiles=TB):
                dve.wait_ge(norm_sum, v + 1)
                dve.tensor_scalar(var[:, 0:tiles], ps[:, stat_bank, 0:tiles], 1.0 / D, eps,
                                  ALU.mult, ALU.add).then_inc(norm_var, 1)

            def diagonal(v, tiles=TB, rs=rs):
                dve.wait_ge(norm_pow, v + 1)
                dve.tensor_tensor(diag[:, 0:tiles, :],
                                  ident[:].unsqueeze(1).to_broadcast([P, tiles, P]),
                                  rs[:, 0:tiles].unsqueeze(2).to_broadcast([P, tiles, P]), ALU.mult)\
                    .then_inc(norm_diag, 1)

            def scaled(n, bank, dst, factor=None):
                dve.wait_ge(blk_done, n + 1)
                if factor is None:
                    ins = dve.tensor_tensor(dst, ps[:, bank, :], rstd[:], ALU.mult)
                else:
                    ins = dve.scalar_tensor_tensor(dst, ps[:, bank, :], factor, rstd[:], ALU.mult, ALU.mult)
                ins.then_inc(lin_read, 1)

            def memory_scaled(n, bank, dst):
                dve.wait_ge(blk_done, n + 1)
                dve.tensor_tensor(dst, ps[:, bank, 0:NMEM], rmem[:], ALU.mult).then_inc(lin_read, 1)

            def residual(k, n, bank):
                dve.wait_ge(blk_done, n + 1)
                dve.tensor_tensor(x[:, k, :], x[:, k, :], ps[:, bank, :], ALU.add).then_inc(lin_read, 1)

            def mem_maxima(layer, i):
                u = 4 * layer + i
                dve.wait_ge(mem_scores, u + 1)
                dve.tensor_reduce(nmx[:, u % 2, :], ps[:, 2:4, :].rearrange("p k (b m) -> p (k b) m", b=2),
                                  AX.X, ALU.max, negate=True).then_inc(mem_max, 1)

            def mem_normalise(layer, i):
                u, pm = 4 * layer + i, (pm0, pm1)[layer]
                dve.wait_ge(mem_exp, 4 * u + 4)
                dve.reciprocal(den[:, u % 2, :], den[:, u % 2, :]).then_inc(mem_rden, 1)
                dve.wait_ge(mem_rden, u + 1)
                dve.tensor_tensor(pm[:, u % 2], pm[:, u % 2],
                                  den[:, u % 2, :].unsqueeze(2).to_broadcast([P, TB, NMEM]), ALU.mult)\
                    .then_inc(mem_probs, 1)

            def mem_evac(layer, i):
                u, pT = 4 * layer + i, (pmT0, pmT1)[layer]
                dve.wait_ge(mem_turned, 2 * u + 1)
                if i:
                    dve.wait_ge(mem_pv, u)
                dve.tensor_copy(pT[:, 0, :], ps[:, 4, :]).then_inc(mem_pT0, 1)

            def mem_out(layer, t):
                dve.wait_ge(ym_hi_ready, 2 * layer + t + 1)
                dve.tensor_tensor(y_lo[:, CT + t, :], ps[:, 6 + t, :], y_hi[:, CT + t, :].bitcast(F32),
                                  ALU.subtract).then_inc(ym_lo_ready, 1)

            def mem_step(layer, n):
                if n - 1 in MEM_STEPS[layer]:
                    mem_evac(layer, MEM_STEPS[layer][n - 1])
                if n in MEM_STEPS[layer]:
                    mem_maxima(layer, MEM_STEPS[layer][n])
                if n - 2 in MEM_STEPS[layer] and MEM_STEPS[layer][n - 2] % 2:
                    mem_out(layer, MEM_STEPS[layer][n - 2] // 2)
                if n in MEM_STEPS[layer]:
                    mem_normalise(layer, MEM_STEPS[layer][n])

            mid = KT * P // 2
            dve.wait_ge(first_hi, 1)
            dve.tensor_tensor(w_lo[:, 0, 0:mid], raw[:, 0, 0:mid], w_hi[:, 0, 0:mid].bitcast(F32),
                              ALU.subtract).then_inc(first_lo, 1)
            for k in range(KT):
                operand(k, G_MIX0, k + 1)
                if k == 1:
                    dve.wait_ge(w_hi_ready, 1)
                    dve.tensor_tensor(w_lo[:, 0, mid:KT * P], raw[:, 0, mid:KT * P],
                                      w_hi[:, 0, mid:KT * P].bitcast(F32), ALU.subtract)\
                        .then_inc(w_lo_ready, 1)
                if k == 5:
                    split(1, KT * P)

            def l0_epilogue(n):
                bank = bank_of(n)
                if n < N_CONV0:
                    scaled(n, bank, qm0[:, n, :], SCALE)
                    return
                if N_MEMKV <= n < N_CONV:
                    t = n - N_MEMKV
                    if t < 4:
                        memory_scaled(n, bank, (mk0, mk1)[t // 2][:, t % 2, :])
                    else:
                        t -= 4
                        if t:
                            dve.wait_ge(mv_turned, t)
                        memory_scaled(n, bank, mvt[:])
                    return
                i = 0 if n < N_CONV else 1 + (n - N_CONV) // 3
                what = n - N_CONV0 if n < N_CONV else (n - N_CONV) % 3
                if what == 0:
                    scaled(n, bank, u_s[:])
                elif what == 1:
                    scaled(n, bank, v_s[:])
                    dve.wait_ge(lin_read, n + 1)
                    dve.tensor_tensor(v_s[:], v_s[:], u_s[:], ALU.mult).then_inc(conv_step, 1)
                    dve.wait_ge(conv_step, 5 * i + 1)
                    dve.tensor_scalar(y_s[:], v_s[:], conv_w[:, i, 2:3], None, ALU.mult)\
                        .then_inc(conv_step, 1)
                    for back in (1, 2):
                        dve.wait_ge(conv_step, 5 * i + 1 + back)
                        dve.scalar_tensor_tensor(y_s[:, back:S], v_s[:, 0:S - back],
                                                 conv_w[:, i, 2 - back:3 - back], y_s[:, back:S],
                                                 ALU.mult, ALU.add).then_inc(conv_step, 1)
                else:
                    scaled(n, bank, u_s[:])
                    dve.wait_ge(lin_read, n + 1)
                    dve.tensor_tensor(y_s[:], y_s[:], u_s[:], ALU.mult).then_inc(conv_step, 1)
                    dve.wait_ge(yc_hi_ready, i + 1)
                    dve.tensor_tensor(y_lo[:, i, :], y_s[:], y_hi[:, i, :].bitcast(F32), ALU.subtract)\
                        .then_inc(yc_lo_ready, 1)

            def mv_evac(t):
                dve.wait_ge(mv_turned, t + 1)
                dst = (mv0, mv1)[t // 2][:, :, t % 2 * P:(t % 2 + 1) * P]
                dve.tensor_copy(dst, ps[:, 6, 0:NMEM].rearrange("p (m f) -> p m f", m=2))\
                    .then_inc(mv_ready, 1)

            for n in range(N_QM0, N_OUT0 + 1):
                if n in (1, 2, 3, 4, 5, 9):
                    split(n + 1, KT * P)
                if n == 4:
                    dve.wait_ge(rstd_ready, 1)
                    for m in range(3):
                        l0_epilogue(m)
                if n == 9:
                    dve.wait_ge(rstd_ready, 2)
                    for m in (5, 6, 7):
                        l0_epilogue(m)
                if n >= 4 and n not in (6, 7, 8):
                    l0_epilogue(n - 1)
                if n >= 6 and n != 9:
                    split(n + 1, KT * P)
                if n in (1, 2):
                    for k in range((n - 1) * KT // 2, n * KT // 2):
                        dve.wait_ge(mem_hi_ready, k + 1)
                        dve.scalar_tensor_tensor(mem_lo[:, k, :], memx[:, k, :], gains[:, G_MEM, k:k + 1],
                                                 mem_hi[:, k, :].bitcast(F32), ALU.mult, ALU.subtract)\
                            .then_inc(mem_lo_ready, 1)
                if n == 3:
                    variance(V_MIX0, EPS_A)
                    dve.wait_ge(const_in, 16 * 2)
                    diagonal(V_MIX0)
                if n == 8:
                    variance(V_MEM, EPS_A, 2)
                    diagonal(V_MEM, 2)
                if N_MEMKV + 6 <= n <= N_MEMKV + 9:
                    mv_evac(n - N_MEMKV - 6)
                mem_step(0, n)

            def out_phase(n0, g, count):
                for m in range(KT):
                    residual(m, n0 + m, out_bank(n0 + m))
                    operand(m, g, count + m + 1)
                    split(n0 + m + 2, KT * P)

            def ffn(layer, n0, v, q0):
                def body(i, first=False, last=False):
                    for j in range(2):
                        n = i * 4 + (n0 + 2 * j)
                        q = i * 4 + (q0 + 2 * j)
                        p = i * 2 + (FT * layer + j)
                        w = SLOT if last and j else KT * P
                        if first and j == 0:
                            diagonal(v)
                            split(n + 2, w, 0, 2)
                            dve.wait_ge(rstd_ready, v + 1)
                        scaled(n, 2 * j, tmp[:, 2 * j, :])
                        if not (first and j == 0):
                            split(n + 2, w, 0, (2 * j + 2) % 4)
                        scaled(n + 1, 2 * j + 1, tmp[:, 2 * j + 1, :])
                        dve.wait_ge(silu_ready, p + 1)
                        dve.wait_ge(lin_read, q + 2)
                        dve.tensor_tensor(tmp[:, 2 * j + 1, :], tmp[:, 2 * j, :], tmp[:, 2 * j + 1, :],
                                          ALU.mult).then_inc(gu_ready, 1)
                        dve.wait_ge(g_hi_ready, p + 1)
                        m = i * 2 + j
                        dve.tensor_tensor(g_lo[:, m, :], tmp[:, 2 * j + 1, :],
                                          g_hi[:, m, :].bitcast(F32), ALU.subtract)\
                            .then_inc(g_lo_ready, 1)
                        split(n + 3, w, 1, (2 * j + 3) % 4)
                variance(v, EPS_A)
                body(0, first=True)
                with dve.Fori(1, FT // 2 - 1, 1) as i:
                    body(i)
                body(FT // 2 - 1, last=True)

            def down(n0, g, count):
                def body(i, last=False):
                    for j in range(2):
                        n = i * 4 + (n0 + 2 * j)
                        m = i * 2 + j
                        w = KT * P if last and j else SLOT
                        split(n + 2, w, 0, (2 * j + 2) % 4)
                        residual(m, n + 1, j)
                        operand(m, g, i * 2 + (count + j + 1))
                        split(n + 3, w, 1, (2 * j + 3) % 4)
                with dve.Fori(0, KT // 2 - 1, 1) as i:
                    body(i)
                body(KT // 2 - 1, last=True)

            out_phase(N_OUT0, G_FFN0, KT)
            dve.wait_ge(table_out, 16)
            dve.tensor_tensor(gains[:, G_PRE, :], gains[:, G_PRE, :], gains[:, G_FINAL, :], ALU.mult)\
                .then_inc(gain_ready, 1)
            ffn(0, N_FFN0, V_FFN0, out_index(N_FFN0))
            down(N_DOWN0, G_MIX1, 2 * KT)

            for k in range(KT):
                dve.wait_ge(kv_hi_ready, k + 1)
                dve.scalar_tensor_tensor(kv_lo[:, k, :], x[:, k, :], gains[:, G_KV, k:k + 1],
                                         kv_hi[:, k, :].bitcast(F32), ALU.mult, ALU.subtract)\
                    .then_inc(kv_lo_ready, 1)

            def sw_maxima(u):
                hp, b, s, keys, _ = sw_unit(u)
                h = 2 * hp + s
                lg = ps[:, 2 + 2 * (u % 2):4 + 2 * (u % 2), :].rearrange("p k (g m) -> p (k g) m", g=2)
                dve.wait_ge(sw_scores, u + 1)
                if u >= 2:
                    dve.wait_ge(sw_exp, GROUP * (u - 1))
                else:
                    dve.wait_ge(mem_turned, 16)
                if u == 0:
                    dve.wait_ge(bias_in, 16)
                dve.tensor_tensor(s_sw[:, u % 2, :, 1:1 + keys], lg[:, 0:GROUP, 0:keys],
                                  bias[:, GROUP * h:GROUP * h + GROUP, 256 - keys:256], ALU.add)\
                    .then_inc(sw_biased, 1)
                dve.wait_ge(sw_biased, u + 1)
                dve.wait_ge(sw_sink, u + 1)
                dve.tensor_reduce(nmx[:, u % 2, 0:GROUP], s_sw[:, u % 2, :, 0:1 + keys], AX.X, ALU.max,
                                  negate=True).then_inc(sw_max, 1)

            def sw_normalise(u):
                keys = sw_unit(u)[3]
                dve.wait_ge(sw_exp, GROUP * (u + 1))
                dve.reciprocal(den[:, u % 2, 0:GROUP], den[:, u % 2, 0:GROUP]).then_inc(sw_den, 1)
                dve.wait_ge(sw_den, u + 1)
                some = GROUP - 1
                dve.tensor_tensor(p_sw[:, u % 2, 0:some, 1:1 + keys], p_sw[:, u % 2, 0:some, 1:1 + keys],
                                  den[:, u % 2, 0:some].unsqueeze(2).to_broadcast([P, some, keys]),
                                  ALU.mult).then_inc(sw_probs, 1)

            def sw_out(u):
                hp, b, s, _, _ = sw_unit(u)
                dve.wait_ge(ys_hi_ready, u // 2 + 1)
                dve.tensor_tensor(y_lo[:, GROUP * hp:GROUP * hp + GROUP, b * P:(b + 1) * P],
                                  ps[:, sw_bank(u), 0:GROUP * P].rearrange("p (g t) -> p g t", g=GROUP),
                                  y_hi[:, GROUP * hp:GROUP * hp + GROUP, b * P:(b + 1) * P].bitcast(F32),
                                  ALU.subtract).then_inc(ys_lo_ready, 1)

            def sw_step(w):
                if w < NSW:
                    sw_maxima(w)
                if 1 <= w < NSW + 1:
                    sw_normalise(w - 1)
                if 3 <= w < NSW + 3 and w % 2 == 0:
                    sw_out(w - 3)

            def l1_epilogue(n):
                if n < N_KV:
                    scaled(n, bank_of(n), qm1[:, n - N_QM1, :], SCALE)
                elif n < N_KV + 2:
                    scaled(n, bank_of(n), kT[:, n - N_KV, :])
                elif n < N_Q:
                    if n > N_KV + 2:
                        dve.wait_ge(v_turned, 1)
                    scaled(n, bank_of(n), vT[:])
                else:
                    scaled(n, bank_of(n), qT[:, n - N_Q, :], SCALE)

            for n in range(N_QM1, N_OUT1 + 1):
                if n == N_QM1 + 2:
                    diagonal(V_MIX1)
                    split(n + 1, KT * P)
                    dve.wait_ge(rstd_ready, V_MIX1 + 1)
                    l1_epilogue(N_QM1)
                if n >= N_QM1 + 2:
                    l1_epilogue(n - 1)
                if n > N_QM1 and n != N_QM1 + 2:
                    split(n + 1, KT * P)
                if n == N_QM1 + 1:
                    variance(V_MIX1, EPS_A)
                if n in (N_KV + 4, N_KV + 5):
                    t = n - N_KV - 4
                    dve.wait_ge(v_turned, t + 1)
                    dve.tensor_copy(vn[:, :, t * P:(t + 1) * P],
                                    ps[:, 7, :].rearrange("p (b f) -> p b f", b=TB)).then_inc(vn_ready, 1)
                mem_step(1, n)
                if SW_FIRST <= n < N_OUT1:
                    for w in ((0,), (1,), (2, 3))[n - SW_FIRST]:
                        sw_step(w)
                if n == N_OUT1:
                    for w in range(4, NSW + 3):
                        sw_step(w)
            out_phase(N_OUT1, G_FFN1, 3 * KT)
            ffn(1, N_FFN1, V_FFN1, out_index(N_FFN1))
            dve.wait_ge(gain_ready, 1)
            down(N_DOWN1, G_PRE, 4 * KT)

            def rotate(n):
                kind, i = ROPE[n][0], turned_before(n)[0]
                dve.wait_ge(rope_in, 16 * 2)
                if kind:
                    dve.wait_ge(lin_read, out_index(n) + 1)
                    first = sum(ROPE[m][0] == 0 for m in ROPES)
                    dve.wait_ge(rope_ready, max(first, i - 1))
                    src, sin, dst = strip_of(n), rope_r[:, 1, :], rot_r[:, i % 2, :]
                    dve.tensor_tensor(dst[0:HD], src[HD:P], sin[HD:P], ALU.mult)
                    dve.tensor_tensor(dst[HD:P], src[0:HD], sin[0:HD], ALU.mult).then_inc(rope_sin, 1)
                    return
                dve.wait_ge(rope_mm, i + 1)
                dve.wait_ge(rope_cos, i + 1)
                dve.tensor_tensor(strip_of(n), ps[:, turn_bank(n), :], (rope_n, rope_r)[kind][:, 1, :],
                                  ALU.mult).then_inc(rope_sin, 1)

            def turn(n):
                dve.wait_ge(turn_mm, turned_before(n)[1] + 1)
                dve.tensor_copy(TURN[n], ps[:, turn_bank(n), :].rearrange("p (b f) -> p b f", b=TB))\
                    .then_inc(turn_ready, 1)

            def windows_of(i):
                if i == 0:
                    dve.wait_ge(rope_ready, 1)
                else:
                    dve.wait_ge(lin_read, out_index(N_SECOND + 1) + 1)
                dve.wait_ge(small2_in, 16 * 5)
                for g in range(2):
                    for odd in range(2):
                        of, to = slice(HD * g, HD * g + HD), slice(HD * odd, HD * odd + HD)
                        src = (kcr, vcr)[i][of].rearrange("p (c l o) -> p l c o", l=CSTRIDE // 2, o=2)
                        for w in range(2):
                            ls = slice(CSTRIDE // 2 * w, CSTRIDE // 2 * (w + 1))
                            place = pe2[of, i, odd, ls].unsqueeze(2).to_broadcast([HD, CSTRIDE // 2, NCMP])
                            dve.tensor_tensor(windows[i][to, ls, g * NCMP:(g + 1) * NCMP],
                                              src[:, :, w:w + NCMP, odd], place, ALU.add)\
                                .then_inc(windows_ready, 1)

            def cmp_maxima(g):
                s = ps[:, 7, 0:16 * NCMP].rearrange("p (k c) -> p k c", c=NCMP)
                dve.wait_ge(cm_scores, g + 1)
                dve.tensor_reduce(nm16[:], s, AX.X, ALU.max, negate=True).then_inc(cm_step, 1)
                dve.wait_ge(cm_step, 3 * g + 1)
                dve.tensor_scalar(nm16[:], nm16[:], -EMPTY, None, ALU.min).then_inc(cm_step, 1)
                dve.wait_ge(cm_step, 3 * g + 2)
                dve.tensor_tensor(p_c[:, g], s, nm16[:].unsqueeze(2).to_broadcast([P, 16, NCMP]), ALU.add)\
                    .then_inc(cm_step, 1)

            def cmp_normalise(g):
                dve.wait_ge(cm_exp, g + 1)
                dve.tensor_reduce(d16[:], p_c[:, g], AX.X, ALU.add).then_inc(cm_probs, 1)
                dve.wait_ge(cm_probs, 5 * g + 1)
                dve.tensor_scalar(d16[:], d16[:], TINY, None, ALU.max).then_inc(cm_probs, 1)
                dve.wait_ge(cm_probs, 5 * g + 2)
                dve.reciprocal(d16[:], d16[:]).then_inc(cm_probs, 1)
                dve.wait_ge(cm_probs, 5 * g + 3)
                dve.wait_ge(gate_ready, 1)
                w = d16[:].rearrange("p (b j) -> p b j", b=TB)
                dve.tensor_tensor(w, w, gate_n[:, :, 12 * g:12 * g + 12:3], ALU.mult).then_inc(cm_probs, 1)
                dve.wait_ge(cm_probs, 5 * g + 4)
                dve.tensor_tensor(p_c[:, g], p_c[:, g], d16[:].unsqueeze(2).to_broadcast([P, 16, NCMP]),
                                  ALU.mult).then_inc(cm_probs, 1)

            def ns_maxima(u):
                keys = ns_unit(u)[3]
                dve.wait_ge(ns_scores, u + 1)
                dve.tensor_reduce(nmx[:, u % 2, :], ps[:, 2:6, 0:keys], AX.X, ALU.max, negate=True)\
                    .then_inc(ns_max, 1)

            def ns_normalise(u):
                b, g, br, keys = ns_unit(u)
                dve.wait_ge(ns_exp, GH * u + GH)
                dve.reciprocal(den[:, u % 2, :], den[:, u % 2, :]).then_inc(ns_den, 1)
                dve.wait_ge(ns_den, 2 * u + 1)
                dve.wait_ge(gate_ready, 1)
                dve.tensor_tensor(den[:, u % 2, :], den[:, u % 2, :],
                                  gate_n[:, b, 12 * g + 1 + br:12 * g + 12:3], ALU.mult).then_inc(ns_den, 1)
                dve.wait_ge(ns_den, 2 * u + 2)
                dve.tensor_tensor(p_n[:, u % 2, 0:2, 0:keys], p_n[:, u % 2, 0:2, 0:keys],
                                  den[:, u % 2, 0:2].unsqueeze(2).to_broadcast([P, 2, keys]), ALU.mult)\
                    .then_inc(ns_probs_d, 1)

            def ns_evac(u):
                b, g, br, keys = ns_unit(u)
                if u:
                    dve.wait_ge(ns_pv, u)
                dve.wait_ge(ns_turned, GH * u + 1)
                dve.tensor_copy(pT_n[:, 0:b + 1, 0:P], ps[:, 6, 0:keys].rearrange("p (c t) -> p c t", t=P))\
                    .then_inc(ns_pTd, 1)

            def cmp_evac(u):
                if ns_unit(u)[2]:
                    dve.wait_ge(cm_turned, u // 2 + 1)
                    dve.tensor_copy(pT_c[:], ps[0:NCMP, 6, :]).then_inc(cm_pT, 1)

            def ret_mask(h):
                if h == 0:
                    dve.wait_ge(decay_in, 16)
                else:
                    dve.wait_ge(rt_out, h)
                dve.wait_ge(rt_scores, h + 1)
                for jc, (bank, c) in enumerate(((2, 0), (3, 0), (4, 0), (3, 3 * P))):
                    w = S - jc * P
                    dve.tensor_tensor(att[:, jc, 0:w], ps[:, bank, c:c + w], decay[:, h, 0:w], ALU.mult)\
                        .then_inc(rt_att, 1)

            def ret_bank(ic):
                return ps[:, (1, 5)[ic // 2], ic % 2 * RDV:(ic % 2 + 1) * RDV]

            def ret_statistics(h):
                dve.wait_ge(rt_out, h + 1)
                for ic in range(TB):
                    dve.bn_stats(bn6[:, ic, :], ret_bank(ic)).then_inc(rt_stats, 1)
                for ic in range(TB):
                    dve.wait_ge(rt_stats, 8 * h + ic + 1)
                    dve.bn_aggr(bn2[:, h % 2, ic, :], bn6[:, ic, :]).then_inc(rt_stats, 1)
                dve.wait_ge(rt_stats, 8 * h + 8)
                dve.tensor_scalar(bn2[:, h % 2, :, 1], bn2[:, h % 2, :, 1], EPS_B, None, ALU.add)\
                    .then_inc(rt_var, 1)

            def ret_norm(h):
                dve.wait_ge(rt_pow, h + 1)
                if h:
                    dve.wait_ge(rt_turned, 2 * h)
                for ic in range(TB):
                    dve.tensor_scalar(on[:, ic, :], ret_bank(ic), bn2[:, h % 2, ic, 0:1],
                                      bn2[:, h % 2, ic, 1:2], ALU.subtract, ALU.mult).then_inc(rt_norm, 1)

            def ret_evac(h):
                dve.wait_ge(rt_turned, 2 * h + 1)
                dve.tensor_copy(ob[h // 2][:, h % 2 * 2, :], ps[:, 6, :]).then_inc(rt_ob0, 1)

            def left_over(i, src, hi, lo):
                dve.wait_ge(zh_ready, i + 1)
                dve.tensor_tensor(lo, src, hi.bitcast(F32), ALU.subtract).then_inc(zl_ready, 1)

            def epilogue(n):
                bank, q = bank_of(n), out_index(n)
                e = gated_index(n)
                t = tmp[:, e % 4, :]
                if n == N_SECOND + 1:
                    scaled(n, bank, vcr[:])
                elif n == N_GATE:
                    dve.wait_ge(blk_done, n + 1)
                    dve.tensor_tensor(tmp[0:24, 2, :], ps[0:24, bank, :], rstd[0:24, :], ALU.mult)\
                        .then_inc(lin_read, 1)
                elif n < N_ZN:
                    head = (n - N_RET) % 4 if n >= N_RET else -1
                    before = n - 4 if n < N_RET else n - 2
                    if before in ROPE and (n < N_RET or before >= N_RET):
                        dve.wait_ge(rope_ready, read_of(before)[0])
                    if before in TURN and (n < N_RET or before >= N_RET):
                        dve.wait_ge(turn_ready, read_of(before)[1])
                    factor = SCALE if N_SECOND + 4 <= n < N_SECOND + 8 else (P ** -0.5 if head == 1 else None)
                    scaled(n, bank, strip_of(n), factor)
                elif n < N_MA or N_ZR <= n < N_MB:
                    i = n - N_ZN if n < N_MA else n - N_ZR
                    scaled(n, bank, t)
                    if n < N_MA:
                        dve.wait_ge(oa_ready, TB)
                        o, hi, lo, k = oa[:, i, :], ya_hi, ya_lo, i
                    else:
                        dve.wait_ge(rt_ob1, RH)
                        o, hi, lo, k = ob[i // 4][:, i % 4, :], yb_hi, yb_lo, 4 + i
                    dve.wait_ge(gated, e + 1)
                    dve.tensor_tensor(t, t, o, ALU.mult).then_inc(prod_ready, 1)
                    left_over(k, t, hi[:, i, :], lo[:, i, :])
                elif n < N_ZR:
                    i = (n - N_MA) // 2
                    if (n - N_MA) % 2 == 0:
                        scaled(n, bank, t)
                    else:
                        dve.wait_ge(blk_done, n + 1)
                        dve.wait_ge(gated, e + 1)
                        dve.tensor_tensor(merged[:, i, :], t, ps[:, bank, :], ALU.mult).then_inc(lin_read, 1)
                elif n < N_FIN:
                    i = (n - N_MB) // 2
                    if (n - N_MB) % 2 == 0:
                        scaled(n, bank, t)
                    else:
                        dve.wait_ge(blk_done, n + 1)
                        dve.wait_ge(gated, e + 1)
                        dve.tensor_tensor(t, t, ps[:, bank, :], ALU.mult).then_inc(lin_read, 1)
                        dve.wait_ge(lin_read, q + 1)
                        dve.tensor_tensor(t, t, merged[:, i, :], ALU.add).then_inc(prod_ready, 1)
                        left_over(12 + i, t, mg_hi[:, i, :], mg_lo[:, i, :])

            for n in range(N_SECOND, N_END):
                if n == N_SECOND + 3:
                    dve.wait_ge(rstd_ready, V_LAST + 1)
                    epilogue(N_SECOND)
                    epilogue(N_SECOND + 1)
                if n == N_RET + 1:
                    dve.wait_ge(gate_mm, 1)
                    dve.tensor_copy(gate_n[:], ps[:, 6, 0:24 * TB].rearrange("p (b c) -> p b c", b=TB))\
                        .then_inc(gate_ready, 1)
                    cmp_maxima(1)
                    ns_normalise(0)
                if n >= N_SECOND + 3 and not short(n):
                    epilogue(n - 1)
                if n == N_RET:
                    cmp_maxima(0)
                if NS_FIRST < n <= NS_FIRST + NS:
                    ns_evac(n - 1 - NS_FIRST)
                if RT_FIRST + 1 <= n < RT_FIRST + 1 + RH:
                    ret_statistics(n - RT_FIRST - 1)
                if N_SECOND < n < N_END - 1:
                    split(n + 1, width(n + 1))
                if short(n):
                    epilogue(n - 1)
                if NS_FIRST <= n < NS_FIRST + NS:
                    ns_maxima(n - NS_FIRST)
                if NS_FIRST < n <= NS_FIRST + NS:
                    cmp_evac(n - 1 - NS_FIRST)
                if n == N_SECOND + 1:
                    dve.wait_ge(norm_sum, V_PRE + 1)
                    variance(V_LAST, EPS_A)
                if n == N_SECOND + 2:
                    dve.wait_ge(norm_sum, V_PRE + 1)
                    dve.wait_ge(norm_pow, V_LAST + 1)
                    dve.tensor_tensor(rs3[:], rs[:], rs[:], ALU.mult).then_inc(pre_step, 1)
                    dve.wait_ge(pre_step, 1)
                    dve.tensor_tensor(rs3[:], rs3[:], ps[:, stat_bank, TB:2 * TB], ALU.mult)\
                        .then_inc(pre_step, 1)
                    dve.wait_ge(pre_step, 2)
                    dve.tensor_scalar(var[:], rs3[:], 1.0 / D, EPS_B, ALU.mult, ALU.add).then_inc(norm_var, 1)
                    dve.wait_ge(norm_pow, V_PRE + 1)
                    dve.tensor_tensor(rs2[:], rs2[:], rs[:], ALU.mult).then_inc(pre_step, 1)
                    dve.wait_ge(pre_step, 3)
                    diagonal(V_LAST, rs=rs2)
                if n == N_SECOND + 3:
                    dve.wait_ge(norm_spread, V_LAST + 1)
                    diagonal(V_PRE)
                for m in handled(n):
                    (rotate if m in ROPE else turn)(m)
                if N_SECOND + 4 <= n < N_SECOND + 12:
                    k = n - N_SECOND - 4
                    dve.wait_ge(rstd_ready, V_PRE + 1)
                    dve.scalar_tensor_tensor(x[:, k, :], x[:, k, :], gains[:, G_FINAL, k:k + 1], r1[:],
                                             ALU.mult, ALU.mult).then_inc(x1_ready, 1)
                if n in (N_SECOND + 5, N_SECOND + 6):
                    windows_of(n - N_SECOND - 5)
                if n == N_SECOND + 7:
                    dve.wait_ge(cmp_mm, 1)
                    dve.tensor_copy(kc[:], ps[:, 4, P:P + NCMP]).then_inc(cmp_ready, 1)
                if n == N_SECOND + 9:
                    dve.wait_ge(cmp_mm, 2)
                    dve.tensor_copy(vc[:], ps[0:NCMP, 7, P:2 * P].rearrange("p (g d) -> p g d", g=2))\
                        .then_inc(cmp_ready, 1)
                if NS_FIRST < n <= NS_FIRST + 2:
                    cmp_normalise(n - 1 - NS_FIRST)
                if NS_FIRST < n < NS_FIRST + NS:
                    ns_normalise(n - NS_FIRST)
                if RT_FIRST <= n < RT_FIRST + RH:
                    ret_mask(n - RT_FIRST)
                if RT_FIRST + 1 <= n < RT_FIRST + 1 + RH:
                    ret_norm(n - RT_FIRST - 1)
                if RT_FIRST + 2 <= n < RT_FIRST + 2 + RH:
                    ret_evac(n - RT_FIRST - 2)
            variance(V_POST, EPS_B)
            diagonal(V_POST)
            dve.wait_ge(rstd_ready, V_POST + 1)
            dve.wait_ge(x1_ready, KT)
            for k in range(LAST_DVE):
                dve.tensor_tensor(yg[:, k, :], yg[:, k, :], rstd[:], ALU.mult)\
                    .then_inc(fin_gain, 1)
                dve.wait_ge(fin_gain, k + 1)
                dve.tensor_tensor(x[:, k, :], x[:, k, :], yg[:, k, :], ALU.add).then_inc(out_part, 1)

        @block.tensor
        def _(pe):
            def strip(n, hi, lo, bank, kt=KT, k0=0, cols=S, slot=None, start=True, stop=True,
                      ready=None, rows=P, late=None,
                      aside=None):
                slot = n % 2 if slot is None else slot
                if isinstance(n, int) and n == 0:
                    pe.wait_ge(first_lo, 1)
                else:
                    pe.wait_ge(w_lo_ready, n + 1)
                o = ps[0:rows, bank, 0:cols]
                order = list(range(kt))
                if late:
                    order = [k for k in order if k not in late[2]] + late[2]
                for at, k in enumerate(order):
                    if late and k == late[2][0]:
                        pe.wait_ge(late[0], late[1])
                    if isinstance(n, int) and n == 0 and k == kt // 2:
                        pe.wait_ge(w_lo_ready, 1)
                    if ready:
                        pe.wait_ge(ready[0], ready[1] + k + 1)
                    wh = w_hi[:, slot, k * rows:(k + 1) * rows]
                    wl = w_lo[:, slot, k * rows:(k + 1) * rows]
                    pe.matmul(o, wh, hi[:, k0 + k, 0:cols], start=start and at == 0, stop=False)
                    pe.matmul(o, wh, lo[:, k0 + k, 0:cols], start=False, stop=False)
                    ins = pe.matmul(o, wl, hi[:, k0 + k, 0:cols], start=False, stop=stop and at == kt - 1)
                    if at == kt - 1:
                        ins.then_inc(blk_done, 1)
                    if aside:
                        aside(at)

            def sums(v, tiles=TB):
                pe.wait_ge(acc_ready, SQUARES * (v + 1))
                for c in range(tiles):
                    ins = pe.matmul(ps[:, stat_bank, c:c + 1], acc[:, c * P:(c + 1) * P], ones[:, 0:1],
                                    start=True, stop=True)
                ins.then_inc(norm_sum, 1)

            def spread(v, tiles=TB):
                pe.wait_ge(norm_diag, v + 1)
                pe.matmul(ps[:, stat_bank, 0:tiles * P], ones[:],
                          diag[:, 0:tiles, :].rearrange("p b t -> p (b t)"),
                          start=True, stop=True).then_inc(norm_spread, 1)

            def mem_scores_of(layer, i):
                u, q, mk = 4 * layer + i, (qm0, qm1)[layer], (mk0, mk1)[layer]
                r, t = HD * (i % 2), i // 2
                if i:
                    pe.wait_ge(mem_exp, 4 * u)
                for b in range(TB):
                    ins = pe.matmul(ps[:, 2 + b // 2, b % 2 * NMEM:(b % 2 + 1) * NMEM],
                                    q[r:r + HD, t, b * P:(b + 1) * P], mk[r:r + HD, t, :],
                                    start=True, stop=True)
                ins.then_inc(mem_scores, 1)

            def mem_turn(layer, i):
                u, pm = 4 * layer + i, (pm0, pm1)[layer]
                pe.wait_ge(mem_probs, u + 1)
                for c in range(2):
                    for b in range(TB):
                        ins = pe.transpose(ps[:, 4 + c, b * P:(b + 1) * P],
                                           pm[:, u % 2, b, c * P:(c + 1) * P], ident[:])
                    ins.then_inc(mem_turned, 1)

            def mem_values(layer, i):
                u, pT, mv = 4 * layer + i, (pmT0, pmT1)[layer], (mv0, mv1)[layer]
                r, t = HD * (i % 2), i // 2
                pe.wait_ge(mem_pT0, u + 1)
                pe.wait_ge(mem_pT1, u + 1)
                for c in range(2):
                    ins = pe.matmul(ps[r:r + HD, 6 + t, :], mv[:, c, t * P + r:t * P + r + HD],
                                    pT[:, c, :], start=(c == 0), stop=(c == 1))
                ins.then_inc(mem_pv, 1)

            def mem_step(layer, n):
                if n - 2 in MEM_STEPS[layer]:
                    mem_values(layer, MEM_STEPS[layer][n - 2])
                if n - 1 in MEM_STEPS[layer]:
                    mem_turn(layer, MEM_STEPS[layer][n - 1])
                if n in MEM_STEPS[layer]:
                    mem_scores_of(layer, MEM_STEPS[layer][n])

            pe.wait_ge(ones_ready, 1)
            pe.wait_ge(half_ready, 1)
            for n in range(N_QM0, N_OUT0):
                if n == 4:
                    pe.wait_ge(small_in, 16 * 4)
                    pe.matmul(ps[0:12, 6, 0:NREL], rb[:], onehot[:], start=True, stop=True)\
                        .then_inc(table_mm, 1)
                if n == 3:
                    sums(V_MIX0)
                if n == 4:
                    spread(V_MIX0)
                if n == 8:
                    pe.wait_ge(rstd_ready, 1)
                    sums(V_MEM, 2)
                if n == 9:
                    spread(V_MEM, 2)
                if N_MEMKV + 6 <= n <= N_MEMKV + 9:
                    t = n - N_MEMKV - 6
                    pe.wait_ge(lin_read, n - 1)
                    if t:
                        pe.wait_ge(mv_ready, t)
                    else:
                        pe.wait_ge(table_ready, 1)
                    for m in range(2):
                        ins = pe.transpose(ps[:, 6, m * P:(m + 1) * P], mvt[:, m * P:(m + 1) * P], ident[:])
                    ins.then_inc(mv_turned, 1)
                if n == N_CONV + 1:
                    pe.wait_ge(lin_read, N_CONV)
                if n == N_CONV + 2:
                    pe.wait_ge(mv_ready, 4)
                mem_step(0, n)
                last = [m for m in range(n) if bank_of(m) == bank_of(n)]
                if last:
                    pe.wait_ge(lin_read, last[-1] + 1)
                if N_MEMKV <= n < N_CONV:
                    if n == N_MEMKV:
                        strip(n, mem_hi, mem_lo, bank_of(n), cols=NMEM, ready=(mem_lo_ready, 0))
                    else:
                        strip(n, mem_hi, mem_lo, bank_of(n), cols=NMEM)
                else:
                    strip(n, a_hi, a_lo, bank_of(n), ready=(a_lo_ready, 0) if n == 0 else None)

            def out_phase(n0, late):
                for m in range(KT):
                    n = n0 + m
                    pe.wait_ge(lin_read, out_index(n) - (1 if m else 0))
                    strip(n, y_hi, y_lo, out_bank(n), late=None if m else late)

            def ffn(n0, v, q0, count):
                def body(i, first=False):
                    for j in range(4):
                        n = i * 4 + (n0 + j)
                        if first and j == 1:
                            sums(v)
                        if first and j == 2:
                            spread(v)
                        if not first:
                            pe.wait_ge(lin_read, i * 4 + (q0 + j - 3))
                        strip(n, a_hi, a_lo, j, slot=j % 2,
                              ready=(a_lo_ready, count) if first and j == 0 else None)
                body(0, first=True)
                with pe.Fori(1, FT // 2, 1) as i:
                    body(i)

            def down(layer, n0, q0):
                with pe.Fori(0, KT // 2, 1) as i:
                    for j in range(2):
                        n = i * 4 + (n0 + 2 * j)
                        pe.wait_ge(lin_read, i * 2 + (q0 + j - 1))
                        pe.wait_ge(g_lo_ready, FT * layer + HALF)
                        strip(n, g_hi, g_lo, j, kt=HALF, slot=0, stop=False)
                        pe.wait_ge(g_lo_ready, FT * (layer + 1))
                        strip(n + 1, g_hi, g_lo, j, kt=HALF, k0=HALF, slot=1, start=False)

            pe.wait_ge(yc_lo_ready, CT - 1)
            pe.wait_ge(ym_lo_ready, 2)
            out_phase(N_OUT0, (yc_lo_ready, CT, [CT - 1]))
            ffn(N_FFN0, V_FFN0, out_index(N_FFN0), KT)
            down(0, N_DOWN0, out_index(N_DOWN0))

            def sw_scores_of(u):
                hp, b, s, keys, k0 = sw_unit(u)
                r = HD * s
                if u >= 2:
                    pe.wait_ge(sw_biased, u - 1)
                elif u:
                    pe.wait_ge(mem_pT0, 8)
                    pe.wait_ge(mem_pT1, 8)
                else:
                    pe.wait_ge(mem_exp, 32)
                    pe.wait_ge(lin_read, out_index(N_Q + 2) + 1)
                if u == NSW // 2:
                    pe.wait_ge(lin_read, out_index(N_OUT1 - 1) + 1)
                for g in range(GROUP):
                    ins = pe.matmul(ps[:, 2 + 2 * (u % 2) + g // 2, g % 2 * 256:g % 2 * 256 + keys],
                                    qT[r:r + HD, GROUP * hp + g, b * P:(b + 1) * P],
                                    kT[r:r + HD, hp, k0:k0 + keys], start=True, stop=True)
                ins.then_inc(sw_scores, 1)

            def sw_turn(u):
                hp, b, s, keys, k0 = sw_unit(u)
                pe.wait_ge(sw_probs, u + 1)
                pe.wait_ge(sw_probs_p, u + 1)
                if u:
                    pe.wait_ge(sw_pT, u)
                else:
                    pe.wait_ge(ym_lo_ready, 4)
                for c in range(keys // P):
                    for g in range(GROUP):
                        ins = pe.transpose(ps[:, 6 + c, g * P:(g + 1) * P],
                                           p_sw[:, u % 2, g, 1 + c * P:1 + (c + 1) * P], ident[:])
                        if g == GROUP - 1 or (keys == P and g == GROUP - 2):
                            ins.then_inc(sw_turned, 1)

            def sw_values(u):
                hp, b, s, keys, k0 = sw_unit(u)
                r, h = HD * s, 2 * hp + s
                pe.wait_ge(sw_pT, u + 1)
                if s == 0 and u >= 4:
                    pe.wait_ge(ys_lo_ready, u // 2 - 1)
                elif s == 0:
                    pe.wait_ge(lin_read, out_index(N_OUT1 - (1 if u else 3)) + 1)
                for c in range(keys // P):
                    ins = pe.matmul(ps[r:r + HD, sw_bank(u), 0:GROUP * P],
                                    vn[:, k0 // P + c, h * HD:(h + 1) * HD], pT_sw[:, c, :],
                                    start=(c == 0), stop=(c == keys // P - 1))
                ins.then_inc(sw_pv, 1)

            def sw_step(v):
                if 3 <= v < NSW + 3:
                    sw_turn(v - 3)
                if v < NSW:
                    sw_scores_of(v)
                if 3 <= v < NSW + 3:
                    sw_values(v - 3)

            for n in range(N_QM1, N_OUT1):
                if n == N_QM1 + 1:
                    sums(V_MIX1)
                if n == N_QM1 + 2:
                    spread(V_MIX1)
                if n in (N_KV + 4, N_KV + 5):
                    t = n - N_KV - 4
                    pe.wait_ge(lin_read, out_index(N_KV + 2 + t) + 1)
                    pe.wait_ge(vn_ready, t) if t else pe.wait_ge(rstd_ready, V_MIX1 + 1)
                    for b in range(TB):
                        ins = pe.transpose(ps[:, 7, b * P:(b + 1) * P], vT[:, b * P:(b + 1) * P], ident[:])
                    ins.then_inc(v_turned, 1)
                if n == N_Q - 1:
                    pe.wait_ge(lin_read, out_index(N_Q - 1))
                if n == N_Q + 2:
                    pe.wait_ge(vn_ready, 2)
                mem_step(1, n)
                if n >= SW_FIRST:
                    for v in ((0,), (1, 2), (3,))[n - SW_FIRST]:
                        sw_step(v)
                last = [m for m in range(N_QM1, n) if bank_of(m) == bank_of(n)]
                if last:
                    pe.wait_ge(lin_read, out_index(last[-1]) + 1)
                if N_KV <= n < N_Q:
                    strip(n, kv_hi, kv_lo, bank_of(n), ready=(kv_lo_ready, 0) if n == N_KV else None)
                else:
                    strip(n, a_hi, a_lo, bank_of(n), ready=(a_lo_ready, 2 * KT) if n == N_QM1 else None)
            for v in range(4, NSW + 3):
                sw_step(v)
            pe.wait_ge(ym_lo_ready, 4)
            pe.wait_ge(ys_lo_ready, NSW // 2 - 1)
            out_phase(N_OUT1, (ys_lo_ready, NSW // 2, list(range(GROUP, CT))))
            ffn(N_FFN1, V_FFN1, out_index(N_FFN1), 3 * KT)
            down(1, N_DOWN1, out_index(N_DOWN1))

            def exchange(n):
                i = turned_before(n)[0]
                pe.wait_ge(lin_read, out_index(n) + 1)
                pe.matmul(ps[:, turn_bank(n), :], perm[:, ROPE[n][0], :], strip_of(n), start=True, stop=True)\
                    .then_inc(rope_mm, 1)

            def turn(n):
                pe.wait_ge(lin_read, out_index(n) + 1)
                for b in range(TB):
                    ins = pe.transpose(ps[:, turn_bank(n), b * P:(b + 1) * P],
                                       strip_of(n)[:, b * P:(b + 1) * P], ident[:])
                ins.then_inc(turn_mm, 1)

            def bank_read(n):
                if n in ROPE:
                    pe.wait_ge(rope_ready, read_of(n)[0])
                else:
                    pe.wait_ge(turn_ready, read_of(n)[1])

            def hidden(i, k):
                if k == 0:
                    pe.wait_ge((w1k_in, w1v_in)[i], 16)
                    pe.wait_ge(windows_ready, 8 * (i + 1))
                    pe.wait_ge(rstd_ready, V_PRE + 1)
                m = k // 4
                for l in range(k % 4 * CLEN // 8, (k % 4 + 1) * CLEN // 8):
                    ins = pe.matmul(ps[:, (4, 7)[i], m * 2 * NCMP:(m + 1) * 2 * NCMP],
                                    w1[:, i, l, m * P:(m + 1) * P], windows[i][:, l, :],
                                    start=(l == 0), stop=(l == CLEN // 2 - 1))
                if k == KT - 1:
                    ins.then_inc(cmp_hidden, 1)

            def compressed(i):
                pe.wait_ge(cmp_gelu, i + 1)
                for g in range(2):
                    for m in range(2):
                        inner = hid[:, m, g * NCMP:(g + 1) * NCMP]
                        if i == 0:
                            o = ps[HD * g:HD * g + HD, 4, P:P + NCMP]
                            ins = pe.matmul(o, w2[:, 0, m, :], inner, start=(m == 0), stop=(m == 1))
                        else:
                            o = ps[0:NCMP, 7, P + g * HD:P + (g + 1) * HD]
                            ins = pe.matmul(o, inner, w2[:, 1, m, :], start=(m == 0), stop=(m == 1))
                ins.then_inc(cmp_mm, 1)

            def cmp_scores(g, at):
                if at == 0:
                    if g == 0:
                        pe.wait_ge(cmp_ready, 2)
                        bank_read(N_SECOND + 7)
                    else:
                        pe.wait_ge(cm_step, 3)
                    pe.matmul(ps[:, 7, 0:16 * NCMP], ident_b, mask_c, start=True, stop=False)
                for k in range(16 * at // KT, 16 * (at + 1) // KT):
                    b, j = k // GH, k % GH
                    ins = pe.matmul(ps[:, 7, k * NCMP:(k + 1) * NCMP],
                                    qn[HD * g:HD * g + HD, j, b * P:(b + 1) * P], kc[HD * g:HD * g + HD, :],
                                    start=False, stop=(k == 15))
                if at == KT - 1:
                    ins.then_inc(cm_scores, 1)

            def ns_scores_of(u):
                b, g, br, keys = ns_unit(u)
                r = slice(HD * g, HD * g + HD)
                if u:
                    pe.wait_ge(ns_exp, GH * u)
                for j in range(GH):
                    pe.matmul(ps[:, 2 + j, 0:keys], qn[r, j, b * P:(b + 1) * P], (ks, kw)[br][r, 0:keys],
                              start=True, stop=False)
                    ins = pe.matmul(ps[:, 2 + j, b * P:keys], ident_b, causal, start=False, stop=True)
                ins.then_inc(ns_scores, 1)

            def ns_turn(u, js):
                b, g, br, keys = ns_unit(u)
                pe.wait_ge(*((ns_probs_d, u + 1) if js[0] == 0 else (ns_probs_a, 2 * u + 2)))
                for j in js:
                    if j >= 2:
                        pe.wait_ge(*((ns_pTd, u + 1) if j == 2 else (ns_pTa, 3 * u + 1)))
                    for c in range(b + 1):
                        ins = pe.transpose(ps[:, 6 + j % 2, c * P:(c + 1) * P],
                                           p_n[:, u % 2, j, c * P:(c + 1) * P], ident[:])
                    ins.then_inc(ns_turned, 1)

            def cmp_turn(u):
                b, g, br, keys = ns_unit(u)
                pe.wait_ge(ns_pTa, 3 * u + 2)
                pe.wait_ge(cm_probs, 5 * (g + 1))
                for j in range(GH):
                    ins = pe.transpose(ps[0:NCMP, 6, j * P:(j + 1) * P], p_c[:, g, b * GH + j, :], ident[:])
                ins.then_inc(cm_turned, 1)

            def ns_values(u):
                b, g, br, keys = ns_unit(u)
                pe.wait_ge(ns_pTd, u + 1)
                pe.wait_ge(ns_pTa, 3 * u + 3)
                if g == 0 and br == 0:
                    pe.wait_ge(oa_ready, b) if b else pe.wait_ge(cmp_ready, 2)
                o = ps[HD * g:HD * g + HD, 1, :]
                for c in range(b + 1):
                    ins = pe.matmul(o, (vs, vw)[br][:, c, g * HD:(g + 1) * HD], pT_n[:, c, :],
                                    start=(br == 0 and c == 0), stop=False)
                if br:
                    pe.wait_ge(cm_pT, u // 2 + 1)
                    ins = pe.matmul(o, vc[:, g, :], pT_c[:], start=False, stop=True)
                ins.then_inc(ns_pv, 1)

            def ret_scores(h):
                if h:
                    pe.wait_ge(rt_att, TB * h)
                for jc, (bank, c) in enumerate(((2, 0), (3, 0), (4, 0), (3, 3 * P))):
                    ins = pe.matmul(ps[:, bank, c:c + S - jc * P], kr[:, h, jc * P:(jc + 1) * P],
                                    qr[:, h, jc * P:S], start=True, stop=True)
                ins.then_inc(rt_scores, 1)

            def ret_values(h):
                pe.wait_ge(rt_att, TB * h + TB)
                if h:
                    pe.wait_ge(rt_norm, TB * h)
                for ic in range(TB):
                    for jc in range(ic + 1):
                        ins = pe.matmul(ps[:, (1, 5)[ic // 2], ic % 2 * RDV:(ic % 2 + 1) * RDV],
                                        att[:, jc, (ic - jc) * P:(ic - jc + 1) * P],
                                        vr[:, jc, h * RDV:(h + 1) * RDV], start=(jc == 0), stop=(jc == ic))
                ins.then_inc(rt_out, 1)

            def ret_turn(h):
                pe.wait_ge(rt_norm, TB * h + TB)
                if h:
                    pe.wait_ge(rt_ob0, h)
                    pe.wait_ge(rt_ob1, h)
                for f in range(2):
                    for ic in range(TB):
                        ins = pe.transpose(ps[:, 6 + f, ic * P:(ic + 1) * P], on[:, ic, f * P:(f + 1) * P],
                                           ident[:])
                    ins.then_inc(rt_turned, 1)

            def post_sums(i):
                pe.wait_ge(post_sq, i + 1)
                for c in range(TB):
                    ins = pe.matmul(ps[:, stat_bank, c:c + 1], sq[:, i % 2, c * P:(c + 1) * P], ones[:, 0:1],
                                    start=(i == 0 and c == 0), stop=(i == KT - 1 and c == TB - 1))
                ins.then_inc(post_sum if i < KT - 1 else norm_sum, 1)

            def turns(n):
                for m in on_tensor(n):
                    if turned_before(m) != (0, 0):
                        order = [k for t in range(N_SECOND, N_END) for k in on_tensor(t)]
                        same = [k for k in order[:order.index(m)] if turn_bank(k) == turn_bank(m)]
                        if same:
                            bank_read(same[-1])
                    (exchange if m in ROPE else turn)(m)

            def beside_ns(n, k):
                u = n - 1 - NS_FIRST
                if k == 0 and ns_unit(u)[2]:
                    cmp_turn(u)
                if n == NS_FIRST + NS and k == 2:
                    ns_values(NS - 1)
                if k == 2 and on_tensor(n):
                    pe.wait_ge(ns_pTa, 3 * u + 3)
                    turns(n)

            for n in range(N_SECOND, N_END):
                if n >= N_FIN + 2:
                    post_sums(n - N_FIN - 2)
                if n == N_SECOND + 1:
                    sums(V_LAST)
                    pe.wait_ge(acc2_ready, 1 + KT)
                    for c in range(TB):
                        ins = pe.matmul(ps[:, stat_bank, TB + c:TB + c + 1], acc2[:, c * P:(c + 1) * P],
                                        ones[:, 0:1], start=True, stop=True)
                    ins.then_inc(norm_sum, 1)
                if n == N_SECOND + 3:
                    spread(V_LAST)
                if n == N_SECOND + 4:
                    pe.wait_ge(rstd_ready, V_LAST + 1)
                    spread(V_PRE)
                    pe.wait_ge(small2_in, 16 * 5)
                if NS_FIRST + 2 <= n <= NS_FIRST + NS:
                    ns_values(n - 2 - NS_FIRST)
                if n == N_RET + 1:
                    pe.wait_ge(gate_sig, 1)
                    bank_read(N_SECOND + 9)
                    for b in range(TB):
                        ins = pe.transpose(ps[:, 6, 24 * b:24 * b + 24], tmp[0:24, 2, b * P:(b + 1) * P],
                                           ident[0:24, 0:24])
                    ins.then_inc(gate_mm, 1)
                if NS_FIRST < n <= NS_FIRST + NS:
                    u = n - 1 - NS_FIRST
                    if u == 0:
                        pe.wait_ge(gate_ready, 1)
                        ns_scores_of(1)
                        pe.wait_ge(cm_step, 6)
                        ns_turn(0, (0, 1))
                    else:
                        if ns_unit(u - 1)[2]:
                            pe.wait_ge(cm_pT, u // 2)
                        for m in on_tensor(n - 1):
                            bank_read(m)
                        ns_turn(u, (0, 1))
                        if u < NS - 1:
                            ns_scores_of(u + 1)
                    ns_turn(u, (2, 3))
                if n == NS_FIRST:
                    pe.wait_ge(lin_read, out_index(N_GATE) + 1)
                    pe.wait_ge(cmp_ready, 2)
                    bank_read(N_SECOND + 8)
                    ns_scores_of(0)
                if not NS_FIRST < n <= NS_FIRST + NS:
                    turns(n)
                if n == N_SECOND + 7:
                    compressed(0)
                if n == N_SECOND + 9:
                    compressed(1)
                if n == RT_FIRST:
                    pe.wait_ge(ns_exp, GH * NS)
                    pe.wait_ge(oa_ready, TB)
                    bank_read(N_ZN - 1)
                if RT_FIRST + 2 <= n < RT_FIRST + 2 + RH:
                    ret_turn(n - RT_FIRST - 2)
                if RT_FIRST + 1 <= n < RT_FIRST + 1 + RH:
                    ret_values(n - RT_FIRST - 1)
                if RT_FIRST <= n < RT_FIRST + RH:
                    ret_scores(n - RT_FIRST)
                last = [m for m in range(N_SECOND, n) if bank_of(m) == bank_of(n)]
                if n >= N_FIN + 2:
                    pe.wait_ge(fin_read, n - N_FIN - 1)
                elif last:
                    pe.wait_ge(lin_read, out_index(last[-1]) + 1)
                if n == N_MA + 1:
                    pe.wait_ge(zl_ready, GH)
                if n == N_MB + 1:
                    pe.wait_ge(zl_ready, GH + KT)
                if n == N_FIN:
                    strip(n, mg_hi, mg_lo, bank_of(n), ready=(zl_ready, GH + KT))
                elif n > N_FIN:
                    strip(n, mg_hi, mg_lo, bank_of(n))
                elif N_MA <= n < N_ZR and (n - N_MA) % 2:
                    strip(n, ya_hi, ya_lo, bank_of(n), kt=GH)
                elif n >= N_MB and (n - N_MB) % 2:
                    strip(n, yb_hi, yb_lo, bank_of(n))
                else:
                    strip(n, a_hi, a_lo, bank_of(n), ready=(a_lo_ready, 4 * KT) if n == N_SECOND else None,
                          rows=24 if n == N_GATE else P,
                          aside=(lambda k, n=n: beside_ns(n, k)) if NS_FIRST < n <= NS_FIRST + NS else
                          {N_SECOND + 6: lambda k: hidden(0, k),
                           N_SECOND + 8: lambda k: hidden(1, k),
                           N_GATE: lambda k: cmp_scores(0, k),
                           N_RET: lambda k: cmp_scores(1, k)}.get(n))
            post_sums(KT - 2)
            post_sums(KT - 1)
            spread(V_POST)


def strips(w):
    k, n = w.shape
    return w.reshape(k // P, P, n // P, P).transpose(2, 1, 0, 3).reshape(n // P, P, -1)


LOW = [0, 1, 2, 6, 7, 8]
HIGH = [3, 4, 5, 9, 10, 11]


def head_order():
    return np.concatenate([np.arange(h * HD, (h + 1) * HD) for p in zip(LOW, HIGH) for h in p])


def relative_onehot():
    exact, count, far = 16, 32, 128
    dist = np.arange(2 * P - 1, 2 * P - 1 - NREL, -1)
    d = np.maximum(dist, 1).astype(np.float32)
    large = exact + (np.log(d / np.float32(exact)) / np.float32(math.log(far / exact))
                     * np.float32(count - exact)).astype(np.int32)
    bucket = np.where(np.maximum(dist, 0) < exact, np.maximum(dist, 0), np.minimum(large, count - 1))
    out = np.zeros((33, NREL), np.float32)
    inside = (dist >= 0) & (dist < P)
    out[bucket[inside], np.nonzero(inside)[0]] = 1.0
    out[32, ~inside] = 1.0
    return out


def exchanges():
    out = np.zeros((P, 2, P), np.float32)
    for d in range(P):
        if d % HD < 16:
            out[d ^ 8, 0, d] = 1.0
        out[d ^ 64, 1, d] = 1.0
    return out


def rotary_tables():
    pos = np.arange(S, dtype=np.float32)
    out = np.zeros((2, P, 2, S), np.float32)
    inv_n = np.float32(1.0) / (np.float32(500000.0) ** (np.arange(0, 16, 2, dtype=np.float32) / np.float32(16)))
    inv_r = np.float32(1.0) / (np.float32(10000.0) ** np.linspace(0.0, 1.0, 64, dtype=np.float32))
    out[0, :, 0, :] = 1.0
    for d in range(P):
        if d % HD < 16:
            ang = (pos * inv_n[d % 8]).astype(np.float32)
            out[0, d, 0], out[0, d, 1] = np.cos(ang), np.sin(ang) * (-1 if d % HD < 8 else 1)
        ang = (pos * inv_r[d % 64]).astype(np.float32)
        out[1, d, 0], out[1, d ^ 64, 1] = np.cos(ang), np.sin(ang) * (-1 if d < 64 else 1)
    return out


def mask_table():
    q, k = np.arange(P)[:, None], np.arange(P)[None, :]
    causal = np.where(k <= q, 0.0, MASKED)
    t = np.arange(TB)[None, :, None, None] * P + np.arange(P)[:, None, None, None]
    end = np.arange(NCMP)[None, None, None, :] * CSTRIDE + CLEN - 1
    cmp = np.where(end <= t, 0.0, MASKED) + np.zeros((P, TB, GH, NCMP))
    return np.concatenate([np.eye(P), causal, cmp.reshape(P, -1)], 1).astype(mybir.dt.np(BF16))


def decays():
    log_g = np.log(np.float32(1.0) - np.float32(2.0) ** (np.float32(-5.0) - np.arange(RH, dtype=np.float32)))
    diff = (np.arange(S)[None, :] - np.arange(P)[:, None]).astype(np.float32)
    out = np.exp(np.maximum(diff, 0)[:, None, :] * log_g[None, :, None]) * (diff >= 0)[:, None, :]
    return out.astype(np.float32)


def feature_major(v):
    return v.T.reshape(v.shape[1] // P, P, -1).transpose(1, 0, 2)


def kernel(**inputs):
    from concourse import bacc
    from concourse.bass_utils import run_bass_kernel_spmd

    w = {k: np.asarray(v) for k, v in inputs.items()}
    nc = bacc.Bacc("TRN2", target_bir_lowering=False, num_devices=1)
    order = head_order()
    a_in = strips(w["a_w_in"][0])
    triple = [a_in[[i, 12 + i, 6 + i]] for i in range(CT)]
    mkv = [strips(w["w_mem_kv"][i]) for i in range(2)]
    b_in = strips(w["b_w_q"][0][:, np.concatenate([order, np.arange(768, 1024)])])
    b_out = strips(w["b_w_out"][0][np.concatenate([order, np.arange(768, 1024)])])

    def pairs(i):
        return np.stack([strips(w["w_gate"][i]), strips(w["w_up"][i])], 1).reshape(2 * FT, P, D)

    w2_in = w["w_in_2"]
    cuts = np.cumsum([512, 128, 128, 128, 128, 128, 128, 24, 512, 512, 512, 1024, 1024, 1024, 1024])[:-1]
    q_n, k_c, v_c, k_s, v_s, k_w, v_w, g_n, z_n, q_r, k_r, v_r, z_r, m_a, m_b = np.split(w2_in, cuts, axis=1)
    pairs_n = np.concatenate([np.arange(h * HD, (h + 1) * HD) for t in range(GH) for h in (t, GH + t)])
    q_r, k_r, v_r = strips(q_r), strips(k_r), strips(v_r)
    ret = np.concatenate([np.stack([q_r[h], k_r[h], v_r[2 * h], v_r[2 * h + 1]]) for h in range(RH)])
    mb_ret = np.stack([strips(m_b), strips(w["w_ret_o_2"])], 1).reshape(2 * KT, P, D)

    def cmp_first(v):
        return v.reshape(CLEN // 2, 2, HD, 256).transpose(1, 2, 0, 3).reshape(P, CLEN // 2, 256)

    def cmp_places(v):
        places = v.reshape(CLEN // 2, 2, HD).transpose(2, 1, 0)
        return np.concatenate([places, places])

    arrays = {
        "w8b": np.concatenate([strips(k_c), strips(v_c), strips(v_s), strips(v_w), strips(q_n[:, pairs_n]),
                               strips(k_s), strips(k_w), ret, strips(z_n[:, pairs_n]), strips(m_a),
                               strips(z_r), mb_ret, strips(w["w_out_2"])]),
        "w_gates": g_n.reshape(KT, P, 24).transpose(1, 0, 2).reshape(P, KT * 24),
        "w_nsa_o": strips(w["w_nsa_o_2"][pairs_n]),
        "cmp_w1": np.stack([cmp_first(w["cmp_w1_k_2"]), cmp_first(w["cmp_w1_v_2"])]),
        "cmp_w2": np.stack([w["cmp_w2_k_2"].reshape(2, P, HD), w["cmp_w2_v_2"].reshape(2, P, HD)])
                    .transpose(2, 0, 1, 3),
        "cmp_pe": np.stack([cmp_places(w["cmp_pe_k_2"]), cmp_places(w["cmp_pe_v_2"])], 1),
        "gate_b": w["b_nsa_gate_2"].reshape(24, 1),
        "perm": exchanges(),
        "masks": mask_table(),
        "rope": rotary_tables(),
        "decay": decays(),
        "w8": np.concatenate([a_in[18:20], triple[0], mkv[0][:2], mkv[1][:2], mkv[0][2:], mkv[1][2:],
                              *triple[1:], strips(w["a_w_out"][0]), pairs(0), b_in[6:8],
                              strips(w["w_kv"]), b_in[:6], b_out, pairs(1)]),
        "w_down": np.concatenate([strips(w["w_down"][i]).reshape(KT, P, 2, SLOT).transpose(0, 2, 1, 3)
                                  .reshape(2 * KT, P, SLOT) for i in range(2)]),
        "xT": feature_major(w["x"][0]),
        "memT": feature_major(w["mem"][0]),
        "gains": np.stack([g.reshape(KT, P).T for g in (
            w["mem_norm"], w["norm_mix"][0], w["norm_ffn"][0], w["kv_norm"], w["norm_mix"][1],
            w["norm_ffn"][1], w["final_norm"], w["norm_pre_2"], w["norm_post_2"])], 1),
        "conv_w": w["a_conv_w"][0].reshape(3, CT, P).transpose(2, 1, 0),
        "sinks": w["b_sinks"][0],
        "rel_bias": w["rel_bias"],
        "onehot": relative_onehot(),
        "masked": np.full((1, 12), MASKED, np.float32),
        "ident": np.eye(P, dtype=np.float32),
    }
    arrays = {k: np.ascontiguousarray(v) for k, v in arrays.items()}
    aps = {k: nc.dram_tensor(k, v.shape, mybir.dt.from_np(v.dtype), kind="ExternalInput").ap()
           for k, v in arrays.items()}
    out = nc.dram_tensor("out", (P, KT, S), F32, kind="ExternalOutput").ap()
    build(nc, aps, out)
    r = run_bass_kernel_spmd(nc, [arrays], core_ids=[0])
    y = r.results[0]["out"]
    return np.ascontiguousarray(y.transpose(2, 1, 0).reshape(1, S, D))
```
